# Optimizing a Trainium2 kernel written in Bass

```python
import jax, jax.numpy as jnp
from jax import lax
import numpy as np

D_MODEL = 1024
BATCH = 1
SEQ = 512
DEPTH = 1

PLE_DIM = 256
MIX_WIDTH = D_MODEL
ATTN_WIDTH = MIX_WIDTH // 2
CONV_WIDTH = MIX_WIDTH - ATTN_WIDTH
V_DIM = 64
NOPE_DIM = 64
ROPE_DIM = 32
N_ATTN_HEADS = ATTN_WIDTH // V_DIM
Q_RANK = D_MODEL // 4
KV_RANK = D_MODEL // 4
N_CONV_GROUPS = 8
CONV_K = 3
IN_COLS = Q_RANK + KV_RANK + ROPE_DIM + 3 * CONV_WIDTH
D_FF = ((8 * D_MODEL // 3 + 255) // 256) * 256
ROPE_THETA = 10000.0
Q_BLOCK = 128
EPS = 1e-6


def rmsnorm(x, g):
    xf = x.astype(jnp.float32)
    y = xf * lax.rsqrt(jnp.mean(xf * xf, axis=-1, keepdims=True) + EPS)
    return (y * g.astype(jnp.float32)).astype(x.dtype)

def rope_tables(positions, dtype):
    half = ROPE_DIM // 2
    inv_freq = 1.0 / (ROPE_THETA ** (jnp.arange(half, dtype=jnp.float32) / half))
    ang = positions.astype(jnp.float32)[..., None] * inv_freq
    return jnp.cos(ang).astype(dtype), jnp.sin(ang).astype(dtype)

def apply_rope(t, cos, sin):
    t1, t2 = jnp.split(t, 2, axis=-1)
    return jnp.concatenate([t1 * cos - t2 * sin, t2 * cos + t1 * sin], axis=-1)

def causal_block_attention(q, k, v):
    B, S, H, Dq = q.shape
    Dv = v.shape[-1]
    nb = S // Q_BLOCK
    scale = Dq ** -0.5
    qb = q.reshape(B, nb, Q_BLOCK, H, Dq).transpose(1, 0, 2, 3, 4)
    k_idx = jnp.arange(S)

    def one_block(args):
        q_blk, blk = args
        q_idx = blk * Q_BLOCK + jnp.arange(Q_BLOCK)
        s = jnp.einsum('bqhd,bkhd->bhqk', q_blk, k).astype(jnp.float32) * scale
        s = jnp.where(k_idx[None, :] <= q_idx[:, None], s, jnp.finfo(jnp.float32).min)
        pr = jax.nn.softmax(s, axis=-1)
        return jnp.einsum('bhqk,bkhd->bqhd', pr.astype(v.dtype), v)

    out = lax.map(one_block, (qb, jnp.arange(nb)))
    return out.transpose(1, 0, 2, 3, 4).reshape(B, S, H * Dv)

def mla(c_q_raw, c_kv_raw, k_rope_raw, positions, q_norm, kv_norm, w_uq, w_ukv):
    B, S, _ = c_q_raw.shape
    H = N_ATTN_HEADS
    q = (rmsnorm(c_q_raw, q_norm) @ w_uq).reshape(B, S, H, NOPE_DIM + ROPE_DIM)
    kv = (rmsnorm(c_kv_raw, kv_norm) @ w_ukv).reshape(B, S, H, NOPE_DIM + V_DIM)
    k_nope, v = kv[..., :NOPE_DIM], kv[..., NOPE_DIM:]
    cos, sin = rope_tables(positions, q.dtype)
    q_rope = apply_rope(q[..., NOPE_DIM:], cos[:, :, None, :], sin[:, :, None, :])
    k_rope = apply_rope(k_rope_raw, cos, sin)
    q_full = jnp.concatenate([q[..., :NOPE_DIM], q_rope], axis=-1)
    k_full = jnp.concatenate(
        [k_nope, jnp.broadcast_to(k_rope[:, :, None, :], (B, S, H, ROPE_DIM))], axis=-1)
    return causal_block_attention(q_full, k_full, v)

def short_gated_conv(b_gate, c_gate, xv, conv_w):
    S = xv.shape[1]
    u = c_gate * xv
    u_pad = jnp.pad(u, ((0, 0), (CONV_K - 1, 0), (0, 0)))
    y = conv_w[0] * u_pad[:, CONV_K - 1:CONV_K - 1 + S]
    for k in range(1, CONV_K):
        y = y + conv_w[k] * u_pad[:, CONV_K - 1 - k:CONV_K - 1 - k + S]
    return b_gate * y

def first_inputs(seed: int = 0) -> dict:
    key = jax.random.key(seed)
    ks = jax.random.split(key, 24)
    f32 = jnp.float32

    def w(k, shape, fan_in):
        return jax.random.normal(k, shape, f32) * (fan_in ** -0.5)

    def gain(k, shape):
        return 1.0 + 0.05 * jax.random.normal(k, shape, f32)

    L = DEPTH
    x = jax.random.normal(ks[0], (BATCH, SEQ, D_MODEL), f32)
    p = jax.random.normal(ks[1], (DEPTH, BATCH, SEQ, PLE_DIM), f32)
    offset = jax.random.randint(ks[2], (BATCH, 1), 0, 4096)
    positions = (offset + jnp.arange(SEQ, dtype=jnp.int32)[None, :]).astype(jnp.int32)
    return {
        "x": x,
        "p": p,
        "positions": positions,
        "mix_pre_norm": gain(ks[3], (L, D_MODEL)),
        "w_in": w(ks[4], (L, D_MODEL, IN_COLS), D_MODEL),
        "q_norm": gain(ks[5], (L, Q_RANK)),
        "kv_norm": gain(ks[6], (L, KV_RANK)),
        "w_uq": w(ks[7], (L, Q_RANK, N_ATTN_HEADS * (NOPE_DIM + ROPE_DIM)), Q_RANK),
        "w_ukv": w(ks[8], (L, KV_RANK, N_ATTN_HEADS * (NOPE_DIM + V_DIM)), KV_RANK),
        "conv_w": w(ks[9], (L, CONV_K, CONV_WIDTH), CONV_K),
        "attn_group_norm": gain(ks[10], (L, ATTN_WIDTH)),
        "conv_group_norm": gain(ks[11], (L, CONV_WIDTH)),
        "w_out": w(ks[12], (L, MIX_WIDTH, D_MODEL), MIX_WIDTH),
        "mix_post_norm": gain(ks[13], (L, D_MODEL)),
        "ffn_pre_norm": gain(ks[14], (L, D_MODEL)),
        "w_gate": w(ks[15], (L, D_MODEL, D_FF), D_MODEL),
        "w_up": w(ks[16], (L, D_MODEL, D_FF), D_MODEL),
        "w_down": w(ks[17], (L, D_FF, D_MODEL), D_FF),
        "ffn_post_norm": gain(ks[18], (L, D_MODEL)),
        "w_ple_proj": w(ks[19], (L, PLE_DIM, D_MODEL), PLE_DIM),
        "ple_norm": gain(ks[20], (L, D_MODEL)),
        "w_ple_gate": w(ks[21], (L, D_MODEL, D_MODEL), D_MODEL),
    }

def first_block(x, p, positions, mix_pre_norm, w_in, q_norm, kv_norm, w_uq, w_ukv,
              conv_w, attn_group_norm, conv_group_norm, w_out, mix_post_norm,
              ffn_pre_norm, w_gate, w_up, w_down, ffn_post_norm,
              w_ple_proj, ple_norm, w_ple_gate):
    o1 = Q_RANK
    o2 = o1 + KV_RANK
    o3 = o2 + ROPE_DIM
    o4 = o3 + CONV_WIDTH
    o5 = o4 + CONV_WIDTH
    for i in range(DEPTH):
        h = rmsnorm(x, mix_pre_norm[i])
        z = h @ w_in[i]
        a = mla(z[..., :o1], z[..., o1:o2], z[..., o2:o3], positions,
                q_norm[i], kv_norm[i], w_uq[i], w_ukv[i])
        c = short_gated_conv(z[..., o3:o4], z[..., o4:o5], z[..., o5:], conv_w[i])
        m = jnp.concatenate([rmsnorm(a, attn_group_norm[i]),
                             rmsnorm(c, conv_group_norm[i])], axis=-1)
        x = x + rmsnorm(m @ w_out[i], mix_post_norm[i])
        h = rmsnorm(x, ffn_pre_norm[i])
        f = (jax.nn.silu(h @ w_gate[i]) * (h @ w_up[i])) @ w_down[i]
        x = x + rmsnorm(f, ffn_post_norm[i])
        e = rmsnorm(p[i] @ w_ple_proj[i], ple_norm[i])
        x = x + jax.nn.sigmoid(x @ w_ple_gate[i]) * e
    return x


DEPTH_2 = 2

CHUNK = 64
N_MIXERS = 2
RET_HEADS = 4
RET_DK = D_MODEL // RET_HEADS
RET_DV = 2 * RET_DK
RET_QK = RET_HEADS * RET_DK
RET_VW = RET_HEADS * RET_DV
ROPE_BASE = 10000.0
ATT_HEADS = 16
ATT_DH = D_MODEL // ATT_HEADS
PAST_CHUNKS = 8
BAND_PAST = PAST_CHUNKS * CHUNK
BAND = (PAST_CHUNKS + 1) * CHUNK
MAX_REL = 256
REL_TABLE = MAX_REL + CHUNK
D_FF_2 = 4 * D_MODEL


def _rmsnorm(x, g):
    xf = x.astype(jnp.float32)
    y = xf * lax.rsqrt(jnp.mean(xf * xf, axis=-1, keepdims=True) + EPS)
    return (y * g.astype(jnp.float32)).astype(x.dtype)

def _rope(t, pos):
    d = t.shape[-1]
    half = d // 2
    inv = jnp.exp(-jnp.log(ROPE_BASE) * jnp.arange(half, dtype=jnp.float32) / half)
    ang = pos[:, None] * inv[None, :]
    cos = jnp.cos(ang)[None, :, None, :]
    sin = jnp.sin(ang)[None, :, None, :]
    tf = t.astype(jnp.float32)
    t1, t2 = tf[..., :half], tf[..., half:]
    return jnp.concatenate([t1 * cos - t2 * sin, t1 * sin + t2 * cos], axis=-1).astype(t.dtype)

def _retention(h, w_in, gn_g, w_out):
    B, S, _ = h.shape
    nc = S // CHUNK
    proj = h @ w_in
    q, k, v, g = jnp.split(proj, [RET_QK, 2 * RET_QK, 2 * RET_QK + RET_VW], axis=-1)
    q = q.reshape(B, S, RET_HEADS, RET_DK)
    k = k.reshape(B, S, RET_HEADS, RET_DK)
    v = v.reshape(B, S, RET_HEADS, RET_DV)
    pos = jnp.arange(S, dtype=jnp.float32)
    q = _rope(q, pos)
    k = _rope(k, pos) * (RET_DK ** -0.5)

    def to_chunks(t):
        return t.reshape(B, nc, CHUNK, RET_HEADS, t.shape[-1]).transpose(1, 0, 3, 2, 4)

    qc, kc, vc = to_chunks(q), to_chunks(k), to_chunks(v)
    dt = q.dtype
    log_gamma = jnp.log1p(-jnp.exp2(-5.0 - jnp.arange(RET_HEADS, dtype=jnp.float32)))
    idx = jnp.arange(CHUNK, dtype=jnp.float32)
    intra_decay = jnp.exp(log_gamma[:, None, None] * jnp.abs(idx[:, None] - idx[None, :])).astype(dt)
    key_decay = jnp.exp(log_gamma[:, None] * (CHUNK - 1 - idx)[None, :]).astype(dt)
    query_decay = jnp.exp(log_gamma[:, None] * (idx + 1.0)[None, :]).astype(dt)
    chunk_decay = jnp.exp(log_gamma * CHUNK).astype(dt)

    def step(state, inp):
        qb, kb, vb = inp
        scores = jnp.einsum('bhid,bhjd->bhij', qb, kb) * intra_decay[None]
        o_intra = jnp.einsum('bhij,bhje->bhie', scores, vb)
        o_cross = jnp.einsum('bhid,bhde->bhie', qb, state) * query_decay[None, :, :, None]
        new_state = (state * chunk_decay[None, :, None, None]
                     + jnp.einsum('bhjd,bhje->bhde', kb * key_decay[None, :, :, None], vb))
        return new_state, o_intra + o_cross

    state0 = jnp.zeros((B, RET_HEADS, RET_DK, RET_DV), dt)
    _, o = lax.scan(step, state0, (qc, kc, vc))
    o = o.transpose(1, 0, 3, 2, 4).reshape(B, S, RET_HEADS, RET_DV).astype(jnp.float32)
    mu = jnp.mean(o, axis=-1, keepdims=True)
    var = jnp.mean(jnp.square(o - mu), axis=-1, keepdims=True)
    o = ((o - mu) * lax.rsqrt(var + EPS)).reshape(B, S, RET_VW) * gn_g.astype(jnp.float32)
    y = (jax.nn.silu(g.astype(jnp.float32)) * o).astype(h.dtype)
    return y @ w_out

def _chunk_attention(h, w_in, rel_bias, w_out):
    B, S, _ = h.shape
    nc = S // CHUNK
    q, k, v = jnp.split(h @ w_in, 3, axis=-1)
    q = q.reshape(B, S, ATT_HEADS, ATT_DH)
    k = k.reshape(B, S, ATT_HEADS, ATT_DH)
    v = v.reshape(B, S, ATT_HEADS, ATT_DH)
    pad = ((0, 0), (BAND_PAST, 0), (0, 0), (0, 0))
    kp = jnp.pad(k, pad)
    vp = jnp.pad(v, pad)
    qi = jnp.arange(CHUNK)[:, None]
    kj = jnp.arange(BAND)[None, :]
    rel = kj - BAND_PAST - qi
    bidx = jnp.maximum(rel, -MAX_REL) + MAX_REL
    bias = rel_bias[:, bidx].astype(jnp.float32)
    scale = ATT_DH ** -0.5

    def one_chunk(c):
        start = c * CHUNK
        qb = lax.dynamic_slice_in_dim(q, start, CHUNK, axis=1)
        kb = lax.dynamic_slice_in_dim(kp, start, BAND, axis=1)
        vb = lax.dynamic_slice_in_dim(vp, start, BAND, axis=1)
        s = jnp.einsum('bqhd,bkhd->bhqk', qb, kb).astype(jnp.float32) * scale + bias[None]
        valid = (start - BAND_PAST + jnp.arange(BAND)) >= 0
        s = jnp.where(valid[None, None, None, :], s, -jnp.inf)
        p = jax.nn.softmax(s, axis=-1).astype(vb.dtype)
        return jnp.einsum('bhqk,bkhd->bqhd', p, vb)

    o = lax.map(one_chunk, jnp.arange(nc))
    o = o.transpose(1, 0, 2, 3, 4).reshape(B, S, ATT_HEADS * ATT_DH)
    return o @ w_out

def _sqrelu_mlp(h, w1, w2):
    u = jax.nn.relu(h @ w1)
    return (u * u) @ w2

def second_inputs(seed: int = 0) -> dict:
    key = jax.random.key(seed)
    ks = jax.random.split(key, 12)
    n_ret = (DEPTH_2 + 1) // 2
    n_att = DEPTH_2 // 2
    f = jnp.float32
    x = jax.random.normal(ks[0], (BATCH, SEQ, D_MODEL), f)
    mix_norm_g = 1.0 + 0.02 * jax.random.normal(ks[1], (DEPTH_2, D_MODEL), f)
    ret_w_in = jax.random.normal(ks[2], (n_ret, D_MODEL, 2 * RET_QK + 2 * RET_VW), f) * D_MODEL ** -0.5
    ret_gn_g = 1.0 + 0.02 * jax.random.normal(ks[3], (n_ret, RET_VW), f)
    ret_w_out = jax.random.normal(ks[4], (n_ret, RET_VW, D_MODEL), f) * RET_VW ** -0.5
    att_w_in = jax.random.normal(ks[5], (n_att, D_MODEL, 3 * D_MODEL), f) * D_MODEL ** -0.5
    att_rel_bias = 0.1 * jax.random.normal(ks[6], (n_att, ATT_HEADS, REL_TABLE), f)
    att_w_out = jax.random.normal(ks[7], (n_att, D_MODEL, D_MODEL), f) * D_MODEL ** -0.5
    mlp_norm_g = 1.0 + 0.02 * jax.random.normal(ks[8], (DEPTH_2, D_MODEL), f)
    mlp_w1 = jax.random.normal(ks[9], (DEPTH_2, D_MODEL, D_FF_2), f) * D_MODEL ** -0.5
    mlp_w2 = jax.random.normal(ks[10], (DEPTH_2, D_FF_2, D_MODEL), f) * D_FF_2 ** -0.5
    final_norm_g = 1.0 + 0.02 * jax.random.normal(ks[11], (D_MODEL,), f)
    return {"x": x, "mix_norm_g": mix_norm_g, "ret_w_in": ret_w_in, "ret_gn_g": ret_gn_g,
            "ret_w_out": ret_w_out, "att_w_in": att_w_in, "att_rel_bias": att_rel_bias,
            "att_w_out": att_w_out, "mlp_norm_g": mlp_norm_g, "mlp_w1": mlp_w1,
            "mlp_w2": mlp_w2, "final_norm_g": final_norm_g}

def second_block(x, mix_norm_g, ret_w_in, ret_gn_g, ret_w_out, att_w_in, att_rel_bias,
              att_w_out, mlp_norm_g, mlp_w1, mlp_w2, final_norm_g):
    h = x
    for i in range(DEPTH_2):
        hn = _rmsnorm(h, mix_norm_g[i])
        j = i // N_MIXERS
        if i % N_MIXERS == 0:
            h = h + _retention(hn, ret_w_in[j], ret_gn_g[j], ret_w_out[j])
        else:
            h = h + _chunk_attention(hn, att_w_in[j], att_rel_bias[j], att_w_out[j])
        h = h + _sqrelu_mlp(_rmsnorm(h, mlp_norm_g[i]), mlp_w1[i], mlp_w2[i])
    return _rmsnorm(h, final_norm_g)


def setup_inputs(seed=0):
    out = dict(first_inputs(seed))
    for name, value in second_inputs(seed + 1).items():
        if name != "x":
            out[name + "_2"] = value
    return out


def reference(
    x, p, positions, mix_pre_norm, w_in, q_norm, kv_norm, w_uq, w_ukv, conv_w, attn_group_norm,
    conv_group_norm, w_out, mix_post_norm, ffn_pre_norm, w_gate, w_up, w_down, ffn_post_norm,
    w_ple_proj, ple_norm, w_ple_gate, mix_norm_g_2, ret_w_in_2, ret_gn_g_2, ret_w_out_2,
    att_w_in_2, att_rel_bias_2, att_w_out_2, mlp_norm_g_2, mlp_w1_2, mlp_w2_2, final_norm_g_2,
):
    x = first_block(
        x, p, positions, mix_pre_norm, w_in, q_norm, kv_norm, w_uq, w_ukv, conv_w,
        attn_group_norm, conv_group_norm, w_out, mix_post_norm, ffn_pre_norm, w_gate, w_up,
        w_down, ffn_post_norm, w_ple_proj, ple_norm, w_ple_gate,
    )
    return second_block(
        x, mix_norm_g_2, ret_w_in_2, ret_gn_g_2, ret_w_out_2, att_w_in_2, att_rel_bias_2,
        att_w_out_2, mlp_norm_g_2, mlp_w1_2, mlp_w2_2, final_norm_g_2,
    )


_drawn_inputs = setup_inputs


def setup_inputs(seed=0):
    import zlib

    import numpy as np

    out = dict(_drawn_inputs(seed))
    spreads = {}
    factors = {'ple_norm': 3.065,
     'mix_norm_g_2': 4.024,
     'ret_gn_g_2': 8.0,
     'att_rel_bias_2': 8.0,
     'mlp_norm_g_2': 3.259}
    for name, (base, spread) in spreads.items():
        noise = np.random.default_rng([zlib.crc32(name.encode()), seed]).standard_normal(out[name].shape)
        drawn = base * np.exp(spread * noise) if base else spread * noise
        out[name] = __import__('jax').numpy.asarray(drawn.astype(out[name].dtype))
    for name, factor in factors.items():
        out[name] = (out[name] * factor).astype(out[name].dtype)
    return out
```

```python
from contextlib import ExitStack

import concourse.bass as bass
from concourse import mybir

F32 = mybir.dt.float32
F32R = mybir.dt.float32r
I32 = mybir.dt.int32
ALU = mybir.AluOpType
ACT = mybir.ActivationFunctionType
P = 128
S = 512
D = 1024
KD = D // P
CH = 2048
EPS = 1e-6
MASKED = -3.0e38
FMIN = -3.4028235e38
INV_TWO_PI = 0.15915494309189535
ROUND = 12582912.0
TWO_PI = (6.25, 0.03125, 0.00193500518798828125, 3.0199159819e-07)
SIN_MAX = 3.1415925
ANGLE_STEPS = 9

Q_RANK = KV_RANK = 256
ROPE = 32
CONV = 512
H1 = 8
NOPE = 64
DQ = NOPE + ROPE
CONV0 = Q_RANK + KV_RANK + ROPE
D_FF = 2816
FF_TILES = D_FF // P
PLE = 256
RH = 4
RDK = 256
RDV = 512
RQK = RH * RDK
RVW = RH * RDV
H2 = 16
DH = 64
MAX_REL = 256
REL_TABLE = 320
EXT = 640
MLP_GROUPS = 4

GAIN_ROWS = [("mix_pre_norm", 8), ("q_norm", 2), ("kv_norm", 2), ("conv_w", 12), ("attn_group_norm", 4),
             ("conv_group_norm", 4), ("mix_post_norm", 8), ("ffn_pre_norm", 8), ("ffn_post_norm", 8),
             ("ple_norm", 8), ("mix_norm_g_2", 16), ("ret_gn_g_2", 16), ("mlp_norm_g_2", 16),
             ("final_norm_g_2", 8)]
GAIN_AT = {}
_row = 0
for _name, _n in GAIN_ROWS:
    GAIN_AT[_name] = _row
    _row += _n
N_GAINS = _row


class Phase:

    def __init__(self, prev, groups, iters=1):
        self.chunks, self.groups, self.iters = len(groups), sum(groups), iters
        self.upto = [sum(groups[:j]) for j in range(len(groups) + 1)]
        self.pair = ((self.groups + 1) // 2, self.groups // 2)
        self.prev = prev
        if prev is None:
            self.chunk0, self.group0, self.pair0 = 0, 0, (0, 0)
        else:
            self.chunk0 = prev.chunk0 + prev.chunks * prev.iters
            self.group0 = prev.group0 + prev.groups * prev.iters
            self.pair0 = tuple(prev.pair0[p] + prev.pair[p] * prev.iters for p in (0, 1))
        assert iters == 1 or self.chunks % 2 == 0

    def chunk(self, j, i=0):
        return Chunk(self, j, i)

    def group(self, pos, i=0):
        return Group(self, pos, i)


class Chunk:

    def __init__(self, ph, j, i):
        self.slot = (ph.chunk0 + j) % 2
        self.number = ph.chunk0 + j + i * ph.chunks
        self.loads = ((ph.chunk0 + j) // 2 + 1) * 16 + i * (ph.chunks // 2 * 16)
        self.early = isinstance(self.number, int) and self.number < 2
        if j >= 2:
            self.two_before = ph.group0 + i * ph.groups + ph.upto[j - 1]
        elif j == 1 and not self.early:
            self.two_before = ph.group0 + i * ph.groups
        elif not self.early:
            p = ph.prev
            self.two_before = ph.group0 - (p.upto[-1] - p.upto[-2])


class Group:

    def __init__(self, ph, pos, i):
        self.pair = pos % 2
        self.done = ph.group0 + pos + 1 + i * ph.groups
        self.empty = (ph.pair0[self.pair] + pos // 2) * 2 + i * (2 * ph.pair[self.pair])
        self.virgin = isinstance(self.empty, int) and self.empty == 0

    def bank(self, m):
        return 2 * self.pair + m

    def freed(self, m):
        return self.empty + m + 1


MIX = Phase(None, [1] * 8)
UKV = Phase(MIX, [4])
UQ = Phase(UKV, [4])
WOUT = Phase(UQ, [1] * 4)
FFN = Phase(WOUT, [1] * 12, 2)
FFN_LAST = Phase(FFN, [1] * 10)
PROJ = Phase(FFN_LAST, [4])
GATE = Phase(PROJ, [1] * 4)
RET = Phase(GATE, [1, 1, 1, 1, 1, 1, 2, 2], RH)
MLP_A = Phase(RET, [1] * 8, MLP_GROUPS)
ATT = Phase(MLP_A, [1, 1, 1, 4], H2 // 4)
MLP_B = Phase(ATT, [1] * 8, MLP_GROUPS)
N_CHUNKS = MLP_B.chunk0 + MLP_B.chunks * MLP_B.iters


class Norm:

    def __init__(self, prev, n, split):
        self.n, self.split = n, split
        self.index = prev.index + 1 if prev else 0
        self.sq0 = prev.sq0 + prev.n if prev else 0
        self.acc0 = prev.acc0 + prev.n - 1 if prev else 0
        self.out0 = prev.out0 + prev.split if prev else 0


N_MIX = Norm(None, 8, 8)
N_Q = Norm(N_MIX, 2, 2)
N_KV = Norm(N_Q, 2, 2)
N_CONVG = Norm(N_KV, 4, 4)
N_ATTG = Norm(N_CONVG, 4, 4)
N_POST = Norm(N_ATTG, 8, 0)
N_FFN = Norm(N_POST, 8, 8)
N_FPOST = Norm(N_FFN, 8, 0)
N_PLE = Norm(N_FPOST, 8, 0)
N_RET = Norm(N_PLE, 8, 8)
N_MLPA = Norm(N_RET, 8, 8)
N_ATT = Norm(N_MLPA, 8, 8)
N_MLPB = Norm(N_ATT, 8, 8)
N_FINAL = Norm(N_MLPB, 8, 0)

SEMAPHORES = """x_in p_in rows_in pos_in consts_in kr_in mask_in ext_in ext_out bias_in0 bias_in1 bias_in2
 bias_in3 decay_in ret_tab_in krep_done out_done raw_ready0 raw_ready1 w_hi_ready w_lo_ready group_done
 pair_free0 pair_free1 memset_done gains_t gains_ready x_t x_copied p_t p_hi p_lo
 norm_sq norm_acc norm_stat norm_ln norm_r norm_tmp norm_hi norm_lo
 angle sin_done table kr_hi kr_lo kr_done krope krope_hi krope_lo
 conv conv_out kv_hi sw_done q_nope q_part q_rope q_hi q_lo
 att_s att_mx att_nmx att_exp att_rs att_p att_t att_hi att_lo att_pv att_ohi att_o ext_built mask_set
 post_x o_zero ffn_hi ffn_lo ple_x ple_xhi ple_xlo ple_e
 ret_part ret_tmp ret_qk_hi ret_qk_lo ret_v_hi ret_s ret_sd ret_s_hi ret_s_lo ret_pv ret_o ret_sum
 ret_mean ret_d ret_sq ret_acc ret_var ret_ln ret_rstd ret_y ret_y_hi ret_y_lo
 mlp_sq mlp_hi mlp_lo att_in_hi fin_tmp fin_t fin_copied""".split()


def build(nc, T, out):
    ext_rows = nc.dram_tensor("ext_rows", (H2, P, EXT), F32, kind="Internal").ap()

    with ExitStack() as ctx:
        def sb(name, shape, dt=F32):
            return ctx.enter_context(nc.sbuf_tensor(name, shape, dt))

        s = {name: ctx.enter_context(nc.semaphore(name)) for name in SEMAPHORES}
        raw_ready = [s["raw_ready0"], s["raw_ready1"]]
        pair_free = [s["pair_free0"], s["pair_free1"]]

        x = sb("x", [P, KD, S])
        o_buf = sb("o_buf", [P, 8, S])
        hn_hi = sb("hn_hi", [P, KD, S], F32R)
        hn_lo = sb("hn_lo", [P, KD, S], F32R)
        hid_hi = sb("hid_hi", [P, 16, S], F32R)
        hid_lo = sb("hid_lo", [P, 16, S], F32R)
        raw = sb("raw", [P, 2, CH])
        w_hi = sb("w_hi", [P, 2, CH], F32R)
        w_lo = sb("w_lo", [P, 2, CH], F32R)
        scr = sb("scr", [P, 6, S])
        tab = sb("tab", [P, 2, S])
        aux = sb("aux", [P, 4, S])
        ident = sb("ident", [P, P])
        ones = sb("ones", [P, P])
        gains = sb("gains", [P, N_GAINS])
        ext = sb("ext", [H2, EXT])
        freq = sb("freq", [P, 2])
        eps = sb("eps", [P, 1])
        small = sb("small", [P, 4, 8])
        ps = ctx.enter_context(nc.psum_tensor("ps", [P, 8, S], F32))

        r_bc, ssq, sq, tmp = scr[:, 0, :], scr[:, 1, :], scr[:, 2:4, :], scr[:, 4:6, :]
        sflat = scr[:, :, :].rearrange("p a b -> p (a b)")
        mx, nmx, sm, rs = (small[:, n, :] for n in range(4))

        def gain(name, t):
            at = GAIN_AT[name] + t
            return gains[:, at:at + 1]

        block = ctx.enter_context(nc.Block())

        def ukv_parts():
            slot = UKV.chunk0 % 2
            src = raw[:, slot, :].rearrange("p (k h t c) -> p k t h c", k=2, h=H1, t=2)
            hi_, lo_ = (ap[:, slot, :].rearrange("p (k t h c) -> p k t h c", k=2, t=2, h=H1) for ap in (w_hi, w_lo))
            for k in range(2):
                for t in range(2):
                    yield lo_[:, k, t], hi_[:, k, t], src[:, k, t]

        def uq_parts():
            slot = UQ.chunk0 % 2
            for k in range(2):
                yield (w_lo[:, slot, k * 1024:k * 1024 + 768], w_hi[:, slot, k * 1024:k * 1024 + 768],
                       raw[:, slot, k * 768:k * 768 + 768])
                src = raw[:, slot, k * 768:k * 768 + 768].rearrange("p (h c) -> p h c", h=H1)
                lo_, hi_ = (ap[:, slot, k * 1024 + 768:k * 1024 + 1024].rearrange("p (h c) -> p h c", h=H1)
                            for ap in (w_lo, w_hi))
                for half in (0, 16):
                    yield (lo_[:, :, half:half + 16], hi_[:, :, half:half + 16],
                           src[:, :, NOPE + 16 - half:NOPE + 32 - half])

        S_OFF = [0, 128, 384, 768]
        Q_ORDER = ((3, 1), (2, 3), (0, 3), (1, 4))
        K_ORDER = ((0, 1), (1, 3), (3, 3), (2, 4))

        def score_sb(h, i):
            at = (h % 2) * 1280 + S_OFF[i]
            return sflat[:, at:at + 128 * (i + 1)]

        def score_ps(i):
            b, at = {3: (0, 0), 2: (1, 0), 0: (1, 384), 1: (2, 0)}[i]
            return ps[:, b, at:at + 128 * (i + 1)]

        def trans_ps(j):
            b, at = {0: (3, 0), 1: (4, 0), 3: (4, 384), 2: (5, 0)}[j]
            return ps[:, b, at:at + 512 - 128 * j]

        Q1_HI = [hn_hi[0:DQ, h, :] for h in range(H1)]
        Q1_LO = [hn_lo[0:DQ, h, :] for h in range(H1)]
        K1_HI = [hid_hi[0:DQ, 4 + h, :] for h in range(H1)]
        K1_LO = [hid_lo[0:DQ, 4 + h, :] for h in range(H1)]

        def q2(ap, h):
            return ap[64 * (h % 2):64 * (h % 2) + 64, h // 2, :]

        def k2(ap, h):
            return ap[64 * (h % 2):64 * (h % 2) + 64, 2 + h // 2, :]

        class Attention:

            def __init__(self, base, heads, block2):
                self.base, self.heads, self.block2 = base, heads, block2

            def n(self, h, i=0):
                return self.base + h + i * self.heads

            def first(self, h, i=0):
                return self.base + h == 0

            def qk(self, h):
                if self.block2:
                    return [(q2(hid_hi, h), k2(hid_hi, h)), (q2(hid_hi, h), k2(hid_lo, h)),
                            (q2(hid_lo, h), k2(hid_hi, h))]
                return [(Q1_HI[h], K1_HI[h]), (Q1_HI[h], K1_LO[h]), (Q1_LO[h], K1_HI[h])]

            def v(self, ap, h, j):
                if self.block2:
                    at = (j % 2) * 256 + (h // 2) * P
                    return ap[:, 4 + j // 2, at:at + P]
                return ap[:, 12 + j, (h // 2) * P:(h // 2) * P + P]

            def pt(self, ap, h, j):
                slot = (8 + 4 * (h % 2) if self.block2 else 0) + j
                return ap[:, slot, 0:512 - 128 * j]

            def out_ps(self, h):
                return ps[64 * (h % 2):64 * (h % 2) + 64, 6 + h % 2, :]

        ATT1 = Attention(0, H1, False)
        ATT2 = Attention(H1, 4, True)

        def ret_score(j):
            b, at = {0: (4, 0), 1: (5, 0), 3: (5, 384), 2: (6, 0)}[j]
            return ps[:, b, at:at + 512 - 128 * j]

        def ret_v(ap, j, d):
            at = (j % 2) * 256 + (d % 2) * P
            return ap[:, 4 + 2 * (d // 2) + j // 2, at:at + P]

        @block.sync
        def _(sp):
            def load(c, src, k):
                if not c.early:
                    sp.wait_ge(s["w_lo_ready"], c.number - 1)
                cols = src.shape[-1]
                dst = raw[:, c.slot, 0:k * cols].rearrange("p (k c) -> p k c", k=k)
                sp.dma_start(dst, src).then_inc(raw_ready[c.slot], 16)

            w_in = T["w_in"][0].rearrange("(k p) c -> p k c", p=P)
            xt = o_buf[:, :, :].rearrange("p (t h) s -> p t (h s)", t=4)
            for t in range(4):
                sp.dma_start(xt[:, t, :], T["x"][0, t * P:(t + 1) * P, :]).then_inc(s["x_in"], 16)
            load(MIX.chunk(0), w_in[:, :, 0:256], KD)
            load(MIX.chunk(1), w_in[:, :, 256:512], KD)
            sp.wait_ge(s["gains_t"], 1)
            sp.dma_start(aux[:, 1, :], T["c_causal"]).then_inc(s["mask_in"], 16)
            for half in range(2):
                for n, part in enumerate((1, 2, 0)):
                    at = CONV0 + part * CONV + half * 256
                    load(MIX.chunk(2 + 3 * half + n), w_in[:, :, at:at + 256], KD)
            load(UKV.chunk(0), T["w_ukv"][0].rearrange("(k p) c -> p k c", p=P), 2)
            load(UQ.chunk(0), T["w_uq"][0].rearrange("(k p) c -> p k c", p=P), 2)
            w_out = T["w_out"][0].rearrange("(k p) (m c) -> m p k c", p=P, c=256)
            for m in range(4):
                load(WOUT.chunk(m), w_out[m], KD)

            w_gate = T["w_gate"][0].rearrange("(k p) (m c) -> m p k c", p=P, c=256)
            w_up = T["w_up"][0].rearrange("(k p) (m c) -> m p k c", p=P, c=256)

            def load_ffn(ph, i, g, pairs):
                for j in range(pairs):
                    load(ph.chunk(2 * j, i), w_gate[g * 4 + j], KD)
                    load(ph.chunk(2 * j + 1, i), w_up[g * 4 + j], KD)

            down = T["w_down"][0, 0:2048, :].rearrange("(g k p) (m c) -> g m p k c", p=P, k=8, c=256)
            sp.wait_ge(s["conv_out"], 4)
            sp.dma_start(aux[:, 2:4, :].rearrange("p a (b c) -> p (a b) c", b=2),
                         T["p"][0, 0].rearrange("(t p) c -> p t c", p=P)).then_inc(s["p_in"], 16)
            sp.wait_ge(s["q_lo"], H1)
            sp.dma_start(tab[:, :, :], T["c_ret_rope"]).then_inc(s["ret_tab_in"], 16)
            with sp.Fori(0, 2) as i:
                load_ffn(FFN, i, i, 4)
                for m in range(4):
                    load(FFN.chunk(8 + m, i), down[i, m], 8)
            load_ffn(FFN_LAST, 0, 2, 3)
            down = T["w_down"][0, 2048:D_FF, :].rearrange("(k p) (m c) -> m p k c", p=P, c=256)
            for m in range(4):
                load(FFN_LAST.chunk(6 + m), down[m], 6)
            load(PROJ.chunk(0), T["w_ple_proj"][0].rearrange("(k p) c -> p k c", p=P), 2)
            pg = T["w_ple_gate"][0].rearrange("(k p) (m c) -> m p k c", p=P, c=256)
            for m in range(4):
                load(GATE.chunk(m), pg[m], KD)

            r_in = T["ret_w_in_2"][0]
            r_qk = r_in[:, 0:2 * RQK].rearrange("(k p) (t h c) -> t h p k c", p=P, t=2, c=256)
            r_vg = r_in[:, 2 * RQK:].rearrange("(k p) (t h n c) -> t h n p k c", p=P, t=2, n=2, c=256)
            r_out = T["ret_w_out_2"][0].rearrange("(h k p) (n c) -> h n p k c", p=P, k=4, c=512)
            with sp.Fori(0, RH) as h:
                load(RET.chunk(0, h), r_qk[0, h], KD)
                load(RET.chunk(1, h), r_qk[1, h], KD)
                load(RET.chunk(2, h), r_vg[0, h, 0], KD)
                load(RET.chunk(3, h), r_vg[0, h, 1], KD)
                load(RET.chunk(4, h), r_vg[1, h, 0], KD)
                load(RET.chunk(5, h), r_vg[1, h, 1], KD)
                load(RET.chunk(6, h), r_out[h, 0], 4)
                load(RET.chunk(7, h), r_out[h, 1], 4)

            def load_mlp(ph, layer):
                w1 = T["mlp_w1_2"][layer].rearrange("(k p) (g m c) -> g m p k c", p=P, m=4, c=256)
                w2 = T["mlp_w2_2"][layer].rearrange("(g k p) (m c) -> g m p k c", p=P, k=8, c=256)
                with sp.Fori(0, MLP_GROUPS) as i:
                    for m in range(4):
                        load(ph.chunk(m, i), w1[i, m], KD)
                    for m in range(4):
                        load(ph.chunk(4 + m, i), w2[i, m], 8)

            load_mlp(MLP_A, 0)
            sp.wait_ge(s["ext_built"], 3)
            sp.dma_start(ext_rows, ext[:, :].unsqueeze(1).to_broadcast([H2, P, EXT])).then_inc(s["ext_out"], 16)
            sp.wait_ge(s["ext_out"], 16)
            sp.wait_ge(s["mask_set"], 4)
            a_in = T["att_w_in_2"][0].rearrange("(k p) (t g c) -> t g p k c", p=P, t=3, c=256)
            a_out = T["att_w_out_2"][0].rearrange("(g k p) c -> g p k c", p=P, k=2)
            ext_h = ext_rows.rearrange("(g h) q e -> g h (q e)", h=4)
            with sp.Fori(0, H2 // 4) as g:
                for t in range(2):
                    load(ATT.chunk(t, g), a_in[t, g], KD)
                sp.wait_ge(s["att_mx"], H1 * 4 + g * 16)
                for h in range(4):
                    for q0, width in ((0, 448), (64, 512)):
                        rows = ext_h[g, h, 0:P * (EXT - 1)].rearrange("(q e) -> q e", e=EXT - 1)
                        sp.dma_start(aux[q0:q0 + 64, h, 0:width], rows[q0:q0 + 64, 127:127 + width])\
                            .then_inc(s[f"bias_in{h}"], 16)
                load(ATT.chunk(2, g), a_in[2, g], KD)
                load(ATT.chunk(3, g), a_out[g], 2)
            load_mlp(MLP_B, 1)

            sp.wait_ge(s["fin_copied"], 8)
            for t in range(4):
                sp.dma_start(out[0, t * P:(t + 1) * P, :], xt[:, t, :]).then_inc(s["out_done"], 16)
            sp.wait_ge(s["out_done"], 64)

        @block.gpsimd
        def _(pool):
            pool.memset(ones[:, :], 1.0).then_inc(s["memset_done"], 1)
            pool.memset(eps[:, :], EPS).then_inc(s["memset_done"], 1)
            pool.dma_start(ident[:, :], T["c_ident"]).then_inc(s["consts_in"], 16)
            pool.dma_start(freq[:, :], T["c_freq"]).then_inc(s["consts_in"], 16)
            stage = aux[:, 1, 0:P]
            for name, n in GAIN_ROWS:
                at = GAIN_AT[name]
                lead = " ".join("abc"[:len(T[name].shape) - 1])
                rows = T[name].rearrange(f"{lead} (t p) -> ({lead} t) p", p=P)
                pool.dma_start(stage[at:at + n, :], rows).then_inc(s["rows_in"], 16)
            pool.dma_start(tab[:, 0, :].bitcast(I32), bass.AP(T["positions"].tensor, 0, [[0, P], [1, S]]))\
                .then_inc(s["pos_in"], 16)
            kr_raw = aux[:, 0, :].rearrange("p (k c) -> p k c", k=KD)
            w_in = T["w_in"][0].rearrange("(k p) c -> p k c", p=P)
            at = Q_RANK + KV_RANK
            for dst, src, n in ((0, 0, 32), (32, 16, 16), (48, 0, 16)):
                pool.dma_start(kr_raw[:, :, dst:dst + n], w_in[:, :, at + src:at + src + n])\
                    .then_inc(s["kr_in"], 16)
            pool.dma_start(ext[:, 255:255 + REL_TABLE], T["att_rel_bias_2"][0]).then_inc(s["ext_in"], 16)

            def lo(number, slot):
                pool.wait_ge(s["w_hi_ready"], number + 1)
                for n in range(4):
                    at = slice(n * 512, n * 512 + 512)
                    ins = pool.tensor_tensor(w_lo[:, slot, at], raw[:, slot, at], w_hi[:, slot, at].bitcast(F32),
                                             ALU.subtract)
                ins.then_inc(s["w_lo_ready"], 1)

            for c in range(UKV.chunk0):
                lo(c, c % 2)
            for ph, parts in ((UKV, ukv_parts()), (UQ, uq_parts())):
                pool.wait_ge(s["w_hi_ready"], ph.chunk0 + 1)
                for w_lo_part, w_hi_part, raw_part in parts:
                    ins = pool.tensor_tensor(w_lo_part, raw_part, w_hi_part.bitcast(F32), ALU.subtract)
                ins.then_inc(s["w_lo_ready"], 1)
            first = UQ.chunk0 + 1
            loops = (N_CHUNKS - first) // 2
            with pool.Fori(0, loops) as i:
                lo(first + 2 * i, first % 2)
                lo(first + 1 + 2 * i, (first + 1) % 2)
            for c in range(first + 2 * loops, N_CHUNKS):
                lo(c, c % 2)

        @block.tensor
        def _(pe):
            def chunk_ready(c):
                pe.wait_ge(s["w_lo_ready"], c.number + 1)

            def three(o, hi, lo, rhs_hi, rhs_lo, start, stop):
                pe.matmul(o, hi, rhs_hi, start=start, stop=False, skip_group_check=True)
                pe.matmul(o, hi, rhs_lo, start=False, stop=False, skip_group_check=True)
                return pe.matmul(o, lo, rhs_hi, start=False, stop=stop, skip_group_check=True)

            def group_empty(g):
                if not g.virgin:
                    pe.wait_ge(pair_free[g.pair], g.empty)

            def product(c, g, kt, cols, m0, act_hi, act_lo, act_wait=None):
                hi = w_hi[:, c.slot, 0:kt * cols].rearrange("p (k c) -> p k c", k=kt)
                lo = w_lo[:, c.slot, 0:kt * cols].rearrange("p (k c) -> p k c", k=kt)
                group_empty(g)
                for k in range(kt):
                    if act_wait is not None:
                        act_wait(k)
                    for m in range(2):
                        at = slice((m0 + m) * P, (m0 + m) * P + P)
                        ins = three(ps[:, g.bank(m), :], hi[:, k, at], lo[:, k, at],
                                    act_hi[:, k, :], act_lo[:, k, :], k == 0, k == kt - 1)
                ins.then_inc(s["group_done"], 1)

            def normed(norm):
                return lambda k: pe.wait_ge(s["norm_lo"], norm.out0 + k + 1)

            def stat(norm):
                pe.wait_ge(s["norm_acc"], norm.acc0 + norm.n - 1)
                if norm.index:
                    pe.wait_ge(s["norm_ln"], norm.index)
                pe.matmul(ps[:, 7, :], ones[:, :], ssq, start=True, stop=True).then_inc(s["norm_stat"], 1)

            pe.wait_ge(s["rows_in"], 16 * len(GAIN_ROWS))
            pe.wait_ge(s["consts_in"], 32)
            pe.transpose(ps[:, 6, 0:N_GAINS], aux[0:N_GAINS, 1, 0:P], ident[0:N_GAINS, 0:N_GAINS])\
                .then_inc(s["gains_t"], 1)
            xt = o_buf[:, :, :].rearrange("p (t h) s -> p t (h s)", t=4)
            pe.wait_ge(s["x_in"], 64)
            for f in range(KD):
                if f >= 2:
                    pe.wait_ge(s["x_copied"], f - 1)
                for t in range(4):
                    ins = pe.transpose(ps[:, 4 + f % 2, t * P:(t + 1) * P], xt[:, t, f * P:(f + 1) * P],
                                       ident[:, :])
                ins.then_inc(s["x_t"], 1)
            pe.wait_ge(s["memset_done"], 2)
            stat(N_MIX)

            chunk_ready(MIX.chunk(0))
            product(MIX.chunk(0), MIX.group(0), KD, 256, 0, hn_hi, hn_lo, normed(N_MIX))
            chunk_ready(MIX.chunk(1))
            product(MIX.chunk(1), MIX.group(1), KD, 256, 0, hn_hi, hn_lo)
            pe.wait_ge(s["kr_lo"], 1)
            for k in range(KD):
                ins = three(ps[:, 4, :], hid_hi[:, 4 + k // 4, (k % 4) * P:(k % 4) * P + P],
                            hid_lo[:, 4 + k // 4, (k % 4) * P:(k % 4) * P + P],
                            hn_hi[:, k, :], hn_lo[:, k, :], k == 0, k == KD - 1)
            ins.then_inc(s["kr_done"], 1)
            for n in range(2, 8):
                chunk_ready(MIX.chunk(n))
                product(MIX.chunk(n), MIX.group(n), KD, 256, 0, hn_hi, hn_lo)
                if n == 2:
                    stat(N_Q)
                if n == 3:
                    stat(N_KV)
            c = UKV.chunk(0)
            chunk_ready(c)
            hi = w_hi[:, c.slot, :].rearrange("p (k t c) -> p k t c", k=2, t=2)
            lo = w_lo[:, c.slot, :].rearrange("p (k t c) -> p k t c", k=2, t=2)
            pe.wait_ge(s["norm_lo"], N_KV.out0 + 2)
            for n in range(2):
                g = UKV.group(n)
                group_empty(g)
                for m in range(2):
                    heads = slice((2 * n + m) * P, (2 * n + m) * P + P)
                    for k in range(2):
                        ins = three(ps[:, g.bank(m), :], hi[:, k, 0, heads], lo[:, k, 0, heads],
                                    hid_hi[:, 2 + k, :], hid_lo[:, 2 + k, :], k == 0, k == 1)
                ins.then_inc(s["group_done"], 1)
            for n in range(2):
                g = UKV.group(2 + n)
                group_empty(g)
                for m in range(2):
                    t = slice((2 * n + m) * P, (2 * n + m) * P + P)
                    for k in range(2):
                        ins = three(ps[:, g.bank(m), :], hid_hi[:, 2 + k, t], hid_lo[:, 2 + k, t],
                                    hi[:, k, 1, :], lo[:, k, 1, :], k == 0, k == 1)
                ins.then_inc(s["group_done"], 1)
            c = UQ.chunk(0)
            chunk_ready(c)
            hi = w_hi[:, c.slot, :].rearrange("p (k c) -> p k c", k=2)
            lo = w_lo[:, c.slot, :].rearrange("p (k c) -> p k c", k=2)
            pe.wait_ge(s["norm_lo"], N_Q.out0 + 2)
            pe.wait_ge(s["krope"], 2)
            for m in range(2):
                at = slice(768 + m * P, 768 + m * P + P)
                for k in range(2):
                    ins = three(ps[:, 4 + m, :], hi[:, k, at], lo[:, k, at], hid_hi[:, k, :], hid_lo[:, k, :],
                                k == 0, k == 1)
                ins.then_inc(s["sw_done"], 1)
            for n in range(4):
                g = UQ.group(n)
                group_empty(g)
                for m in range(2):
                    at = slice((2 * n + m) * DQ, (2 * n + m) * DQ + DQ)
                    for k in range(2):
                        ins = three(ps[0:DQ, g.bank(m), :], hi[:, k, at], lo[:, k, at],
                                    hid_hi[:, k, :], hid_lo[:, k, :], k == 0, k == 1)
                ins.then_inc(s["group_done"], 1)

            def scores(a, h, i=0):
                if not a.first(h, i):
                    pe.wait_ge(s["att_mx"], a.n(h, i) * 4)
                for t, _ in Q_ORDER:
                    for n, (q, k) in enumerate(a.qk(h)):
                        ins = pe.matmul(score_ps(t), q[:, t * P:(t + 1) * P], k[:, 0:(t + 1) * P],
                                        start=(n == 0), stop=(n == 2), skip_group_check=True)
                    ins.then_inc(s["att_s"], 1)

            def transposes(a, h, i=0):
                if not a.first(h, i):
                    pe.wait_ge(s["att_lo"], a.n(h, i) * 4)
                pe.wait_ge(s["att_p"], a.n(h, i) * 4 + 4)
                for j, _ in K_ORDER:
                    for t in range(j, 4):
                        ins = pe.transpose(trans_ps(j)[:, (t - j) * P:(t - j + 1) * P],
                                           score_sb(h, t)[:, j * P:(j + 1) * P], ident[:, :])
                    ins.then_inc(s["att_t"], 1)

            def values(a, h, i=0):
                if h >= 2 or a.block2:
                    pe.wait_ge(s["att_o"], a.n(h, i) - 1)
                for n, (j, _) in enumerate(K_ORDER):
                    pe.wait_ge(s["att_lo"], a.n(h, i) * 4 + n + 1)
                    ins = three(ps[:, 6 + h % 2, j * P:], a.v(hid_hi, h, j), a.v(hid_lo, h, j),
                                a.pt(hid_hi, h, j), a.pt(hid_lo, h, j), n == 0, n == 3)
                ins.then_inc(s["att_pv"], 1)

            def attend(a, i=0):
                scores(a, 0, i)
                for h in range(a.heads):
                    if h + 1 < a.heads:
                        scores(a, h + 1, i)
                    transposes(a, h, i)
                    values(a, h, i)

            for n in (2, 3):
                pe.wait_ge(pair_free[n % 2], UKV.group(n).freed(1))
            pe.wait_ge(s["krep_done"], 32)
            pe.wait_ge(s["q_lo"], H1)
            attend(ATT1)
            stat(N_CONVG)
            stat(N_ATTG)
            for m in range(4):
                chunk_ready(WOUT.chunk(m))
                if m == 0:
                    pe.wait_ge(s["norm_lo"], N_CONVG.out0 + 4)
                product(WOUT.chunk(m), WOUT.group(m), KD, 256, 0, hn_hi, hn_lo,
                        (lambda k: k < 4 and pe.wait_ge(s["norm_lo"], N_ATTG.out0 + k + 1)) if m == 0 else None)
            stat(N_POST)
            stat(N_FFN)

            def ffn(ph, i, g_hid, kt):
                for j in range(kt // 2):
                    for n in range(2):
                        chunk_ready(ph.chunk(2 * j + n, i))
                        product(ph.chunk(2 * j + n, i), ph.group(2 * j + n, i), KD, 256, 0, hn_hi, hn_lo,
                                normed(N_FFN) if j == 0 and n == 0 else None)
                for m in range(4):
                    c = ph.chunk(kt + m, i)
                    chunk_ready(c)
                    product(c, ph.group(kt + m, i), kt, 256, 0, hid_hi, hid_lo,
                            (lambda k: pe.wait_ge(s["ffn_lo"], g_hid + k + 1)) if m == 0 else None)

            pe.wait_ge(s["p_in"], 16)
            pt = aux[:, 2:4, :].rearrange("p a (b c) -> p (a b) c", b=2)
            for f in range(2):
                for t in range(4):
                    ins = pe.transpose(ps[:, 4 + f, t * P:(t + 1) * P], pt[:, t, f * P:(f + 1) * P], ident[:, :])
                ins.then_inc(s["p_t"], 1)
            with pe.Fori(0, 2) as i:
                ffn(FFN, i, i * 8, 8)
            ffn(FFN_LAST, 0, 16, 6)
            stat(N_FPOST)
            c = PROJ.chunk(0)
            chunk_ready(c)
            pe.wait_ge(s["p_lo"], 2)
            for n in range(4):
                product(c, PROJ.group(n), 2, 1024, 2 * n, hid_hi[:, 8:10, :], hid_lo[:, 8:10, :])
            stat(N_PLE)
            for m in range(4):
                chunk_ready(GATE.chunk(m))
                product(GATE.chunk(m), GATE.group(m), KD, 256, 0, hn_hi, hn_lo,
                        (lambda k: pe.wait_ge(s["ple_xlo"], k + 1)) if m == 0 else None)

            stat(N_RET)
            pe.wait_ge(s["norm_lo"], N_RET.out0 + 8)

            def token_major(c, g):
                hi = w_hi[:, c.slot, :].rearrange("p (k c) -> p k c", k=KD)
                lo = w_lo[:, c.slot, :].rearrange("p (k c) -> p k c", k=KD)
                group_empty(g)
                for t in range(4):
                    o = ps[:, g.bank(t // 2), (t % 2) * 256:(t % 2) * 256 + 256]
                    for k in range(KD):
                        at = slice(t * P, t * P + P)
                        ins = three(o, hn_hi[:, k, at], hn_lo[:, k, at], hi[:, k, :], lo[:, k, :],
                                    k == 0, k == KD - 1)
                ins.then_inc(s["group_done"], 1)

            with pe.Fori(0, RH) as h:
                for n in range(2):
                    chunk_ready(RET.chunk(n, h))
                    product(RET.chunk(n, h), RET.group(n, h), KD, 256, 0, hn_hi, hn_lo)
                chunk_ready(RET.chunk(2, h))
                token_major(RET.chunk(2, h), RET.group(2, h))
                pe.wait_ge(s["ret_qk_lo"], h * 4 + 4)
                for j, _ in K_ORDER:
                    o = ret_score(j)
                    for k in range(2):
                        at = slice(j * P, j * P + P)
                        ins = three(o, hid_hi[:, 2 + k, at], hid_lo[:, 2 + k, at],
                                    hid_hi[:, k, j * P:], hid_lo[:, k, j * P:], k == 0, k == 1)
                    ins.then_inc(s["ret_s"], 1)
                chunk_ready(RET.chunk(3, h))
                token_major(RET.chunk(3, h), RET.group(3, h))
                pe.wait_ge(s["ret_s_lo"], h * 4 + 4)
                for n in (2, 3):
                    pe.wait_ge(pair_free[n % 2], RET.group(n, h).freed(1))
                for d in range(4):
                    for j in range(4):
                        ins = three(ps[:, 4 + d, j * P:], ret_v(hid_hi, j, d), ret_v(hid_lo, j, d),
                                    hid_hi[:, 8 + j, j * P:], hid_lo[:, 8 + j, j * P:], j == 0, j == 3)
                    ins.then_inc(s["ret_pv"], 1)
                chunk_ready(RET.chunk(4, h))
                product(RET.chunk(4, h), RET.group(4, h), KD, 256, 0, hn_hi, hn_lo)
                pe.wait_ge(s["ret_sum"], h * 3 + 3)
                pe.matmul(ps[:, 4, :], ones[:, :], ssq, start=True, stop=True).then_inc(s["ret_mean"], 1)
                chunk_ready(RET.chunk(5, h))
                product(RET.chunk(5, h), RET.group(5, h), KD, 256, 0, hn_hi, hn_lo)
                pe.wait_ge(s["ret_acc"], h * 3 + 3)
                pe.matmul(ps[:, 5, :], ones[:, :], ssq, start=True, stop=True).then_inc(s["ret_var"], 1)
                for n in range(4):
                    c = RET.chunk(6 + n // 2, h)
                    if n % 2 == 0:
                        chunk_ready(c)
                    product(c, RET.group(6 + n, h), 4, 512, 2 * (n % 2), hid_hi[:, 12:16, :],
                            hid_lo[:, 12:16, :],
                            (lambda k: pe.wait_ge(s["ret_y_lo"], h * 4 + k + 1)) if n == 0 else None)

            def mlp(ph, norm, base):
                stat(norm)
                with pe.Fori(0, MLP_GROUPS) as i:
                    for m in range(4):
                        chunk_ready(ph.chunk(m, i))
                        product(ph.chunk(m, i), ph.group(m, i), KD, 256, 0, hn_hi, hn_lo,
                                normed(norm) if m == 0 else None)
                    for m in range(4):
                        chunk_ready(ph.chunk(4 + m, i))
                        product(ph.chunk(4 + m, i), ph.group(4 + m, i), 8, 256, 0, hid_hi, hid_lo,
                                (lambda k: pe.wait_ge(s["mlp_lo"], base + i * 8 + k + 1)) if m == 0 else None)

            mlp(MLP_A, N_MLPA, 0)
            stat(N_ATT)
            pe.wait_ge(s["norm_lo"], N_ATT.out0 + 8)
            with pe.Fori(0, H2 // 4) as i:
                for n in range(2):
                    chunk_ready(ATT.chunk(n, i))
                    product(ATT.chunk(n, i), ATT.group(n, i), KD, 256, 0, hn_hi, hn_lo)
                chunk_ready(ATT.chunk(2, i))
                token_major(ATT.chunk(2, i), ATT.group(2, i))
                for n in (1, 2):
                    pe.wait_ge(pair_free[n % 2], ATT.group(n, i).freed(1))
                attend(ATT2, i)
                c = ATT.chunk(3, i)
                chunk_ready(c)
                pe.wait_ge(s["att_o"], ATT2.n(3, i) + 1)
                for n in range(4):
                    product(c, ATT.group(3 + n, i), 2, 1024, 2 * n, hid_hi[:, 6:8, :], hid_lo[:, 6:8, :])
            mlp(MLP_B, N_MLPB, MLP_GROUPS * 8)
            stat(N_FINAL)
            for f in range(KD):
                pe.wait_ge(s["fin_tmp"], f + 1)
                if f >= 2:
                    pe.wait_ge(s["fin_copied"], f - 1)
                for t in range(4):
                    ins = pe.transpose(ps[:, 4 + f % 2, t * P:(t + 1) * P], tmp[:, f % 2, t * P:(t + 1) * P],
                                       ident[:, :])
                ins.then_inc(s["fin_t"], 1)

        @block.scalar
        def _(act):
            def split(c):
                act.wait_ge(raw_ready[c.slot], c.loads)
                if not c.early:
                    act.wait_ge(s["group_done"], c.two_before)
                act.activation(w_hi[:, c.slot, :], raw[:, c.slot, :], ACT.Copy).then_inc(s["w_hi_ready"], 1)

            def group_ready(g):
                act.wait_ge(s["group_done"], g.done)

            def copy_out(g, m, dst, func=ACT.Copy):
                act.activation(dst, ps[:, g.bank(m), :], func).then_inc(pair_free[g.pair], 1)

            def square(norm, t, src):
                if t == 0:
                    if norm.index:
                        act.wait_ge(s["norm_stat"], norm.index)
                    act.activation(ssq, src, ACT.Square).then_inc(s["norm_sq"], 1)
                else:
                    used = norm.acc0 + max(0, t - 2)
                    if used:
                        act.wait_ge(s["norm_acc"], used)
                    act.activation(sq[:, t % 2, :], src, ACT.Square).then_inc(s["norm_sq"], 1)

            def rsqrt(norm, dim):
                act.wait_ge(s["norm_stat"], norm.index + 1)
                act.activation(r_bc, ps[:, 7, :], ACT.Ln, scale=1.0 / dim, bias=eps[:, 0:1])\
                    .then_inc(s["norm_ln"], 1)
                act.wait_ge(s["norm_ln"], norm.index + 1)
                act.activation(r_bc, r_bc, ACT.Exp, scale=-0.5).then_inc(s["norm_r"], 1)

            def hi_tile(norm, t, dst):
                act.wait_ge(s["norm_tmp"], norm.out0 + t + 1)
                act.activation(dst, tmp[:, t % 2, :], ACT.Copy).then_inc(s["norm_hi"], 1)

            def x_squares(norm, g_last):
                for m in range(2):
                    act.wait_ge(pair_free[g_last.pair], g_last.freed(m))
                for t in range(KD):
                    square(norm, t, x[:, t, :])

            act.wait_ge(s["gains_t"], 1)
            act.activation(gains[:, :], ps[:, 6, 0:N_GAINS], ACT.Copy).then_inc(s["gains_ready"], 1)
            act.wait_ge(s["angle"], ANGLE_STEPS)
            act.activation(tab[:, 1, :], aux[:, 2, :], ACT.Sin).then_inc(s["sin_done"], 1)
            act.activation(tab[:, 0, :], aux[:, 2, :], ACT.Sin, scale=0.5).then_inc(s["sin_done"], 1)
            act.preload_act_table_set("natural_log_exp_and_others")
            kr_dst = hid_hi[:, 4:6, :].rearrange("p a (k c) -> p (a k) c", c=P)
            kr_raw = aux[:, 0, :].rearrange("p (k c) -> p k c", k=KD)
            act.wait_ge(s["kr_in"], 48)
            act.activation(kr_dst[:, :, 0:64], kr_raw, ACT.Copy)
            act.activation(kr_dst[:, :, 64:128], kr_raw, ACT.Copy).then_inc(s["kr_hi"], 1)
            for f in range(KD):
                act.wait_ge(s["x_t"], f + 1)
                act.activation(x[:, f, :], ps[:, 4 + f % 2, :], ACT.Copy).then_inc(s["x_copied"], 1)
                act.wait_ge(s["x_copied"], f + 1)
                square(N_MIX, f, x[:, f, :])
            act.wait_ge(s["memset_done"], 2)
            rsqrt(N_MIX, D)
            split(MIX.chunk(0))
            for t in range(KD):
                hi_tile(N_MIX, t, hn_hi[:, t, :])

            split(MIX.chunk(1))
            g = MIX.group(0)
            group_ready(g)
            for m in range(2):
                square(N_Q, m, ps[:, g.bank(m), :])
                copy_out(g, m, o_buf[:, m, :])
            split(MIX.chunk(2))
            g = MIX.group(1)
            group_ready(g)
            for m in range(2):
                copy_out(g, m, o_buf[:, 2 + m, :])
            split(MIX.chunk(3))
            g = MIX.group(2)
            group_ready(g)
            for m in range(2):
                copy_out(g, m, o_buf[:, 4 + m, :])
            rsqrt(N_Q, Q_RANK)
            for t in range(2):
                hi_tile(N_Q, t, hid_hi[:, t, :])
            for t in range(2):
                act.wait_ge(pair_free[MIX.group(1).pair], MIX.group(1).freed(t))
                square(N_KV, t, o_buf[:, 2 + t, :])
            split(MIX.chunk(4))
            rsqrt(N_KV, KV_RANK)
            for t in range(2):
                hi_tile(N_KV, t, hid_hi[:, 2 + t, :])
            split(MIX.chunk(5))
            act.wait_ge(s["krope"], 3)
            act.activation(hid_hi[64:96, 4, :], aux[64:96, 0, :], ACT.Copy).then_inc(s["krope_hi"], 1)
            act.wait_ge(s["krope_hi"], 1)
            act.wait_ge(s["krope_lo"], 1)
            for ap in (hid_hi[:, :, :].bitcast(F32), hid_lo[:, :, :].bitcast(F32)):
                act.dma_start(ap[64:96, 5:12, :], ap[64:96, 4:5, :].to_broadcast([32, 7, S]))\
                    .then_inc(s["krep_done"], 16)
            split(MIX.chunk(6))
            g = MIX.group(5)
            group_ready(g)
            for m in range(2):
                copy_out(g, m, o_buf[:, 6 + m, :])
            split(MIX.chunk(7))

            for c, parts in ((UKV.chunk(0), ukv_parts()), (UQ.chunk(0), uq_parts())):
                act.wait_ge(raw_ready[c.slot], c.loads)
                act.wait_ge(s["group_done"], c.two_before)
                for _w_lo, w_hi_part, raw_part in parts:
                    ins = act.activation(w_hi_part, raw_part, ACT.Copy)
                ins.then_inc(s["w_hi_ready"], 1)
            for n in range(2):
                g = UKV.group(n)
                group_ready(g)
                for m in range(2):
                    for half in range(2):
                        act.activation(hid_hi[0:NOPE, 4 + 4 * n + 2 * m + half, :],
                                       ps[64 * half:64 * half + 64, g.bank(m), :], ACT.Copy)\
                            .then_inc(s["kv_hi"], 1)
            for n in range(2):
                g = UKV.group(2 + n)
                group_ready(g)
                for m in range(2):
                    act.activation(hid_hi[:, 12 + 2 * n + m, :], ps[:, g.bank(m), :], ACT.Copy)\
                        .then_inc(s["kv_hi"], 1)
            split(WOUT.chunk(0))
            for h in range(H1):
                g = UQ.group(h // 2)
                group_ready(g)
                if h >= 2:
                    act.wait_ge(s["q_lo"], h - 1)
                act.activation(tmp[0:NOPE, h % 2, :], ps[0:NOPE, g.bank(h % 2), :], ACT.Copy)\
                    .then_inc(s["q_nope"], 1)
                act.wait_ge(s["q_nope"], h + 1)
                act.wait_ge(s["q_rope"], h + 1)
                act.activation(hn_hi[0:DQ, h, :], tmp[0:DQ, h % 2, :], ACT.Copy).then_inc(s["q_hi"], 1)

            def exps(a, h, i=0):
                act.wait_ge(s["att_nmx"], a.n(h, i) + 1)
                for t in range(4):
                    col = slice(4 * (h % 2) + t, 4 * (h % 2) + t + 1)
                    act.activation(score_sb(h, t), score_sb(h, t), ACT.Exp, bias=nmx[:, col],
                                   accum_out=sm[:, col]).then_inc(s["att_exp"], 1)

            def prob_hi(a, h, i=0):
                if a.block2:
                    act.wait_ge(s["att_pv"], a.n(h, i) - 1)
                elif h:
                    act.wait_ge(s["att_pv"], h)
                for j, done in K_ORDER:
                    act.wait_ge(s["att_t"], a.n(h, i) * 4 + done)
                    act.activation(a.pt(hid_hi, h, j), trans_ps(j), ACT.Copy).then_inc(s["att_hi"], 1)

            def attend(a, empty_out, i=0):
                exps(a, 0, i)
                for h in range(a.heads):
                    prob_hi(a, h, i)
                    if h + 1 < a.heads:
                        exps(a, h + 1, i)
                    act.wait_ge(s["att_pv"], a.n(h, i) + 1)
                    empty_out(h)

            def out_plain(h):
                act.activation(o_buf[64 * (h % 2):64 * (h % 2) + 64, h // 2, :], ATT1.out_ps(h), ACT.Copy)\
                    .then_inc(s["att_o"], 1)

            def out_hi(h):
                act.activation(hid_hi[64 * (h % 2):64 * (h % 2) + 64, 6 + h // 2, :], ATT2.out_ps(h), ACT.Copy)\
                    .then_inc(s["att_ohi"], 1)

            attend(ATT1, out_plain)

            act.wait_ge(s["conv_out"], 4)
            for t in range(4):
                square(N_CONVG, t, o_buf[:, 4 + t, :])
            rsqrt(N_CONVG, CONV)
            for t in range(4):
                hi_tile(N_CONVG, t, hn_hi[:, 4 + t, :])
            act.wait_ge(s["att_o"], H1)
            for t in range(4):
                square(N_ATTG, t, o_buf[:, t, :])
            rsqrt(N_ATTG, CONV)
            for t in range(4):
                hi_tile(N_ATTG, t, hn_hi[:, t, :])
            for m in range(4):
                split(WOUT.chunk(m + 1))
                g = WOUT.group(m)
                group_ready(g)
                for t in range(2):
                    square(N_POST, 2 * m + t, ps[:, g.bank(t), :])
                    copy_out(g, t, o_buf[:, 2 * m + t, :])
            rsqrt(N_POST, D)
            for t in range(KD):
                act.wait_ge(s["post_x"], 2 * t + 2)
                square(N_FFN, t, x[:, t, :])
            rsqrt(N_FFN, D)
            for t in range(KD):
                hi_tile(N_FFN, t, hn_hi[:, t, :])
            for f in range(2):
                act.wait_ge(s["p_t"], f + 1)
                act.activation(hid_hi[:, 8 + f, :], ps[:, 4 + f, :], ACT.Copy).then_inc(s["p_hi"], 1)

            def gate_up(ph, i, g_hid, pairs):
                for j in range(pairs):
                    gate, up = ph.group(2 * j, i), ph.group(2 * j + 1, i)
                    split(ph.chunk(2 * j + 1, i))
                    group_ready(gate)
                    if j:
                        act.wait_ge(s["ffn_lo"], g_hid + 2 * j)
                    for m in range(2):
                        copy_out(gate, m, sq[:, m, :], ACT.Silu)
                    split(ph.chunk(2 * j + 2, i))
                    for m in range(2):
                        act.wait_ge(pair_free[up.pair], up.freed(m))
                        act.activation(hid_hi[:, 2 * j + m, :], sq[:, m, :], ACT.Copy).then_inc(s["ffn_hi"], 1)

            act.preload_act_table_set("silu_and_others")
            with act.Fori(0, 2) as i:
                gate_up(FFN, i, i * 8, 4)
                for m in range(4):
                    split(FFN.chunk(9 + m, i))
            gate_up(FFN_LAST, 0, 16, 3)
            for m in range(4):
                split(FFN_LAST.chunk(7 + m))
                g = FFN_LAST.group(6 + m)
                for t in range(2):
                    act.wait_ge(pair_free[g.pair], g.freed(t))
                    square(N_FPOST, 2 * m + t, o_buf[:, 2 * m + t, :])
            act.preload_act_table_set("natural_log_exp_and_others")
            rsqrt(N_FPOST, D)

            split(GATE.chunk(0))
            for n in range(4):
                g = PROJ.group(n)
                for m in range(2):
                    t = 2 * n + m
                    act.wait_ge(s["ple_x"], 2 * t + 2)
                    act.activation(hn_hi[:, t, :], x[:, t, :], ACT.Copy).then_inc(s["ple_xhi"], 1)
                group_ready(g)
                for m in range(2):
                    square(N_PLE, 2 * n + m, ps[:, g.bank(m), :])
                    copy_out(g, m, o_buf[:, 2 * n + m, :])
            rsqrt(N_PLE, D)
            act.preload_act_table_set("sigmoid_and_others")
            for m in range(4):
                split(GATE.chunk(m + 1))
                g = GATE.group(m)
                group_ready(g)
                for t in range(2):
                    if m:
                        act.wait_ge(s["ple_e"], 3 * (2 * m + t - 1))
                    copy_out(g, t, aux[:, 2 + t, :], ACT.Sigmoid)
                for t in range(2):
                    act.wait_ge(s["ple_e"], 3 * (2 * m + t + 1))
                    square(N_RET, 2 * m + t, x[:, 2 * m + t, :])
            act.dma_start(aux[:, :, :], T["c_decay"]).then_inc(s["decay_in"], 16)
            act.preload_act_table_set("natural_log_exp_and_others")
            rsqrt(N_RET, D)
            for t in range(KD):
                hi_tile(N_RET, t, hn_hi[:, t, :])

            with act.Fori(0, RH) as h:
                for n in range(2):
                    split(RET.chunk(n + 1, h))
                    for t in range(2):
                        act.wait_ge(s["ret_tmp"], h * 4 + 2 * n + t + 1)
                        act.activation(hid_hi[:, 2 * n + t, :], tmp[:, t, :], ACT.Copy)\
                            .then_inc(s["ret_qk_hi"], 1)
                split(RET.chunk(3, h))
                g = RET.group(2, h)
                group_ready(g)
                for m in range(2):
                    act.activation(hid_hi[:, 4 + m, :], ps[:, g.bank(m), :], ACT.Copy).then_inc(s["ret_v_hi"], 1)
                for n, (j, _) in enumerate(K_ORDER):
                    act.wait_ge(s["ret_sd"], h * 4 + n + 1)
                    act.activation(hid_hi[:, 8 + j, j * P:], o_buf[:, j, j * P:], ACT.Copy)\
                        .then_inc(s["ret_s_hi"], 1)
                split(RET.chunk(4, h))
                g = RET.group(3, h)
                group_ready(g)
                for m in range(2):
                    act.activation(hid_hi[:, 6 + m, :], ps[:, g.bank(m), :], ACT.Copy).then_inc(s["ret_v_hi"], 1)
                act.wait_ge(s["ret_s_lo"], h * 4 + 4)
                for d in range(4):
                    act.wait_ge(s["ret_pv"], h * 4 + d + 1)
                    act.activation(o_buf[:, d, :], ps[:, 4 + d, :], ACT.Copy).then_inc(s["ret_o"], 1)
                split(RET.chunk(5, h))
                g = RET.group(4, h)
                act.preload_act_table_set("silu_and_others")
                group_ready(g)
                for m in range(2):
                    copy_out(g, m, o_buf[:, 4 + m, :], ACT.Silu)
                for t in range(4):
                    act.wait_ge(s["ret_d"], h * 4 + t + 1)
                    if t == 3:
                        act.wait_ge(s["ret_acc"], h * 3 + 1)
                    act.activation(sq[:, t % 2, :] if t else ssq, o_buf[:, t, :], ACT.Square)\
                        .then_inc(s["ret_sq"], 1)
                split(RET.chunk(6, h))
                g = RET.group(5, h)
                group_ready(g)
                for m in range(2):
                    copy_out(g, m, o_buf[:, 6 + m, :], ACT.Silu)
                act.preload_act_table_set("natural_log_exp_and_others")
                act.wait_ge(s["ret_var"], h + 1)
                act.activation(r_bc, ps[:, 5, :], ACT.Ln, scale=1.0 / RDV, bias=eps[:, 0:1])\
                    .then_inc(s["ret_ln"], 1)
                act.wait_ge(s["ret_ln"], h + 1)
                act.activation(r_bc, r_bc, ACT.Exp, scale=-0.5).then_inc(s["ret_rstd"], 1)
                for t in range(4):
                    act.wait_ge(s["ret_y"], h * 8 + 2 * t + 2)
                    act.activation(hid_hi[:, 12 + t, :], o_buf[:, t, :], ACT.Copy).then_inc(s["ret_y_hi"], 1)
                split(RET.chunk(7, h))
                split(RET.chunk(8, h))

            def mlp(ph, norm, base, next_norm, last):
                rsqrt(norm, D)
                for t in range(KD):
                    hi_tile(norm, t, hn_hi[:, t, :])

                def up(i):
                    for m in range(4):
                        split(ph.chunk(m + 1, i))
                        g = ph.group(m, i)
                        group_ready(g)
                        for t in range(2):
                            copy_out(g, t, sq[:, t, :], ACT.Relu)
                        for t in range(2):
                            act.wait_ge(s["mlp_sq"], base + i * 8 + 2 * m + t + 1)
                            act.activation(hid_hi[:, 2 * m + t, :], tmp[:, t, :], ACT.Copy)\
                                .then_inc(s["mlp_hi"], 1)

                with act.Fori(0, MLP_GROUPS - 1) as i:
                    up(i)
                    for m in range(4):
                        split(ph.chunk(5 + m, i))
                i = MLP_GROUPS - 1
                up(i)
                for m in range(4):
                    if not (last and m == 3):
                        split(ph.chunk(5 + m, i))
                    g = ph.group(4 + m, i)
                    for t in range(2):
                        act.wait_ge(pair_free[g.pair], g.freed(t))
                        square(next_norm, 2 * m + t, x[:, 2 * m + t, :])

            x_squares(N_MLPA, RET.group(9, RH - 1))
            mlp(MLP_A, N_MLPA, 0, N_ATT, False)

            rsqrt(N_ATT, D)
            for t in range(KD):
                hi_tile(N_ATT, t, hn_hi[:, t, :])
            with act.Fori(0, H2 // 4) as i:
                for n in range(3):
                    split(ATT.chunk(n + 1, i))
                    g = ATT.group(n, i)
                    group_ready(g)
                    for m in range(2):
                        act.activation(hid_hi[:, 2 * n + m, :], ps[:, g.bank(m), :], ACT.Copy,
                                       scale=DH ** -0.5 if n == 0 else 1.0).then_inc(s["att_in_hi"], 1)
                attend(ATT2, out_hi, i)
                split(ATT.chunk(4, i))
            x_squares(N_MLPB, ATT.group(6, H2 // 4 - 1))
            mlp(MLP_B, N_MLPB, MLP_GROUPS * 8, N_FINAL, True)

            rsqrt(N_FINAL, D)
            for f in range(KD):
                act.wait_ge(s["fin_t"], f + 1)
                dst = o_buf[:, :, :].rearrange("p (t h) s -> p t (h s)", t=4)[:, :, f * P:(f + 1) * P]
                act.activation(dst, ps[:, 4 + f % 2, :].rearrange("p (t c) -> p t c", t=4), ACT.Copy)\
                    .then_inc(s["fin_copied"], 1)

        @block.vector
        def _(dve):
            def sums(norm, t):
                dve.wait_ge(s["norm_sq"], norm.sq0 + t + 1)
                if t >= 2:
                    dve.wait_ge(s["norm_acc"], norm.acc0 + t - 1)
                dve.tensor_tensor(ssq, ssq, sq[:, t % 2, :], ALU.add).then_inc(s["norm_acc"], 1)

            def all_sums(norm):
                for t in range(1, norm.n):
                    sums(norm, t)

            def low(norm, name, src, base, slot):
                hi_ap, lo_ap = base
                dve.wait_ge(s["norm_r"], norm.index + 1)
                for t in range(norm.n + 1):
                    if t < norm.n:
                        if norm.out0 + t >= 2:
                            dve.wait_ge(s["norm_lo"], norm.out0 + t - 1)
                        dve.scalar_tensor_tensor(tmp[:, t % 2, :], src(t), gain(*name(t)), r_bc, ALU.mult,
                                                 ALU.mult).then_inc(s["norm_tmp"], 1)
                    if t:
                        dve.wait_ge(s["norm_hi"], norm.out0 + t)
                        dve.tensor_tensor(lo_ap[:, slot + t - 1, :], tmp[:, (t - 1) % 2, :],
                                          hi_ap[:, slot + t - 1, :].bitcast(F32), ALU.subtract)\
                            .then_inc(s["norm_lo"], 1)

            def group_ready(g):
                dve.wait_ge(s["group_done"], g.done)

            def add_to(g, m, dst):
                dve.tensor_tensor(dst, ps[:, g.bank(m), :], dst, ALU.add).then_inc(pair_free[g.pair], 1)

            hn, hid = (hn_hi, hn_lo), (hid_hi, hid_lo)

            dve.wait_ge(s["consts_in"], 32)
            dve.wait_ge(s["pos_in"], 16)
            a, n = aux[:, 2, :], aux[:, 3, :]
            steps = [
                lambda: dve.tensor_copy(a, tab[:, 0, :].bitcast(I32)),
                lambda: dve.tensor_scalar(a, a, freq[:, 0:1], None, ALU.mult),
                lambda: dve.tensor_scalar(n, a, INV_TWO_PI, ROUND, ALU.mult, ALU.add),
                lambda: dve.tensor_scalar(n, n, ROUND, None, ALU.subtract),
                lambda: dve.scalar_tensor_tensor(a, n, -TWO_PI[0], a, ALU.mult, ALU.add),
                lambda: dve.scalar_tensor_tensor(a, n, -TWO_PI[1], a, ALU.mult, ALU.add),
                lambda: dve.scalar_tensor_tensor(a, n, -TWO_PI[2], a, ALU.mult, ALU.add),
                lambda: dve.scalar_tensor_tensor(a, n, -TWO_PI[3], a, ALU.mult, ALU.add),
                lambda: dve.tensor_scalar(a, a, SIN_MAX, -SIN_MAX, ALU.min, ALU.max),
            ]
            assert len(steps) == ANGLE_STEPS
            for k, step in enumerate(steps):
                if k:
                    dve.wait_ge(s["angle"], k)
                step().then_inc(s["angle"], 1)
            dve.wait_ge(s["sin_done"], 2)
            dve.tensor_scalar(tab[:, 1, :], tab[:, 1, :], freq[:, 1:2], None, ALU.mult).then_inc(s["table"], 1)
            dve.tensor_tensor(tab[:, 0, :], tab[:, 0, :], tab[:, 0, :], ALU.mult).then_inc(s["table"], 1)
            dve.wait_ge(s["table"], 2)
            dve.tensor_scalar(tab[:, 0, :], tab[:, 0, :], -2.0, 1.0, ALU.mult, ALU.add).then_inc(s["table"], 1)
            kr = [ap[:, 4:6, :].rearrange("p a (k c) -> p (a k) c", c=P) for ap in hid]
            kr_raw = aux[:, 0, :].rearrange("p (k c) -> p k c", k=KD)
            dve.wait_ge(s["kr_hi"], 1)
            for at in (0, 64):
                ins = dve.tensor_tensor(kr[1][:, :, at:at + 64], kr_raw, kr[0][:, :, at:at + 64].bitcast(F32),
                                        ALU.subtract)
            ins.then_inc(s["kr_lo"], 1)
            dve.wait_ge(s["ext_in"], 16)
            dve.memset(ext[:, 0:255], 0.0).then_inc(s["ext_built"], 1)
            dve.memset(ext[:, 255 + REL_TABLE:], 0.0).then_inc(s["ext_built"], 1)
            dve.wait_ge(s["ext_built"], 1)
            dve.tensor_scalar(ext[:, 0:255], ext[:, 0:255], ext[:, 255:256], None, ALU.add)\
                .then_inc(s["ext_built"], 1)

            all_sums(N_MIX)
            dve.wait_ge(s["gains_ready"], 1)
            low(N_MIX, lambda t: ("mix_pre_norm", t), lambda t: x[:, t, :], hn, 0)

            all_sums(N_Q)
            dve.wait_ge(s["table"], 3)
            dve.wait_ge(s["kr_done"], 1)
            dve.tensor_tensor(aux[64:96, 0, :], ps[0:32, 4, :], tab[0:32, 0, :], ALU.mult).then_inc(s["krope"], 1)
            dve.tensor_tensor(aux[64:96, 2, :], ps[32:64, 4, :], tab[32:64, 1, :], ALU.mult)\
                .then_inc(s["krope"], 1)
            dve.wait_ge(s["krope"], 2)
            dve.tensor_tensor(aux[64:96, 0, :], aux[64:96, 0, :], aux[64:96, 2, :], ALU.add)\
                .then_inc(s["krope"], 1)
            low(N_Q, lambda t: ("q_norm", t), lambda t: o_buf[:, t, :], hid, 0)
            all_sums(N_KV)
            low(N_KV, lambda t: ("kv_norm", t), lambda t: o_buf[:, 2 + t, :], hid, 2)
            dve.wait_ge(s["krope_hi"], 1)
            dve.tensor_tensor(hid_lo[64:96, 4, :], aux[64:96, 0, :], hid_hi[64:96, 4, :].bitcast(F32),
                              ALU.subtract).then_inc(s["krope_lo"], 1)
            for half in range(2):
                cg, xv, bg = (MIX.group(2 + 3 * half + n) for n in range(3))
                u = [o_buf[:, 4 + 2 * half + m, :] for m in range(2)]
                y = [aux[:, 2 + m, :] for m in range(2)]
                group_ready(xv)
                for m in range(2):
                    dve.wait_ge(pair_free[cg.pair], cg.freed(m))
                    dve.tensor_tensor(u[m], ps[:, xv.bank(m), :], u[m], ALU.mult)\
                        .then_inc(pair_free[xv.pair], 1)
                done = half * 8
                for tap in range(3):
                    for m in range(2):
                        w = gain("conv_w", 4 * tap + 2 * half + m)
                        if tap == 0:
                            dve.wait_ge(pair_free[xv.pair], xv.freed(m))
                            ins = dve.tensor_scalar(y[m], u[m], w, None, ALU.mult)
                        else:
                            dve.wait_ge(s["conv"], done + 2 * tap + m - 1)
                            ins = dve.scalar_tensor_tensor(y[m][:, tap:], u[m][:, 0:S - tap], w, y[m][:, tap:],
                                                           ALU.mult, ALU.add)
                        ins.then_inc(s["conv"], 1)
                group_ready(bg)
                for m in range(2):
                    dve.wait_ge(s["conv"], done + 5 + m)
                    dve.tensor_tensor(u[m], ps[:, bg.bank(m), :], y[m], ALU.mult)\
                        .then_inc(pair_free[bg.pair], 1)
                for m in range(2):
                    dve.wait_ge(pair_free[bg.pair], bg.freed(m))
                dve.sem_inc(s["conv"], 2)
                dve.sem_inc(s["conv_out"], 2)

            for n in range(2):
                g = UKV.group(n)
                for m in range(2):
                    for half in range(2):
                        h = 4 * n + 2 * m + half
                        dve.wait_ge(s["kv_hi"], h + 1)
                        ins = dve.tensor_tensor(hid_lo[0:NOPE, 4 + h, :], ps[64 * half:64 * half + 64, g.bank(m), :],
                                                hid_hi[0:NOPE, 4 + h, :].bitcast(F32), ALU.subtract)
                    ins.then_inc(pair_free[g.pair], 1)
            for n in range(2):
                g = UKV.group(2 + n)
                for m in range(2):
                    dve.wait_ge(s["kv_hi"], H1 + 2 * n + m + 1)
                    dve.tensor_tensor(hid_lo[:, 12 + 2 * n + m, :], ps[:, g.bank(m), :],
                                      hid_hi[:, 12 + 2 * n + m, :].bitcast(F32), ALU.subtract)\
                        .then_inc(pair_free[g.pair], 1)
            for h in range(H1):
                g = UQ.group(h // 2)
                at, j = h % 2, h % 4
                dve.wait_ge(s["sw_done"], h // 4 + 1)
                dve.tensor_tensor(sq[64:96, at, :], ps[32 * j:32 * j + 32, 4 + h // 4, :],
                                  tab[32 * j:32 * j + 32, 1, :], ALU.mult).then_inc(s["q_part"], 1)
                dve.wait_ge(s["q_nope"], h + 1)
                dve.tensor_tensor(tmp[64:96, at, :], ps[64:96, g.bank(at), :], tab[64:96, 0, :], ALU.mult)\
                    .then_inc(pair_free[g.pair], 1)
                dve.wait_ge(s["q_part"], h + 1)
                dve.wait_ge(pair_free[g.pair], g.freed(at))
                dve.tensor_tensor(tmp[64:96, at, :], tmp[64:96, at, :], sq[64:96, at, :], ALU.add)\
                    .then_inc(s["q_rope"], 1)
                dve.wait_ge(s["q_hi"], h + 1)
                dve.tensor_tensor(hn_lo[0:DQ, h, :], tmp[0:DQ, at, :], hn_hi[0:DQ, h, :].bitcast(F32),
                                  ALU.subtract).then_inc(s["q_lo"], 1)

            def masked_scores(a, h, i=0):
                if a.block2:
                    dve.wait_ge(s["mask_set"], 4)
                    dve.wait_ge(s[f"bias_in{h}"], i * 32 + 32)
                for t, done in Q_ORDER:
                    dve.wait_ge(s["att_s"], a.n(h, i) * 4 + done)
                    if a.block2:
                        dve.nop(nofuse=True)
                    col = 4 * (h % 2) + t
                    dve.tensor_tensor_reduce(score_sb(h, t), score_ps(t),
                                             aux[:, h if a.block2 else 1, 512 - 128 * (t + 1):],
                                             1.0 if a.block2 else DQ ** -0.5, FMIN, ALU.add, ALU.max,
                                             mx[:, col:col + 1]).then_inc(s["att_mx"], 1)
                dve.wait_ge(s["att_mx"], a.n(h, i) * 4 + 4)
                four = slice(4 * (h % 2), 4 * (h % 2) + 4)
                dve.tensor_scalar(nmx[:, four], mx[:, four], -1.0, None, ALU.mult).then_inc(s["att_nmx"], 1)

            def probabilities(a, h, i=0):
                four = slice(4 * (h % 2), 4 * (h % 2) + 4)
                dve.wait_ge(s["att_exp"], a.n(h, i) * 4 + 4)
                dve.reciprocal(rs[:, four], sm[:, four]).then_inc(s["att_rs"], 1)
                dve.wait_ge(s["att_rs"], a.n(h, i) + 1)
                for t in range(4):
                    col = 4 * (h % 2) + t
                    dve.tensor_scalar(score_sb(h, t), score_sb(h, t), rs[:, col:col + 1], None, ALU.mult)\
                        .then_inc(s["att_p"], 1)

            def prob_lo(a, h, i=0):
                for j, done in K_ORDER:
                    dve.wait_ge(s["att_hi"], a.n(h, i) * 4 + done)
                    dve.tensor_tensor(a.pt(hid_lo, h, j), trans_ps(j), a.pt(hid_hi, h, j).bitcast(F32),
                                      ALU.subtract).then_inc(s["att_lo"], 1)

            def out_lo(h, i):
                rows = slice(64 * (h % 2), 64 * (h % 2) + 64)
                dve.wait_ge(s["att_ohi"], h + 1 + i * 4)
                dve.tensor_tensor(hid_lo[rows, 6 + h // 2, :], ATT2.out_ps(h),
                                  hid_hi[rows, 6 + h // 2, :].bitcast(F32), ALU.subtract).then_inc(s["att_o"], 1)

            def attend(a, i=0):
                masked_scores(a, 0, i)
                probabilities(a, 0, i)
                for h in range(a.heads):
                    if h + 1 < a.heads:
                        masked_scores(a, h + 1, i)
                    prob_lo(a, h, i)
                    if h + 1 < a.heads:
                        probabilities(a, h + 1, i)
                    if a.block2:
                        out_lo(h, i)

            dve.wait_ge(s["mask_in"], 16)
            attend(ATT1)

            all_sums(N_CONVG)
            low(N_CONVG, lambda t: ("conv_group_norm", t), lambda t: o_buf[:, 4 + t, :], hn, 4)
            all_sums(N_ATTG)
            low(N_ATTG, lambda t: ("attn_group_norm", t), lambda t: o_buf[:, t, :], hn, 0)
            all_sums(N_POST)

            def post(norm, name, sem, next_norm=None):
                dve.wait_ge(s["norm_r"], norm.index + 1)
                for t in range(KD):
                    if t >= 2:
                        dve.wait_ge(sem, 2 * t - 2)
                    dve.scalar_tensor_tensor(tmp[:, t % 2, :], o_buf[:, t, :], gain(name, t), r_bc, ALU.mult,
                                             ALU.mult).then_inc(sem, 1)
                    dve.wait_ge(sem, 2 * t + 1)
                    dve.tensor_tensor(x[:, t, :], x[:, t, :], tmp[:, t % 2, :], ALU.add).then_inc(sem, 1)
                    if next_norm and t >= 2:
                        sums(next_norm, t - 1)
                if next_norm:
                    sums(next_norm, KD - 1)

            post(N_POST, "mix_post_norm", s["post_x"], N_FFN)
            low(N_FFN, lambda t: ("ffn_pre_norm", t), lambda t: x[:, t, :], hn, 0)
            dve.memset(o_buf[:, :, :], 0.0).then_inc(s["o_zero"], 1)
            for f in range(2):
                dve.wait_ge(s["p_hi"], f + 1)
                dve.tensor_tensor(hid_lo[:, 8 + f, :], ps[:, 4 + f, :], hid_hi[:, 8 + f, :].bitcast(F32),
                                  ALU.subtract).then_inc(s["p_lo"], 1)
            dve.wait_ge(s["o_zero"], 1)

            def ffn(ph, i, g_hid, kt, next_norm=None):
                for j in range(kt // 2):
                    gate, up = ph.group(2 * j, i), ph.group(2 * j + 1, i)
                    group_ready(up)
                    for m in range(2):
                        dve.wait_ge(pair_free[gate.pair], gate.freed(m))
                        dve.tensor_tensor(sq[:, m, :], ps[:, up.bank(m), :], sq[:, m, :], ALU.mult)\
                            .then_inc(pair_free[up.pair], 1)
                    for m in range(2):
                        dve.wait_ge(s["ffn_hi"], g_hid + 2 * j + m + 1)
                        dve.tensor_tensor(hid_lo[:, 2 * j + m, :], sq[:, m, :],
                                          hid_hi[:, 2 * j + m, :].bitcast(F32), ALU.subtract)\
                            .then_inc(s["ffn_lo"], 1)
                for m in range(4):
                    g = ph.group(kt + m, i)
                    group_ready(g)
                    for t in range(2):
                        add_to(g, t, o_buf[:, 2 * m + t, :])
                        if next_norm and 2 * m + t >= 2:
                            sums(next_norm, 2 * m + t - 1)

            with dve.Fori(0, 2) as i:
                ffn(FFN, i, i * 8, 8)
            ffn(FFN_LAST, 0, 16, 6, N_FPOST)
            sums(N_FPOST, KD - 1)

            dve.wait_ge(s["norm_r"], N_FPOST.index + 1)
            for t in range(KD):
                dve.scalar_tensor_tensor(tmp[:, t % 2, :], o_buf[:, t, :], gain("ffn_post_norm", t), r_bc,
                                         ALU.mult, ALU.mult).then_inc(s["ple_x"], 1)
                dve.wait_ge(s["ple_x"], 2 * t + 1)
                dve.tensor_tensor(x[:, t, :], x[:, t, :], tmp[:, t % 2, :], ALU.add).then_inc(s["ple_x"], 1)
                dve.wait_ge(s["ple_x"], 2 * t + 2)
                dve.wait_ge(s["ple_xhi"], t + 1)
                dve.tensor_tensor(hn_lo[:, t, :], x[:, t, :], hn_hi[:, t, :].bitcast(F32), ALU.subtract)\
                    .then_inc(s["ple_xlo"], 1)
                if t % 2 and t > 1:
                    sums_upto = t - 2
                    for k in ((1,) if sums_upto == 1 else (sums_upto - 1, sums_upto)):
                        sums(N_PLE, k)
            for k in (6, 7):
                sums(N_PLE, k)
            dve.wait_ge(s["norm_r"], N_PLE.index + 1)
            for m in range(4):
                g = GATE.group(m)
                for t in range(2):
                    k = 2 * m + t
                    if k >= 2:
                        dve.wait_ge(s["ple_e"], 3 * k - 3)
                    dve.scalar_tensor_tensor(tmp[:, t, :], o_buf[:, k, :], gain("ple_norm", k), r_bc, ALU.mult,
                                             ALU.mult).then_inc(s["ple_e"], 1)
                    dve.wait_ge(s["ple_e"], 3 * k + 1)
                    dve.wait_ge(pair_free[g.pair], g.freed(t))
                    dve.tensor_tensor(tmp[:, t, :], tmp[:, t, :], aux[:, 2 + t, :], ALU.mult)\
                        .then_inc(s["ple_e"], 1)
                    dve.wait_ge(s["ple_e"], 3 * k + 2)
                    dve.tensor_tensor(x[:, k, :], x[:, k, :], tmp[:, t, :], ALU.add).then_inc(s["ple_e"], 1)
                    if k >= 2:
                        sums(N_RET, k - 1)
            sums(N_RET, KD - 1)

            low(N_RET, lambda t: ("mix_norm_g_2", t), lambda t: x[:, t, :], hn, 0)
            dve.wait_ge(s["ret_tab_in"], 16)
            dve.wait_ge(s["decay_in"], 16)
            cos, sin = tab[:, 0, :], tab[:, 1, :]
            with dve.Fori(0, RH) as h:
                last = RET.group(1, h)
                dve.wait_ge(pair_free[last.pair], last.empty)
                for n in range(2):
                    if n:
                        dve.wait_ge(s["ret_qk_lo"], h * 4 + 2)
                    g = RET.group(n, h)
                    t1, t2 = ps[:, g.bank(0), :], ps[:, g.bank(1), :]
                    group_ready(g)
                    dve.tensor_tensor(tmp[:, 0, :], t1, cos, ALU.mult).then_inc(s["ret_part"], 1)
                    dve.tensor_tensor(sq[:, 0, :], t2, sin, ALU.mult).then_inc(s["ret_part"], 1)
                    dve.tensor_tensor(sq[:, 1, :], t1, sin, ALU.mult).then_inc(pair_free[g.pair], 1)
                    dve.tensor_tensor(tmp[:, 1, :], t2, cos, ALU.mult).then_inc(pair_free[g.pair], 1)
                    dve.wait_ge(s["ret_part"], h * 4 + 2 * n + 2)
                    dve.tensor_tensor(tmp[:, 0, :], tmp[:, 0, :], sq[:, 0, :], ALU.subtract)\
                        .then_inc(s["ret_tmp"], 1)
                    dve.wait_ge(pair_free[g.pair], g.freed(1))
                    dve.tensor_tensor(tmp[:, 1, :], tmp[:, 1, :], sq[:, 1, :], ALU.add).then_inc(s["ret_tmp"], 1)
                    for t in range(2):
                        dve.wait_ge(s["ret_qk_hi"], h * 4 + 2 * n + t + 1)
                        dve.tensor_tensor(hid_lo[:, 2 * n + t, :], tmp[:, t, :],
                                          hid_hi[:, 2 * n + t, :].bitcast(F32), ALU.subtract)\
                            .then_inc(s["ret_qk_lo"], 1)

                def v_lo(n):
                    g = RET.group(2 + n, h)
                    for m in range(2):
                        dve.wait_ge(s["ret_v_hi"], h * 4 + 2 * n + m + 1)
                        dve.tensor_tensor(hid_lo[:, 4 + 2 * n + m, :], ps[:, g.bank(m), :],
                                          hid_hi[:, 4 + 2 * n + m, :].bitcast(F32), ALU.subtract)\
                            .then_inc(pair_free[g.pair], 1)

                v_lo(0)
                for j, done in K_ORDER:
                    dve.wait_ge(s["ret_s"], h * 4 + done)
                    dve.tensor_tensor(o_buf[:, j, j * P:], ret_score(j), aux[:, h, 0:S - j * P], ALU.mult)\
                        .then_inc(s["ret_sd"], 1)
                for n, (j, _) in enumerate(K_ORDER):
                    dve.wait_ge(s["ret_s_hi"], h * 4 + n + 1)
                    dve.tensor_tensor(hid_lo[:, 8 + j, j * P:], o_buf[:, j, j * P:],
                                      hid_hi[:, 8 + j, j * P:].bitcast(F32), ALU.subtract)\
                        .then_inc(s["ret_s_lo"], 1)
                v_lo(1)
                for d in range(1, 4):
                    dve.wait_ge(s["ret_o"], h * 4 + d + 1)
                    if d > 1:
                        dve.wait_ge(s["ret_sum"], h * 3 + d - 1)
                    dve.tensor_tensor(ssq, o_buf[:, 0, :] if d == 1 else ssq, o_buf[:, d, :], ALU.add)\
                        .then_inc(s["ret_sum"], 1)
                dve.wait_ge(s["ret_mean"], h + 1)
                for t in range(4):
                    dve.scalar_tensor_tensor(o_buf[:, t, :], ps[:, 4, :], -1.0 / RDV, o_buf[:, t, :], ALU.mult,
                                             ALU.add).then_inc(s["ret_d"], 1)
                for t in range(1, 4):
                    dve.wait_ge(s["ret_sq"], h * 4 + t + 1)
                    if t > 1:
                        dve.wait_ge(s["ret_acc"], h * 3 + t - 1)
                    dve.tensor_tensor(ssq, ssq, sq[:, t % 2, :], ALU.add).then_inc(s["ret_acc"], 1)
                dve.wait_ge(s["ret_rstd"], h + 1)
                at = GAIN_AT["ret_gn_g_2"]
                head_gains = gains[:, at:at + 16].rearrange("p (h t) -> p h t", t=4)
                for t in range(5):
                    if t < 4:
                        dve.scalar_tensor_tensor(o_buf[:, t, :], o_buf[:, t, :], head_gains[:, h, t:t + 1], r_bc,
                                                 ALU.mult, ALU.mult).then_inc(s["ret_y"], 1)
                        g = RET.group(4 + t // 2, h)
                        dve.wait_ge(pair_free[g.pair], g.freed(t % 2))
                        dve.wait_ge(s["ret_y"], h * 8 + 2 * t + 1)
                        dve.tensor_tensor(o_buf[:, t, :], o_buf[:, t, :], o_buf[:, 4 + t, :], ALU.mult)\
                            .then_inc(s["ret_y"], 1)
                    if t:
                        dve.wait_ge(s["ret_y_hi"], h * 4 + t)
                        dve.tensor_tensor(hid_lo[:, 11 + t, :], o_buf[:, t - 1, :],
                                          hid_hi[:, 11 + t, :].bitcast(F32), ALU.subtract)\
                            .then_inc(s["ret_y_lo"], 1)
                for n in range(4):
                    g = RET.group(6 + n, h)
                    group_ready(g)
                    for m in range(2):
                        add_to(g, m, x[:, 2 * n + m, :])

            def mlp(ph, norm, row, base, next_norm):
                low(norm, lambda t: ("mlp_norm_g_2", row + t), lambda t: x[:, t, :], hn, 0)

                def body(i):
                    for m in range(4):
                        g = ph.group(m, i)
                        if m:
                            dve.wait_ge(s["mlp_lo"], base + i * 8 + 2 * m)
                        for t in range(2):
                            dve.wait_ge(pair_free[g.pair], g.freed(t))
                            dve.tensor_tensor(tmp[:, t, :], sq[:, t, :], sq[:, t, :], ALU.mult)\
                                .then_inc(s["mlp_sq"], 1)
                        for t in range(2):
                            dve.wait_ge(s["mlp_hi"], base + i * 8 + 2 * m + t + 1)
                            dve.tensor_tensor(hid_lo[:, 2 * m + t, :], tmp[:, t, :],
                                              hid_hi[:, 2 * m + t, :].bitcast(F32), ALU.subtract)\
                                .then_inc(s["mlp_lo"], 1)
                    for m in range(4):
                        g = ph.group(4 + m, i)
                        group_ready(g)
                        for t in range(2):
                            add_to(g, t, x[:, 2 * m + t, :])
                            if isinstance(i, int) and 2 * m + t >= 2:
                                sums(next_norm, 2 * m + t - 1)

                with dve.Fori(0, MLP_GROUPS - 1) as i:
                    body(i)
                body(MLP_GROUPS - 1)
                sums(next_norm, KD - 1)

            all_sums(N_MLPA)
            for h in range(4):
                dve.memset(aux[0:64, h, 448:512], MASKED).then_inc(s["mask_set"], 1)
            mlp(MLP_A, N_MLPA, 0, 0, N_ATT)
            low(N_ATT, lambda t: ("mix_norm_g_2", 8 + t), lambda t: x[:, t, :], hn, 0)
            with dve.Fori(0, H2 // 4) as i:
                for n in range(3):
                    g = ATT.group(n, i)
                    for m in range(2):
                        dve.wait_ge(s["att_in_hi"], i * 6 + 2 * n + m + 1)
                        dve.scalar_tensor_tensor(hid_lo[:, 2 * n + m, :], ps[:, g.bank(m), :],
                                                 DH ** -0.5 if n == 0 else 1.0,
                                                 hid_hi[:, 2 * n + m, :].bitcast(F32), ALU.mult, ALU.subtract)\
                            .then_inc(pair_free[g.pair], 1)
                attend(ATT2, i)
                for n in range(4):
                    g = ATT.group(3 + n, i)
                    group_ready(g)
                    for m in range(2):
                        add_to(g, m, x[:, 2 * n + m, :])
            all_sums(N_MLPB)
            mlp(MLP_B, N_MLPB, 8, MLP_GROUPS * 8, N_FINAL)

            dve.wait_ge(s["norm_r"], N_FINAL.index + 1)
            for f in range(KD):
                if f >= 2:
                    dve.wait_ge(s["fin_t"], f - 1)
                dve.scalar_tensor_tensor(tmp[:, f % 2, :], x[:, f, :], gain("final_norm_g_2", f), r_bc, ALU.mult,
                                         ALU.mult).then_inc(s["fin_tmp"], 1)


_INS = ["x", "p", "positions", "mix_pre_norm", "w_in", "q_norm", "kv_norm", "w_uq", "w_ukv", "conv_w",
        "attn_group_norm", "conv_group_norm", "w_out", "mix_post_norm", "ffn_pre_norm", "w_gate", "w_up",
        "w_down", "ffn_post_norm", "w_ple_proj", "ple_norm", "w_ple_gate", "mix_norm_g_2", "ret_w_in_2",
        "ret_gn_g_2", "ret_w_out_2", "att_w_in_2", "att_rel_bias_2", "att_w_out_2", "mlp_norm_g_2",
        "mlp_w1_2", "mlp_w2_2", "final_norm_g_2"]


def constants():
    import numpy as np
    f = np.float32
    half = ROPE // 2
    inv_freq = f(1) / (f(10000) ** (np.arange(half, dtype=f) / f(half)))
    part = np.arange(P)
    freq = np.stack([inv_freq[part % half], np.where(part % ROPE < half, -1, 1)], 1).astype(f)
    causal = np.zeros((P, S), f)
    causal[:, S - P:] = np.where(np.arange(P)[None, :] <= part[:, None], 0, MASKED)
    inv = np.exp(-np.log(f(10000)) * np.arange(RDK // 2, dtype=f) / f(RDK // 2)).astype(f)
    ang = inv[:, None] * np.arange(S, dtype=f)[None, :]
    ret_rope = np.stack([np.cos(ang), np.sin(ang)], 1).astype(f)
    log_gamma = np.log1p(-np.exp2(-5.0 - np.arange(RH)))
    key, query = part[:, None, None], np.arange(S)[None, None, :]
    decay = np.exp(log_gamma[None, :, None] * np.abs(query - key)) * RDK ** -0.5
    decay = np.where(key // 64 <= query // 64, decay, 0).astype(f)
    return {"c_ident": np.eye(P, dtype=f), "c_freq": freq, "c_causal": causal, "c_ret_rope": ret_rope,
            "c_decay": decay}


def kernel(**inputs):
    import numpy as _np
    import concourse.bacc as _bacc
    from concourse import mybir as _mybir
    from concourse.bass_utils import run_bass_kernel_spmd as _run

    nc = _bacc.Bacc("TRN2", target_bir_lowering=False, num_devices=1)
    arrays, tensors = {}, {}
    given = {name: inputs[name] for name in _INS}
    given.update(constants())
    for name, value in given.items():
        a = _np.ascontiguousarray(value)
        arrays[f"in_{name}"] = a
        tensors[name] = nc.dram_tensor(f"in_{name}", a.shape, _mybir.dt.from_np(a.dtype),
                                       kind="ExternalInput").ap()
    out = nc.dram_tensor("out_0", (1, S, D), F32, kind="ExternalOutput").ap()
    build(nc, tensors, out)
    r = _run(nc, [arrays], core_ids=[0])
    return r.results[0]["out_0"]
```

```python
from contextlib import ExitStack

import concourse.bass as bass
from concourse import mybir

F32 = mybir.dt.float32
F32R = mybir.dt.float32r
I32 = mybir.dt.int32
ALU = mybir.AluOpType
ACT = mybir.ActivationFunctionType
P = 128
S = 512
D = 1024
KD = D // P
CH = 2048
EPS = 1e-6
MASKED = -3.0e38
FMIN = -3.4028235e38
INV_TWO_PI = 0.15915494309189535
ROUND = 12582912.0
TWO_PI = (6.25, 0.03125, 0.00193500518798828125, 3.0199159819e-07)
SIN_MAX = 3.1415925
ANGLE_STEPS = 9

Q_RANK = KV_RANK = 256
ROPE = 32
CONV = 512
H1 = 8
NOPE = 64
DQ = NOPE + ROPE
CONV0 = Q_RANK + KV_RANK + ROPE
D_FF = 2816
FF_TILES = D_FF // P
PLE = 256
RH = 4
RDK = 256
RDV = 512
RQK = RH * RDK
RVW = RH * RDV
H2 = 16
DH = 64
MAX_REL = 256
REL_TABLE = 320
EXT = 640
MLP_GROUPS = 4

GAIN_ROWS = [("mix_pre_norm", 8), ("q_norm", 2), ("kv_norm", 2), ("conv_w", 12), ("attn_group_norm", 4),
             ("conv_group_norm", 4), ("mix_post_norm", 8), ("ffn_pre_norm", 8), ("ffn_post_norm", 8),
             ("ple_norm", 8), ("mix_norm_g_2", 16), ("ret_gn_g_2", 16), ("mlp_norm_g_2", 16),
             ("final_norm_g_2", 8)]
GAIN_AT = {}
_row = 0
for _name, _n in GAIN_ROWS:
    GAIN_AT[_name] = _row
    _row += _n
N_GAINS = _row


class Phase:

    def __init__(self, prev, groups, iters=1):
        self.chunks, self.groups, self.iters = len(groups), sum(groups), iters
        self.upto = [sum(groups[:j]) for j in range(len(groups) + 1)]
        self.pair = ((self.groups + 1) // 2, self.groups // 2)
        self.prev = prev
        if prev is None:
            self.chunk0, self.group0, self.pair0 = 0, 0, (0, 0)
        else:
            self.chunk0 = prev.chunk0 + prev.chunks * prev.iters
            self.group0 = prev.group0 + prev.groups * prev.iters
            self.pair0 = tuple(prev.pair0[p] + prev.pair[p] * prev.iters for p in (0, 1))
        assert iters == 1 or self.chunks % 2 == 0

    def chunk(self, j, i=0):
        return Chunk(self, j, i)

    def group(self, pos, i=0):
        return Group(self, pos, i)


class Chunk:

    def __init__(self, ph, j, i):
        self.slot = (ph.chunk0 + j) % 2
        self.number = ph.chunk0 + j + i * ph.chunks
        self.loads = ((ph.chunk0 + j) // 2 + 1) * 16 + i * (ph.chunks // 2 * 16)
        self.early = isinstance(self.number, int) and self.number < 2
        if j >= 2:
            self.two_before = ph.group0 + i * ph.groups + ph.upto[j - 1]
        elif j == 1 and not self.early:
            self.two_before = ph.group0 + i * ph.groups
        elif not self.early:
            p = ph.prev
            self.two_before = ph.group0 - (p.upto[-1] - p.upto[-2])


class Group:

    def __init__(self, ph, pos, i):
        self.pair = pos % 2
        self.done = ph.group0 + pos + 1 + i * ph.groups
        self.empty = (ph.pair0[self.pair] + pos // 2) * 2 + i * (2 * ph.pair[self.pair])
        self.virgin = isinstance(self.empty, int) and self.empty == 0

    def bank(self, m):
        return 2 * self.pair + m

    def freed(self, m):
        return self.empty + m + 1


MIX = Phase(None, [1] * 8)
UKV = Phase(MIX, [4])
UQ = Phase(UKV, [4])
WOUT = Phase(UQ, [1] * 4)
FFN = Phase(WOUT, [1] * 12, 2)
FFN_LAST = Phase(FFN, [1] * 10)
PROJ = Phase(FFN_LAST, [4])
GATE = Phase(PROJ, [1] * 4)
RET = Phase(GATE, [1, 1, 1, 1, 1, 1, 2, 2], RH)
MLP_A = Phase(RET, [1] * 8, MLP_GROUPS)
ATT = Phase(MLP_A, [1, 1, 1, 4], H2 // 4)
MLP_B = Phase(ATT, [1] * 8, MLP_GROUPS)
N_CHUNKS = MLP_B.chunk0 + MLP_B.chunks * MLP_B.iters


class Norm:

    def __init__(self, prev, n, split):
        self.n, self.split = n, split
        self.index = prev.index + 1 if prev else 0
        self.sq0 = prev.sq0 + prev.n if prev else 0
        self.acc0 = prev.acc0 + prev.n - 1 if prev else 0
        self.out0 = prev.out0 + prev.split if prev else 0


N_MIX = Norm(None, 8, 8)
N_Q = Norm(N_MIX, 2, 2)
N_KV = Norm(N_Q, 2, 2)
N_CONVG = Norm(N_KV, 4, 4)
N_ATTG = Norm(N_CONVG, 4, 4)
N_POST = Norm(N_ATTG, 8, 0)
N_FFN = Norm(N_POST, 8, 8)
N_FPOST = Norm(N_FFN, 8, 0)
N_PLE = Norm(N_FPOST, 8, 0)
N_RET = Norm(N_PLE, 8, 8)
N_MLPA = Norm(N_RET, 8, 8)
N_ATT = Norm(N_MLPA, 8, 8)
N_MLPB = Norm(N_ATT, 8, 8)
N_FINAL = Norm(N_MLPB, 8, 0)

SEMAPHORES = """x_in p_in rows_in pos_in consts_in kr_in mask_in ext_in ext_out bias_in0 bias_in1 bias_in2
 bias_in3 decay_in ret_tab_in krep_done out_done raw_ready0 raw_ready1 w_hi_ready w_lo_ready group_done
 pair_free0 pair_free1 memset_done gains_t gains_ready x_t x_copied p_t p_hi p_lo
 norm_sq norm_acc norm_stat norm_ln norm_r col_stat col_ln col_r norm_tmp norm_hi norm_lo
 angle sin_done table kr_hi kr_lo kr_done krope krope_hi krope_lo
 conv conv_out kv_hi sw_done q_nope q_part q_rope q_hi q_lo
 att_s att_mx att_nmx att_exp att_rs att_p att_t att_hi att_lo att_pv att_ohi att_o ext_built mask_set
 post_x o_zero ffn_hi ffn_lo ple_x ple_xhi ple_xlo ple_e
 ret_part ret_tmp ret_qk_hi ret_qk_lo ret_v_hi ret_s ret_sd ret_s_hi ret_s_lo ret_pv ret_o ret_sum
 ret_mean ret_d ret_sq ret_acc ret_var ret_ln ret_rstd ret_ys ret_gate ret_y ret_y_hi ret_y_lo
 mlp_sq mlp_hi mlp_lo att_in_hi att_in_lo tab_scaled ffn_silu ffn_part fin_tmp fin_t fin_copied""".split()


def build(nc, T, out):
    ext_rows = nc.dram_tensor("ext_rows", (H2, P, EXT), F32, kind="Internal").ap()

    with ExitStack() as ctx:
        def sb(name, shape, dt=F32):
            return ctx.enter_context(nc.sbuf_tensor(name, shape, dt))

        s = {name: ctx.enter_context(nc.semaphore(name)) for name in SEMAPHORES}
        raw_ready = [s["raw_ready0"], s["raw_ready1"]]
        pair_free = [s["pair_free0"], s["pair_free1"]]

        x = sb("x", [P, KD, S])
        o_buf = sb("o_buf", [P, 8, S])
        hn_hi = sb("hn_hi", [P, KD, S], F32R)
        hn_lo = sb("hn_lo", [P, KD, S], F32R)
        hid_hi = sb("hid_hi", [P, 16, S], F32R)
        hid_lo = sb("hid_lo", [P, 16, S], F32R)
        raw = sb("raw", [P, 2, CH])
        w_hi = sb("w_hi", [P, 2, CH], F32R)
        w_lo = sb("w_lo", [P, 2, CH], F32R)
        scr = sb("scr", [P, 6, S])
        tab = sb("tab", [P, 2, S])
        aux = sb("aux", [P, 4, S])
        ident = sb("ident", [P, P])
        ones = sb("ones", [P, P])
        gains = sb("gains", [P, N_GAINS])
        ext = sb("ext", [H2, EXT])
        freq = sb("freq", [P, 2])
        eps = sb("eps", [P, 1])
        small = sb("small", [P, 5, 8])
        rstd = sb("rstd", [P, S])
        ps = ctx.enter_context(nc.psum_tensor("ps", [P, 8, S], F32))

        ssq, sq, tmp, r_bc = scr[:, 0, :], scr[:, 1:3, :], scr[:, 3:5, :], scr[:, 5, :]
        sflat = scr[:, :, :].rearrange("p a b -> p (a b)")
        mx, nmx, sm, rs, r_col = (small[:, n, :] for n in range(5))

        def gain(name, t):
            at = GAIN_AT[name] + t
            return gains[:, at:at + 1]

        block = ctx.enter_context(nc.Block())

        def ukv_parts():
            slot = UKV.chunk0 % 2
            src = raw[:, slot, :].rearrange("p (k h t c) -> p k t h c", k=2, h=H1, t=2)
            hi_, lo_ = (ap[:, slot, :].rearrange("p (k t h c) -> p k t h c", k=2, t=2, h=H1) for ap in (w_hi, w_lo))
            for k in range(2):
                for t in range(2):
                    yield lo_[:, k, t], hi_[:, k, t], src[:, k, t]

        def uq_parts():
            slot = UQ.chunk0 % 2
            for k in range(2):
                yield (w_lo[:, slot, k * 1024:k * 1024 + 768], w_hi[:, slot, k * 1024:k * 1024 + 768],
                       raw[:, slot, k * 768:k * 768 + 768])
                src = raw[:, slot, k * 768:k * 768 + 768].rearrange("p (h c) -> p h c", h=H1)
                lo_, hi_ = (ap[:, slot, k * 1024 + 768:k * 1024 + 1024].rearrange("p (h c) -> p h c", h=H1)
                            for ap in (w_lo, w_hi))
                for half in (0, 16):
                    yield (lo_[:, :, half:half + 16], hi_[:, :, half:half + 16],
                           src[:, :, NOPE + 16 - half:NOPE + 32 - half])

        S_OFF = [0, 128, 384, 768]
        Q_ORDER = ((3, 1), (2, 3), (0, 3), (1, 4))
        K_ORDER = ((0, 1), (1, 3), (3, 3), (2, 4))

        def score_sb(h, i):
            at = (h % 2) * 1280 + S_OFF[i]
            return sflat[:, at:at + 128 * (i + 1)]

        def score_ps(i):
            b, at = {3: (0, 0), 2: (1, 0), 0: (1, 384), 1: (2, 0)}[i]
            return ps[:, b, at:at + 128 * (i + 1)]

        def trans_ps(j):
            b, at = {0: (3, 0), 1: (4, 0), 3: (4, 384), 2: (5, 0)}[j]
            return ps[:, b, at:at + 512 - 128 * j]

        Q1_HI = [hn_hi[0:DQ, h, :] for h in range(H1)]
        Q1_LO = [hn_lo[0:DQ, h, :] for h in range(H1)]
        K1_HI = [hid_hi[0:DQ, 4 + h, :] for h in range(H1)]
        K1_LO = [hid_lo[0:DQ, 4 + h, :] for h in range(H1)]

        def q2(ap, h):
            return ap[64 * (h % 2):64 * (h % 2) + 64, h // 2, :]

        def k2(ap, h):
            return ap[64 * (h % 2):64 * (h % 2) + 64, 2 + h // 2, :]

        class Attention:

            def __init__(self, base, heads, block2):
                self.base, self.heads, self.block2 = base, heads, block2

            def n(self, h, i=0):
                return self.base + h + i * self.heads

            def first(self, h, i=0):
                return self.base + h == 0

            def qk(self, h):
                if self.block2:
                    return [(q2(hid_hi, h), k2(hid_hi, h)), (q2(hid_hi, h), k2(hid_lo, h)),
                            (q2(hid_lo, h), k2(hid_hi, h))]
                return [(Q1_HI[h], K1_HI[h]), (Q1_HI[h], K1_LO[h]), (Q1_LO[h], K1_HI[h])]

            def v(self, ap, h, j):
                if self.block2:
                    at = (j % 2) * 256 + (h // 2) * P
                    return ap[:, 4 + j // 2, at:at + P]
                return ap[:, 12 + j, (h // 2) * P:(h // 2) * P + P]

            def pt(self, ap, h, j):
                slot = (8 + 4 * (h % 2) if self.block2 else 0) + j
                return ap[:, slot, 0:512 - 128 * j]

            def out_ps(self, h):
                return ps[64 * (h % 2):64 * (h % 2) + 64, 6 + h % 2, :]

        ATT1 = Attention(0, H1, False)
        ATT2 = Attention(H1, 4, True)

        def ret_score(j):
            b, at = {0: (4, 0), 1: (5, 0), 3: (5, 384), 2: (6, 0)}[j]
            return ps[:, b, at:at + 512 - 128 * j]

        def ret_v(ap, j, d):
            at = (j % 2) * 256 + (d % 2) * P
            return ap[:, 4 + 2 * (d // 2) + j // 2, at:at + P]

        @block.sync
        def _(sp):
            def load(c, src, k):
                if not c.early:
                    sp.wait_ge(s["w_lo_ready"], c.number - 1)
                cols = src.shape[-1]
                dst = raw[:, c.slot, 0:k * cols].rearrange("p (k c) -> p k c", k=k)
                sp.dma_start(dst, src).then_inc(raw_ready[c.slot], 16)

            w_in = T["w_in"][0].rearrange("(k p) c -> p k c", p=P)
            xt = o_buf[:, :, :].rearrange("p (t h) s -> p t (h s)", t=4)
            for t in range(4):
                sp.dma_start(xt[:, t, :], T["x"][0, t * P:(t + 1) * P, :]).then_inc(s["x_in"], 16)
            load(MIX.chunk(0), w_in[:, :, 0:256], KD)
            load(MIX.chunk(1), w_in[:, :, 256:512], KD)
            sp.wait_ge(s["gains_t"], 1)
            sp.dma_start(aux[:, 1, :], T["c_causal"]).then_inc(s["mask_in"], 16)
            for half in range(2):
                for n, part in enumerate((1, 2, 0)):
                    at = CONV0 + part * CONV + half * 256
                    load(MIX.chunk(2 + 3 * half + n), w_in[:, :, at:at + 256], KD)
            load(UKV.chunk(0), T["w_ukv"][0].rearrange("(k p) c -> p k c", p=P), 2)
            load(UQ.chunk(0), T["w_uq"][0].rearrange("(k p) c -> p k c", p=P), 2)
            w_out = T["w_out"][0].rearrange("(k p) (m c) -> m p k c", p=P, c=256)
            for m in range(4):
                load(WOUT.chunk(m), w_out[m], KD)

            w_gate = T["w_gate"][0].rearrange("(k p) (m c) -> m p k c", p=P, c=256)
            w_up = T["w_up"][0].rearrange("(k p) (m c) -> m p k c", p=P, c=256)

            def load_ffn(ph, i, g, pairs):
                for j in range(pairs):
                    load(ph.chunk(2 * j, i), w_gate[g * 4 + j], KD)
                    load(ph.chunk(2 * j + 1, i), w_up[g * 4 + j], KD)

            down = T["w_down"][0, 0:2048, :].rearrange("(g k p) (m c) -> g m p k c", p=P, k=8, c=256)
            sp.wait_ge(s["conv_out"], 4)
            sp.dma_start(aux[:, 2:4, :].rearrange("p a (b c) -> p (a b) c", b=2),
                         T["p"][0, 0].rearrange("(t p) c -> p t c", p=P)).then_inc(s["p_in"], 16)
            sp.wait_ge(s["q_lo"], H1)
            sp.dma_start(tab[:, :, :], T["c_ret_rope"]).then_inc(s["ret_tab_in"], 16)
            with sp.Fori(0, 2) as i:
                load_ffn(FFN, i, i, 4)
                for m in range(4):
                    load(FFN.chunk(8 + m, i), down[i, m], 8)
            load_ffn(FFN_LAST, 0, 2, 3)
            down = T["w_down"][0, 2048:D_FF, :].rearrange("(k p) (m c) -> m p k c", p=P, c=256)
            for m in range(4):
                load(FFN_LAST.chunk(6 + m), down[m], 6)
            load(PROJ.chunk(0), T["w_ple_proj"][0].rearrange("(k p) c -> p k c", p=P), 2)
            pg = T["w_ple_gate"][0].rearrange("(k p) (m c) -> m p k c", p=P, c=256)
            for m in range(4):
                load(GATE.chunk(m), pg[m], KD)

            r_in = T["ret_w_in_2"][0]
            r_qk = r_in[:, 0:2 * RQK].rearrange("(k p) (t h c) -> t h p k c", p=P, t=2, c=256)
            r_vg = r_in[:, 2 * RQK:].rearrange("(k p) (t h n c) -> t h n p k c", p=P, t=2, n=2, c=256)
            r_out = T["ret_w_out_2"][0].rearrange("(h k p) (n c) -> h n p k c", p=P, k=4, c=512)
            with sp.Fori(0, RH) as h:
                load(RET.chunk(0, h), r_qk[0, h], KD)
                load(RET.chunk(1, h), r_qk[1, h], KD)
                load(RET.chunk(2, h), r_vg[0, h, 0], KD)
                load(RET.chunk(3, h), r_vg[0, h, 1], KD)
                load(RET.chunk(4, h), r_vg[1, h, 0], KD)
                load(RET.chunk(5, h), r_vg[1, h, 1], KD)
                load(RET.chunk(6, h), r_out[h, 0], 4)
                load(RET.chunk(7, h), r_out[h, 1], 4)

            def load_mlp(ph, layer):
                w1 = T["mlp_w1_2"][layer].rearrange("(k p) (g m c) -> g m p k c", p=P, m=4, c=256)
                w2 = T["mlp_w2_2"][layer].rearrange("(g k p) (m c) -> g m p k c", p=P, k=8, c=256)
                with sp.Fori(0, MLP_GROUPS) as i:
                    for m in range(4):
                        load(ph.chunk(m, i), w1[i, m], KD)
                    for m in range(4):
                        load(ph.chunk(4 + m, i), w2[i, m], 8)

            load_mlp(MLP_A, 0)
            sp.wait_ge(s["ext_built"], 3)
            sp.dma_start(ext_rows, ext[:, :].unsqueeze(1).to_broadcast([H2, P, EXT])).then_inc(s["ext_out"], 16)
            sp.wait_ge(s["ext_out"], 16)
            sp.wait_ge(s["mask_set"], 4)
            a_in = T["att_w_in_2"][0].rearrange("(k p) (t g c) -> t g p k c", p=P, t=3, c=256)
            a_out = T["att_w_out_2"][0].rearrange("(g k p) c -> g p k c", p=P, k=2)
            ext_h = ext_rows.rearrange("(g h) q e -> g h (q e)", h=4)
            with sp.Fori(0, H2 // 4) as g:
                for t in range(2):
                    load(ATT.chunk(t, g), a_in[t, g], KD)
                sp.wait_ge(s["att_mx"], H1 * 4 + g * 16)
                for h in range(4):
                    for q0, width in ((0, 448), (64, 512)):
                        rows = ext_h[g, h, 0:P * (EXT - 1)].rearrange("(q e) -> q e", e=EXT - 1)
                        sp.dma_start(aux[q0:q0 + 64, h, 0:width], rows[q0:q0 + 64, 127:127 + width])\
                            .then_inc(s[f"bias_in{h}"], 16)
                load(ATT.chunk(2, g), a_in[2, g], KD)
                load(ATT.chunk(3, g), a_out[g], 2)
            load_mlp(MLP_B, 1)

            sp.wait_ge(s["fin_copied"], 8)
            for t in range(4):
                sp.dma_start(out[0, t * P:(t + 1) * P, :], xt[:, t, :]).then_inc(s["out_done"], 16)
            sp.wait_ge(s["out_done"], 64)

        @block.gpsimd
        def _(pool):
            pool.memset(ones[:, :], 1.0).then_inc(s["memset_done"], 1)
            pool.memset(eps[:, :], EPS).then_inc(s["memset_done"], 1)
            pool.dma_start(ident[:, :], T["c_ident"]).then_inc(s["consts_in"], 16)
            pool.dma_start(freq[:, :], T["c_freq"]).then_inc(s["consts_in"], 16)
            stage = aux[:, 1, 0:P]
            for name, n in GAIN_ROWS:
                at = GAIN_AT[name]
                lead = " ".join("abc"[:len(T[name].shape) - 1])
                rows = T[name].rearrange(f"{lead} (t p) -> ({lead} t) p", p=P)
                pool.dma_start(stage[at:at + n, :], rows).then_inc(s["rows_in"], 16)
            pool.dma_start(tab[:, 0, :].bitcast(I32), bass.AP(T["positions"].tensor, 0, [[0, P], [1, S]]))\
                .then_inc(s["pos_in"], 16)
            kr_raw = aux[:, 0, :].rearrange("p (k c) -> p k c", k=KD)
            w_in = T["w_in"][0].rearrange("(k p) c -> p k c", p=P)
            at = Q_RANK + KV_RANK
            for dst, src, n in ((0, 0, 32), (32, 16, 16), (48, 0, 16)):
                pool.dma_start(kr_raw[:, :, dst:dst + n], w_in[:, :, at + src:at + src + n])\
                    .then_inc(s["kr_in"], 16)
            pool.dma_start(ext[:, 255:255 + REL_TABLE], T["att_rel_bias_2"][0]).then_inc(s["ext_in"], 16)

            def lo(number, slot):
                pool.wait_ge(s["w_hi_ready"], number + 1)
                for n in range(4):
                    at = slice(n * 512, n * 512 + 512)
                    ins = pool.tensor_tensor(w_lo[:, slot, at], raw[:, slot, at], w_hi[:, slot, at].bitcast(F32),
                                             ALU.subtract)
                ins.then_inc(s["w_lo_ready"], 1)

            for c in range(UKV.chunk0):
                lo(c, c % 2)
            for ph, parts in ((UKV, ukv_parts()), (UQ, uq_parts())):
                pool.wait_ge(s["w_hi_ready"], ph.chunk0 + 1)
                for w_lo_part, w_hi_part, raw_part in parts:
                    ins = pool.tensor_tensor(w_lo_part, raw_part, w_hi_part.bitcast(F32), ALU.subtract)
                ins.then_inc(s["w_lo_ready"], 1)
            first = UQ.chunk0 + 1
            loops = (N_CHUNKS - first) // 2
            with pool.Fori(0, loops) as i:
                lo(first + 2 * i, first % 2)
                lo(first + 1 + 2 * i, (first + 1) % 2)
            for c in range(first + 2 * loops, N_CHUNKS):
                lo(c, c % 2)

        @block.tensor
        def _(pe):
            def chunk_ready(c):
                pe.wait_ge(s["w_lo_ready"], c.number + 1)

            def three(o, hi, lo, rhs_hi, rhs_lo, start, stop):
                pe.matmul(o, hi, rhs_hi, start=start, stop=False, skip_group_check=True)
                pe.matmul(o, hi, rhs_lo, start=False, stop=False, skip_group_check=True)
                return pe.matmul(o, lo, rhs_hi, start=False, stop=stop, skip_group_check=True)

            def group_empty(g):
                if not g.virgin:
                    pe.wait_ge(pair_free[g.pair], g.empty)

            def product(c, g, kt, cols, m0, act_hi, act_lo, act_wait=None):
                hi = w_hi[:, c.slot, 0:kt * cols].rearrange("p (k c) -> p k c", k=kt)
                lo = w_lo[:, c.slot, 0:kt * cols].rearrange("p (k c) -> p k c", k=kt)
                group_empty(g)
                for k in range(kt):
                    if act_wait is not None:
                        act_wait(k)
                    for m in range(2):
                        at = slice((m0 + m) * P, (m0 + m) * P + P)
                        ins = three(ps[:, g.bank(m), :], hi[:, k, at], lo[:, k, at],
                                    act_hi[:, k, :], act_lo[:, k, :], k == 0, k == kt - 1)
                ins.then_inc(s["group_done"], 1)

            def normed(norm):
                return lambda k: pe.wait_ge(s["norm_lo"], norm.out0 + k + 1)

            def stat(norm):
                pe.wait_ge(s["norm_acc"], norm.acc0 + norm.n - 1)
                if norm.index:
                    pe.wait_ge(s["norm_ln"], norm.index)
                pe.matmul(ps[:, 7, :], ones[:, :], ssq, start=True, stop=True).then_inc(s["norm_stat"], 1)

            def stat_columns(norm):
                pe.wait_ge(s["norm_acc"], norm.acc0 + norm.n - 1)
                for t in range(4):
                    ins = pe.matmul(ps[:, 6, t:t + 1], ssq[:, t * P:(t + 1) * P], ones[:, 0:1], start=True, stop=True)
                ins.then_inc(s["col_stat"], 1)

            pe.wait_ge(s["rows_in"], 16 * len(GAIN_ROWS))
            pe.wait_ge(s["consts_in"], 32)
            pe.transpose(ps[:, 6, 0:N_GAINS], aux[0:N_GAINS, 1, 0:P], ident[0:N_GAINS, 0:N_GAINS])\
                .then_inc(s["gains_t"], 1)
            xt = o_buf[:, :, :].rearrange("p (t h) s -> p t (h s)", t=4)
            pe.wait_ge(s["x_in"], 64)
            for f in range(KD):
                if f >= 2:
                    pe.wait_ge(s["x_copied"], f - 1)
                for t in range(4):
                    ins = pe.transpose(ps[:, 4 + f % 2, t * P:(t + 1) * P], xt[:, t, f * P:(f + 1) * P],
                                       ident[:, :])
                ins.then_inc(s["x_t"], 1)
            pe.wait_ge(s["memset_done"], 2)
            stat(N_MIX)

            chunk_ready(MIX.chunk(0))
            product(MIX.chunk(0), MIX.group(0), KD, 256, 0, hn_hi, hn_lo, normed(N_MIX))
            chunk_ready(MIX.chunk(1))
            product(MIX.chunk(1), MIX.group(1), KD, 256, 0, hn_hi, hn_lo)
            pe.wait_ge(s["kr_lo"], 1)
            for k in range(KD):
                ins = three(ps[:, 4, :], hid_hi[:, 4 + k // 4, (k % 4) * P:(k % 4) * P + P],
                            hid_lo[:, 4 + k // 4, (k % 4) * P:(k % 4) * P + P],
                            hn_hi[:, k, :], hn_lo[:, k, :], k == 0, k == KD - 1)
            ins.then_inc(s["kr_done"], 1)
            for n in range(2, 8):
                chunk_ready(MIX.chunk(n))
                product(MIX.chunk(n), MIX.group(n), KD, 256, 0, hn_hi, hn_lo)
                if n == 2:
                    stat(N_Q)
                if n == 3:
                    stat(N_KV)
            c = UKV.chunk(0)
            chunk_ready(c)
            hi = w_hi[:, c.slot, :].rearrange("p (k t c) -> p k t c", k=2, t=2)
            lo = w_lo[:, c.slot, :].rearrange("p (k t c) -> p k t c", k=2, t=2)
            pe.wait_ge(s["norm_lo"], N_KV.out0 + 2)
            for n in range(2):
                g = UKV.group(n)
                group_empty(g)
                for m in range(2):
                    heads = slice((2 * n + m) * P, (2 * n + m) * P + P)
                    for k in range(2):
                        ins = three(ps[:, g.bank(m), :], hi[:, k, 0, heads], lo[:, k, 0, heads],
                                    hid_hi[:, 2 + k, :], hid_lo[:, 2 + k, :], k == 0, k == 1)
                ins.then_inc(s["group_done"], 1)
            for n in range(2):
                g = UKV.group(2 + n)
                group_empty(g)
                for m in range(2):
                    t = slice((2 * n + m) * P, (2 * n + m) * P + P)
                    for k in range(2):
                        ins = three(ps[:, g.bank(m), :], hid_hi[:, 2 + k, t], hid_lo[:, 2 + k, t],
                                    hi[:, k, 1, :], lo[:, k, 1, :], k == 0, k == 1)
                ins.then_inc(s["group_done"], 1)
            c = UQ.chunk(0)
            chunk_ready(c)
            hi = w_hi[:, c.slot, :].rearrange("p (k c) -> p k c", k=2)
            lo = w_lo[:, c.slot, :].rearrange("p (k c) -> p k c", k=2)
            pe.wait_ge(s["norm_lo"], N_Q.out0 + 2)
            pe.wait_ge(s["krope"], 2)
            for m in range(2):
                at = slice(768 + m * P, 768 + m * P + P)
                for k in range(2):
                    ins = three(ps[:, 4 + m, :], hi[:, k, at], lo[:, k, at], hid_hi[:, k, :], hid_lo[:, k, :],
                                k == 0, k == 1)
                ins.then_inc(s["sw_done"], 1)
            for n in range(4):
                g = UQ.group(n)
                group_empty(g)
                for m in range(2):
                    at = slice((2 * n + m) * DQ, (2 * n + m) * DQ + DQ)
                    for k in range(2):
                        ins = three(ps[0:DQ, g.bank(m), :], hi[:, k, at], lo[:, k, at],
                                    hid_hi[:, k, :], hid_lo[:, k, :], k == 0, k == 1)
                ins.then_inc(s["group_done"], 1)

            def scores(a, h, i=0):
                if not a.first(h, i):
                    pe.wait_ge(s["att_mx"], a.n(h, i) * 4)
                for t, _ in Q_ORDER:
                    for n, (q, k) in enumerate(a.qk(h)):
                        ins = pe.matmul(score_ps(t), q[:, t * P:(t + 1) * P], k[:, 0:(t + 1) * P],
                                        start=(n == 0), stop=(n == 2), skip_group_check=True)
                    ins.then_inc(s["att_s"], 1)

            def transposes(a, h, i=0):
                if not a.first(h, i):
                    pe.wait_ge(s["att_lo"], a.n(h, i) * 4)
                pe.wait_ge(s["att_p"], a.n(h, i) * 4 + 4)
                for j, _ in K_ORDER:
                    for t in range(j, 4):
                        ins = pe.transpose(trans_ps(j)[:, (t - j) * P:(t - j + 1) * P],
                                           score_sb(h, t)[:, j * P:(j + 1) * P], ident[:, :])
                    ins.then_inc(s["att_t"], 1)

            def values(a, h, i=0):
                if h >= 2 or a.block2:
                    pe.wait_ge(s["att_o"], a.n(h, i) - 1)
                for n, (j, _) in enumerate(K_ORDER):
                    pe.wait_ge(s["att_lo"], a.n(h, i) * 4 + n + 1)
                    ins = three(ps[:, 6 + h % 2, j * P:], a.v(hid_hi, h, j), a.v(hid_lo, h, j),
                                a.pt(hid_hi, h, j), a.pt(hid_lo, h, j), n == 0, n == 3)
                ins.then_inc(s["att_pv"], 1)

            def attend(a, i=0, between=None):
                scores(a, 0, i)
                scores(a, 1, i)
                if between:
                    between()
                transposes(a, 0, i)
                for h in range(a.heads):
                    if h + 2 < a.heads:
                        scores(a, h + 2, i)
                    values(a, h, i)
                    if h + 1 < a.heads:
                        transposes(a, h + 1, i)

            for n in (2, 3):
                pe.wait_ge(pair_free[n % 2], UKV.group(n).freed(1))
            pe.wait_ge(s["krep_done"], 32)
            pe.wait_ge(s["q_lo"], H1)
            attend(ATT1)
            stat(N_CONVG)
            stat(N_ATTG)
            for m in range(4):
                chunk_ready(WOUT.chunk(m))
                if m == 0:
                    pe.wait_ge(s["norm_lo"], N_CONVG.out0 + 4)
                product(WOUT.chunk(m), WOUT.group(m), KD, 256, 0, hn_hi, hn_lo,
                        (lambda k: k < 4 and pe.wait_ge(s["norm_lo"], N_ATTG.out0 + k + 1)) if m == 0 else None)
            stat(N_POST)

            def ffn(ph, i, g_hid, kt, first=False):
                for j in range(kt // 2):
                    for n in range(2):
                        chunk_ready(ph.chunk(2 * j + n, i))
                        product(ph.chunk(2 * j + n, i), ph.group(2 * j + n, i), KD, 256, 0, hn_hi, hn_lo,
                                normed(N_FFN) if first and j == 0 and n == 0 else None)
                        if first and j == 0 and n == 0:
                            stat(N_FFN)
                for m in range(4):
                    c = ph.chunk(kt + m, i)
                    chunk_ready(c)
                    product(c, ph.group(kt + m, i), kt, 256, 0, hid_hi, hid_lo,
                            (lambda k: pe.wait_ge(s["ffn_lo"], g_hid + k + 1)) if m == 0 else None)

            pe.wait_ge(s["p_in"], 16)
            pt = aux[:, 2:4, :].rearrange("p a (b c) -> p (a b) c", b=2)
            for f in range(2):
                for t in range(4):
                    ins = pe.transpose(ps[:, 4 + f, t * P:(t + 1) * P], pt[:, t, f * P:(f + 1) * P], ident[:, :])
                ins.then_inc(s["p_t"], 1)
            ffn(FFN, 0, 0, 8, first=True)
            ffn(FFN, 1, 8, 8)
            ffn(FFN_LAST, 0, 16, 6)
            stat(N_FPOST)
            c = PROJ.chunk(0)
            chunk_ready(c)
            pe.wait_ge(s["p_lo"], 2)
            for n in range(4):
                product(c, PROJ.group(n), 2, 1024, 2 * n, hid_hi[:, 8:10, :], hid_lo[:, 8:10, :])
            stat(N_PLE)
            for m in range(4):
                chunk_ready(GATE.chunk(m))
                product(GATE.chunk(m), GATE.group(m), KD, 256, 0, hn_hi, hn_lo,
                        (lambda k: pe.wait_ge(s["ple_xlo"], k + 1)) if m == 0 else None)


            def token_major(c, g):
                hi = w_hi[:, c.slot, :].rearrange("p (k c) -> p k c", k=KD)
                lo = w_lo[:, c.slot, :].rearrange("p (k c) -> p k c", k=KD)
                group_empty(g)
                for t in range(4):
                    o = ps[:, g.bank(t // 2), (t % 2) * 256:(t % 2) * 256 + 256]
                    for k in range(KD):
                        at = slice(t * P, t * P + P)
                        ins = three(o, hn_hi[:, k, at], hn_lo[:, k, at], hi[:, k, :], lo[:, k, :],
                                    k == 0, k == KD - 1)
                ins.then_inc(s["group_done"], 1)

            def sum_hook(h):
                def hook(k):
                    if k == 2:
                        pe.wait_ge(s["ret_sum"], h * 3 + 3)
                        pe.matmul(ps[:, 4, :], ones[:, :], ssq, start=True, stop=True).then_inc(s["ret_mean"], 1)
                    if k == 7:
                        pe.wait_ge(s["ret_acc"], h * 3 + 3)
                        pe.matmul(ps[:, 5, :], ones[:, :], ssq, start=True, stop=True).then_inc(s["ret_var"], 1)
                return hook

            def head(h, first=False):
                for n in range(2):
                    chunk_ready(RET.chunk(n, h))
                    product(RET.chunk(n, h), RET.group(n, h), KD, 256, 0, hn_hi, hn_lo,
                            normed(N_RET) if first and n == 0 else None)
                    if first and n == 0:
                        stat_columns(N_RET)
                        stat(N_RET)
                chunk_ready(RET.chunk(2, h))
                token_major(RET.chunk(2, h), RET.group(2, h))
                pe.wait_ge(s["ret_qk_lo"], h * 4 + 4)
                for j, _ in K_ORDER:
                    o = ret_score(j)
                    for k in range(2):
                        at = slice(j * P, j * P + P)
                        ins = three(o, hid_hi[:, 2 + k, at], hid_lo[:, 2 + k, at],
                                    hid_hi[:, k, j * P:], hid_lo[:, k, j * P:], k == 0, k == 1)
                    ins.then_inc(s["ret_s"], 1)
                chunk_ready(RET.chunk(3, h))
                token_major(RET.chunk(3, h), RET.group(3, h))
                pe.wait_ge(s["ret_s_lo"], h * 4 + 4)
                for n in (2, 3):
                    pe.wait_ge(pair_free[n % 2], RET.group(n, h).freed(1))
                for d in range(4):
                    for j in range(4):
                        ins = three(ps[:, 4 + d, j * P:], ret_v(hid_hi, j, d), ret_v(hid_lo, j, d),
                                    hid_hi[:, 8 + j, j * P:], hid_lo[:, 8 + j, j * P:], j == 0, j == 3)
                    ins.then_inc(s["ret_pv"], 1)
                for n in (4, 5):
                    chunk_ready(RET.chunk(n, h))
                    product(RET.chunk(n, h), RET.group(n, h), KD, 256, 0, hn_hi, hn_lo,
                            sum_hook(h) if n == 4 else None)
                for n in range(4):
                    c = RET.chunk(6 + n // 2, h)
                    if n % 2 == 0:
                        chunk_ready(c)
                    product(c, RET.group(6 + n, h), 4, 512, 2 * (n % 2), hid_hi[:, 12:16, :],
                            hid_lo[:, 12:16, :],
                            (lambda k: pe.wait_ge(s["ret_y_lo"], h * 4 + k + 1)) if n == 0 else None)

            head(0, first=True)
            with pe.Fori(1, RH) as h:
                head(h)

            def mlp(ph, norm, base):
                def body(i, first=False):
                    for m in range(4):
                        chunk_ready(ph.chunk(m, i))
                        product(ph.chunk(m, i), ph.group(m, i), KD, 256, 0, hn_hi, hn_lo,
                                normed(norm) if first and m == 0 else None)
                        if first and m == 0:
                            stat(norm)
                    for m in range(4):
                        chunk_ready(ph.chunk(4 + m, i))
                        product(ph.chunk(4 + m, i), ph.group(4 + m, i), 8, 256, 0, hid_hi, hid_lo,
                                (lambda k: pe.wait_ge(s["mlp_lo"], base + i * 8 + k + 1)) if m == 0 else None)

                body(0, first=True)
                with pe.Fori(1, MLP_GROUPS) as i:
                    body(i)

            mlp(MLP_A, N_MLPA, 0)

            def four_heads(i, first=False):
                for n in range(2):
                    chunk_ready(ATT.chunk(n, i))
                    product(ATT.chunk(n, i), ATT.group(n, i), KD, 256, 0, hn_hi, hn_lo,
                            normed(N_ATT) if first and n == 0 else None)
                    if first and n == 0:
                        stat_columns(N_ATT)
                        stat(N_ATT)
                pe.wait_ge(s["att_in_lo"], i * 4 + 4)

                def project_v():
                    pe.wait_ge(s["att_mx"], ATT2.n(1, i) * 4 + 4)
                    chunk_ready(ATT.chunk(2, i))
                    token_major(ATT.chunk(2, i), ATT.group(2, i))
                    pe.wait_ge(pair_free[0], ATT.group(2, i).freed(1))

                attend(ATT2, i, project_v)
                c = ATT.chunk(3, i)
                chunk_ready(c)
                pe.wait_ge(s["att_o"], ATT2.n(3, i) + 1)
                for n in range(4):
                    product(c, ATT.group(3 + n, i), 2, 1024, 2 * n, hid_hi[:, 6:8, :], hid_lo[:, 6:8, :])

            four_heads(0, first=True)
            with pe.Fori(1, H2 // 4) as i:
                four_heads(i)
            mlp(MLP_B, N_MLPB, MLP_GROUPS * 8)
            stat(N_FINAL)
            for f in range(KD):
                pe.wait_ge(s["fin_tmp"], f + 1)
                if f >= 2:
                    pe.wait_ge(s["fin_copied"], f - 1)
                for t in range(4):
                    ins = pe.transpose(ps[:, 4 + f % 2, t * P:(t + 1) * P], tmp[:, f % 2, t * P:(t + 1) * P],
                                       ident[:, :])
                ins.then_inc(s["fin_t"], 1)

        @block.scalar
        def _(act):
            def split(c):
                act.wait_ge(raw_ready[c.slot], c.loads)
                if not c.early:
                    act.wait_ge(s["group_done"], c.two_before)
                act.activation(w_hi[:, c.slot, :], raw[:, c.slot, :], ACT.Copy).then_inc(s["w_hi_ready"], 1)

            def group_ready(g):
                act.wait_ge(s["group_done"], g.done)

            def copy_out(g, m, dst, func=ACT.Copy):
                act.activation(dst, ps[:, g.bank(m), :], func).then_inc(pair_free[g.pair], 1)

            def square(norm, t, src):
                if t == 0:
                    if norm.index:
                        act.wait_ge(s["norm_stat"], norm.index)
                    act.activation(ssq, src, ACT.Square).then_inc(s["norm_sq"], 1)
                else:
                    used = norm.acc0 + max(0, t - 2)
                    if used:
                        act.wait_ge(s["norm_acc"], used)
                    act.activation(sq[:, t % 2, :], src, ACT.Square).then_inc(s["norm_sq"], 1)

            def rsqrt_columns(nth, dim):
                act.wait_ge(s["col_stat"], nth + 1)
                act.activation(r_col[:, 0:4], ps[:, 6, 0:4], ACT.Ln, scale=1.0 / dim, bias=eps[:, 0:1])\
                    .then_inc(s["col_ln"], 1)
                act.wait_ge(s["col_ln"], nth + 1)
                act.activation(r_col[:, 0:4], r_col[:, 0:4], ACT.Exp, scale=-0.5).then_inc(s["col_r"], 1)

            def rsqrt(norm, dim):
                act.wait_ge(s["norm_stat"], norm.index + 1)
                act.activation(r_bc, ps[:, 7, :], ACT.Ln, scale=1.0 / dim, bias=eps[:, 0:1])\
                    .then_inc(s["norm_ln"], 1)
                act.wait_ge(s["norm_ln"], norm.index + 1)
                act.activation(r_bc, r_bc, ACT.Exp, scale=-0.5).then_inc(s["norm_r"], 1)

            def hi_tile(norm, t, dst):
                act.wait_ge(s["norm_tmp"], norm.out0 + t + 1)
                act.activation(dst, tmp[:, t % 2, :], ACT.Copy).then_inc(s["norm_hi"], 1)

            def gained_hi(norm, t, at):
                act.activation(hn_hi[:, t, :], x[:, t, :], ACT.Copy, scale=gain(*at)).then_inc(s["norm_hi"], 1)

            def gained_x(norm, g_last, name, row):
                for m in range(2):
                    act.wait_ge(pair_free[g_last.pair], g_last.freed(m))
                for t in range(KD):
                    gained_hi(norm, t, (name, row + t))
                    square(norm, t, x[:, t, :])

            act.wait_ge(s["gains_t"], 1)
            act.activation(gains[:, :], ps[:, 6, 0:N_GAINS], ACT.Copy).then_inc(s["gains_ready"], 1)
            act.wait_ge(s["angle"], ANGLE_STEPS)
            act.activation(tab[:, 1, :], aux[:, 2, :], ACT.Sin).then_inc(s["sin_done"], 1)
            act.activation(tab[:, 0, :], aux[:, 2, :], ACT.Sin, scale=0.5).then_inc(s["sin_done"], 1)
            act.preload_act_table_set("natural_log_exp_and_others")
            kr_dst = hid_hi[:, 4:6, :].rearrange("p a (k c) -> p (a k) c", c=P)
            kr_raw = aux[:, 0, :].rearrange("p (k c) -> p k c", k=KD)
            act.wait_ge(s["kr_in"], 48)
            act.activation(kr_dst[:, :, 0:64], kr_raw, ACT.Copy)
            act.activation(kr_dst[:, :, 64:128], kr_raw, ACT.Copy).then_inc(s["kr_hi"], 1)
            for f in range(KD):
                act.wait_ge(s["x_t"], f + 1)
                act.activation(x[:, f, :], ps[:, 4 + f % 2, :], ACT.Copy).then_inc(s["x_copied"], 1)
                act.wait_ge(s["x_copied"], f + 1)
                square(N_MIX, f, x[:, f, :])
            act.wait_ge(s["memset_done"], 2)
            rsqrt(N_MIX, D)
            split(MIX.chunk(0))
            for t in range(KD):
                hi_tile(N_MIX, t, hn_hi[:, t, :])

            split(MIX.chunk(1))
            g = MIX.group(0)
            group_ready(g)
            for m in range(2):
                square(N_Q, m, ps[:, g.bank(m), :])
                copy_out(g, m, o_buf[:, m, :])
            split(MIX.chunk(2))
            g = MIX.group(1)
            group_ready(g)
            for m in range(2):
                copy_out(g, m, o_buf[:, 2 + m, :])
            split(MIX.chunk(3))
            g = MIX.group(2)
            group_ready(g)
            for m in range(2):
                copy_out(g, m, o_buf[:, 4 + m, :])
            rsqrt(N_Q, Q_RANK)
            for t in range(2):
                hi_tile(N_Q, t, hid_hi[:, t, :])
            for t in range(2):
                act.wait_ge(pair_free[MIX.group(1).pair], MIX.group(1).freed(t))
                square(N_KV, t, o_buf[:, 2 + t, :])
            split(MIX.chunk(4))
            rsqrt(N_KV, KV_RANK)
            for t in range(2):
                hi_tile(N_KV, t, hid_hi[:, 2 + t, :])
            split(MIX.chunk(5))
            act.wait_ge(s["krope"], 3)
            act.activation(hid_hi[64:96, 4, :], aux[64:96, 0, :], ACT.Copy).then_inc(s["krope_hi"], 1)
            act.wait_ge(s["krope_hi"], 1)
            act.wait_ge(s["krope_lo"], 1)
            for ap in (hid_hi[:, :, :].bitcast(F32), hid_lo[:, :, :].bitcast(F32)):
                act.dma_start(ap[64:96, 5:12, :], ap[64:96, 4:5, :].to_broadcast([32, 7, S]))\
                    .then_inc(s["krep_done"], 16)
            split(MIX.chunk(6))
            g = MIX.group(5)
            group_ready(g)
            for m in range(2):
                copy_out(g, m, o_buf[:, 6 + m, :])
            split(MIX.chunk(7))

            for c, parts in ((UKV.chunk(0), ukv_parts()), (UQ.chunk(0), uq_parts())):
                act.wait_ge(raw_ready[c.slot], c.loads)
                act.wait_ge(s["group_done"], c.two_before)
                for _w_lo, w_hi_part, raw_part in parts:
                    ins = act.activation(w_hi_part, raw_part, ACT.Copy)
                ins.then_inc(s["w_hi_ready"], 1)
            for n in range(2):
                g = UKV.group(n)
                group_ready(g)
                for m in range(2):
                    for half in range(2):
                        act.activation(hid_hi[0:NOPE, 4 + 4 * n + 2 * m + half, :],
                                       ps[64 * half:64 * half + 64, g.bank(m), :], ACT.Copy)\
                            .then_inc(s["kv_hi"], 1)
            for n in range(2):
                g = UKV.group(2 + n)
                group_ready(g)
                for m in range(2):
                    act.activation(hid_hi[:, 12 + 2 * n + m, :], ps[:, g.bank(m), :], ACT.Copy)\
                        .then_inc(s["kv_hi"], 1)
            split(WOUT.chunk(0))
            for h in range(H1):
                g = UQ.group(h // 2)
                group_ready(g)
                if h >= 2:
                    act.wait_ge(s["q_lo"], h - 1)
                act.activation(tmp[0:NOPE, h % 2, :], ps[0:NOPE, g.bank(h % 2), :], ACT.Copy)\
                    .then_inc(s["q_nope"], 1)
                act.wait_ge(s["q_nope"], h + 1)
                act.wait_ge(s["q_rope"], h + 1)
                act.activation(hn_hi[0:DQ, h, :], tmp[0:DQ, h % 2, :], ACT.Copy).then_inc(s["q_hi"], 1)

            def exps(a, h, i=0):
                act.wait_ge(s["att_nmx"], a.n(h, i) + 1)
                for t in range(4):
                    col = slice(4 * (h % 2) + t, 4 * (h % 2) + t + 1)
                    act.activation(score_sb(h, t), score_sb(h, t), ACT.Exp, bias=nmx[:, col],
                                   accum_out=sm[:, col]).then_inc(s["att_exp"], 1)

            def prob_hi(a, h, i=0):
                if a.block2:
                    act.wait_ge(s["att_pv"], a.n(h, i) - 1)
                elif h:
                    act.wait_ge(s["att_pv"], h)
                for j, done in K_ORDER:
                    act.wait_ge(s["att_t"], a.n(h, i) * 4 + done)
                    act.activation(a.pt(hid_hi, h, j), trans_ps(j), ACT.Copy).then_inc(s["att_hi"], 1)

            def attend(a, empty_out, i=0, between=None):
                exps(a, 0, i)
                exps(a, 1, i)
                if between:
                    between()
                prob_hi(a, 0, i)
                for h in range(a.heads):
                    act.wait_ge(s["att_pv"], a.n(h, i) + 1)
                    empty_out(h)
                    if h + 1 < a.heads:
                        prob_hi(a, h + 1, i)
                    if h + 2 < a.heads:
                        exps(a, h + 2, i)

            def out_plain(h):
                act.activation(o_buf[64 * (h % 2):64 * (h % 2) + 64, h // 2, :], ATT1.out_ps(h), ACT.Copy)\
                    .then_inc(s["att_o"], 1)

            def out_hi(h):
                act.activation(hid_hi[64 * (h % 2):64 * (h % 2) + 64, 6 + h // 2, :], ATT2.out_ps(h), ACT.Copy)\
                    .then_inc(s["att_ohi"], 1)

            attend(ATT1, out_plain)

            act.wait_ge(s["conv_out"], 4)
            for t in range(4):
                square(N_CONVG, t, o_buf[:, 4 + t, :])
            rsqrt(N_CONVG, CONV)
            for t in range(4):
                hi_tile(N_CONVG, t, hn_hi[:, 4 + t, :])
            act.wait_ge(s["att_o"], H1)
            for t in range(4):
                square(N_ATTG, t, o_buf[:, t, :])
            rsqrt(N_ATTG, CONV)
            for t in range(4):
                hi_tile(N_ATTG, t, hn_hi[:, t, :])
            for m in range(4):
                split(WOUT.chunk(m + 1))
                g = WOUT.group(m)
                group_ready(g)
                for t in range(2):
                    square(N_POST, 2 * m + t, ps[:, g.bank(t), :])
                    copy_out(g, t, o_buf[:, 2 * m + t, :])
            rsqrt(N_POST, D)
            for t in range(KD):
                act.wait_ge(s["post_x"], 2 * t + 2)
                gained_hi(N_FFN, t, ("ffn_pre_norm", t))
                square(N_FFN, t, x[:, t, :])
            for f in range(2):
                act.wait_ge(s["p_t"], f + 1)
                act.activation(hid_hi[:, 8 + f, :], ps[:, 4 + f, :], ACT.Copy).then_inc(s["p_hi"], 1)

            def gate_up(ph, i, g_hid, pairs, first=False):
                for j in range(pairs):
                    gate = ph.group(2 * j, i)
                    split(ph.chunk(2 * j + 1, i))
                    if first and j == 0:
                        rsqrt(N_FFN, D)
                        act.preload_act_table_set("silu_and_others")
                    for m in range(2):
                        act.wait_ge(pair_free[gate.pair], gate.freed(m))
                        act.activation(sq[:, m, :], sq[:, m, :], ACT.Silu).then_inc(s["ffn_silu"], 1)
                    split(ph.chunk(2 * j + 2, i))
                    for m in range(2):
                        act.wait_ge(s["ffn_part"], g_hid + 2 * j + m + 1)
                        act.activation(hid_hi[:, 2 * j + m, :], tmp[:, m, :], ACT.Copy).then_inc(s["ffn_hi"], 1)

            for i in range(2):
                gate_up(FFN, i, i * 8, 4, first=i == 0)
                for m in range(4):
                    split(FFN.chunk(9 + m, i))
            gate_up(FFN_LAST, 0, 16, 3)
            for m in range(4):
                split(FFN_LAST.chunk(7 + m))
                g = FFN_LAST.group(6 + m)
                for t in range(2):
                    act.wait_ge(pair_free[g.pair], g.freed(t))
                    square(N_FPOST, 2 * m + t, o_buf[:, 2 * m + t, :])
            act.preload_act_table_set("natural_log_exp_and_others")
            rsqrt(N_FPOST, D)

            split(GATE.chunk(0))
            for n in range(4):
                g = PROJ.group(n)
                for m in range(2):
                    t = 2 * n + m
                    act.wait_ge(s["ple_x"], 2 * t + 2)
                    act.activation(hn_hi[:, t, :], x[:, t, :], ACT.Copy).then_inc(s["ple_xhi"], 1)
                group_ready(g)
                for m in range(2):
                    square(N_PLE, 2 * n + m, ps[:, g.bank(m), :])
                    copy_out(g, m, o_buf[:, 2 * n + m, :])
            rsqrt(N_PLE, D)
            act.preload_act_table_set("sigmoid_and_others")
            for m in range(4):
                split(GATE.chunk(m + 1))
                g = GATE.group(m)
                group_ready(g)
                if m == 3:
                    for t in range(2):
                        gained_hi(N_RET, t, ("mix_norm_g_2", t))
                for t in range(2):
                    if m:
                        act.wait_ge(s["ple_e"], 3 * (2 * m + t - 1))
                    copy_out(g, t, aux[:, 2 + t, :], ACT.Sigmoid)
                if m == 3:
                    for t in range(2, 6):
                        gained_hi(N_RET, t, ("mix_norm_g_2", t))
                for t in range(2):
                    act.wait_ge(s["ple_e"], 3 * (2 * m + t + 1))
                    if m == 3:
                        gained_hi(N_RET, 6 + t, ("mix_norm_g_2", 6 + t))
                    square(N_RET, 2 * m + t, x[:, 2 * m + t, :])
            act.dma_start(aux[:, :, :], T["c_decay"]).then_inc(s["decay_in"], 16)
            act.preload_act_table_set("natural_log_exp_and_others")

            def tokens_hi(g, slot, sem):
                group_ready(g)
                for t in range(4):
                    half = slice((t % 2) * 256, (t % 2) * 256 + 256)
                    act.activation(hid_hi[:, slot + t // 2, half], ps[:, g.bank(t // 2), half], ACT.Copy,
                                   scale=r_col[:, t:t + 1]).then_inc(sem, 1)

            def head(h, first=False):
                for n in range(2):
                    split(RET.chunk(n + 1, h))
                    if first and n == 0:
                        rsqrt_columns(0, D)
                        rsqrt(N_RET, D)
                    for t in range(2):
                        act.wait_ge(s["ret_tmp"], h * 4 + 2 * n + t + 1)
                        act.activation(hid_hi[:, 2 * n + t, :], tmp[:, t, :], ACT.Copy)\
                            .then_inc(s["ret_qk_hi"], 1)
                split(RET.chunk(3, h))
                act.wait_ge(s["col_r"], 1)
                tokens_hi(RET.group(2, h), 4, s["ret_v_hi"])
                for n, (j, _) in enumerate(K_ORDER):
                    act.wait_ge(s["ret_sd"], h * 4 + n + 1)
                    act.activation(hid_hi[:, 8 + j, j * P:], o_buf[:, j, j * P:], ACT.Copy)\
                        .then_inc(s["ret_s_hi"], 1)
                split(RET.chunk(4, h))
                tokens_hi(RET.group(3, h), 6, s["ret_v_hi"])
                act.wait_ge(s["ret_s_lo"], h * 4 + 4)
                for d in range(4):
                    act.wait_ge(s["ret_pv"], h * 4 + d + 1)
                    act.activation(o_buf[:, d, :], ps[:, 4 + d, :], ACT.Copy).then_inc(s["ret_o"], 1)
                split(RET.chunk(5, h))
                for t in range(4):
                    act.wait_ge(s["ret_d"], h * 4 + t + 1)
                    if t == 3:
                        act.wait_ge(s["ret_acc"], h * 3 + 1)
                    act.activation(sq[:, t % 2, :] if t else ssq, o_buf[:, t, :], ACT.Square)\
                        .then_inc(s["ret_sq"], 1)
                act.wait_ge(s["ret_var"], h + 1)
                act.activation(rstd[:, :], ps[:, 5, :], ACT.Ln, scale=1.0 / RDV, bias=eps[:, 0:1])\
                    .then_inc(s["ret_ln"], 1)
                act.wait_ge(s["ret_ln"], h + 1)
                act.activation(rstd[:, :], rstd[:, :], ACT.Exp, scale=-0.5).then_inc(s["ret_rstd"], 1)
                act.preload_act_table_set("silu_and_others")
                split(RET.chunk(6, h))
                for n in range(2):
                    g = RET.group(4 + n, h)
                    for m in range(2):
                        act.wait_ge(pair_free[g.pair], g.freed(m))
                        act.activation(o_buf[:, 4 + 2 * n + m, :], o_buf[:, 4 + 2 * n + m, :], ACT.Silu)\
                            .then_inc(s["ret_gate"], 1)
                    for t in (2 * n, 2 * n + 1):
                        act.wait_ge(s["ret_y"], h * 4 + t + 1)
                        act.activation(hid_hi[:, 12 + t, :], o_buf[:, t, :], ACT.Copy).then_inc(s["ret_y_hi"], 1)
                act.preload_act_table_set("natural_log_exp_and_others")
                split(RET.chunk(7, h))
                split(RET.chunk(8, h))

            head(0, first=True)
            with act.Fori(1, RH) as h:
                head(h)

            def mlp(ph, norm, base, next_norm, next_gain):
                def up(i, first=False):
                    for m in range(4):
                        split(ph.chunk(m + 1, i))
                        if first and m == 0:
                            rsqrt(norm, D)
                        g = ph.group(m, i)
                        if m:
                            act.wait_ge(s["mlp_lo"], base + i * 8 + 2 * m)
                        for t in range(2):
                            act.wait_ge(pair_free[g.pair], g.freed(t))
                            act.activation(tmp[:, t, :], sq[:, t, :], ACT.Square).then_inc(s["mlp_sq"], 1)
                        for t in range(2):
                            act.wait_ge(s["mlp_sq"], base + i * 8 + 2 * m + t + 1)
                            act.activation(hid_hi[:, 2 * m + t, :], tmp[:, t, :], ACT.Copy)\
                                .then_inc(s["mlp_hi"], 1)

                def down_splits(i):
                    for m in range(4):
                        split(ph.chunk(5 + m, i))

                up(0, first=True)
                down_splits(0)
                with act.Fori(1, MLP_GROUPS - 1) as i:
                    up(i)
                    down_splits(i)
                i = MLP_GROUPS - 1
                up(i)
                for m in range(4):
                    if next_gain or m < 3:
                        split(ph.chunk(5 + m, i))
                    g = ph.group(4 + m, i)
                    for t in range(2):
                        act.wait_ge(pair_free[g.pair], g.freed(t))
                        if next_gain:
                            gained_hi(next_norm, 2 * m + t, (next_gain[0], next_gain[1] + 2 * m + t))
                        square(next_norm, 2 * m + t, x[:, 2 * m + t, :])

            gained_x(N_MLPA, RET.group(9, RH - 1), "mlp_norm_g_2", 0)
            mlp(MLP_A, N_MLPA, 0, N_ATT, ("mix_norm_g_2", 8))

            def four_heads(i, first=False):
                for n in range(2):
                    split(ATT.chunk(n + 1, i))
                    if first and n == 0:
                        rsqrt_columns(1, D)
                        rsqrt(N_ATT, D)
                    for m in range(2):
                        g = ATT.group(n, i)
                        act.wait_ge(pair_free[g.pair], g.freed(m))
                        act.activation(hid_hi[:, 2 * n + m, :], tmp[:, m, :], ACT.Copy)\
                            .then_inc(s["att_in_hi"], 1)

                def take_v():
                    split(ATT.chunk(3, i))
                    act.wait_ge(s["col_r"], 2)
                    tokens_hi(ATT.group(2, i), 4, s["att_in_hi"])

                attend(ATT2, out_hi, i, take_v)
                split(ATT.chunk(4, i))

            four_heads(0, first=True)
            with act.Fori(1, H2 // 4) as i:
                four_heads(i)
            gained_x(N_MLPB, ATT.group(6, H2 // 4 - 1), "mlp_norm_g_2", 8)
            mlp(MLP_B, N_MLPB, MLP_GROUPS * 8, N_FINAL, None)

            rsqrt(N_FINAL, D)
            for f in range(KD):
                act.wait_ge(s["fin_t"], f + 1)
                dst = o_buf[:, :, :].rearrange("p (t h) s -> p t (h s)", t=4)[:, :, f * P:(f + 1) * P]
                act.activation(dst, ps[:, 4 + f % 2, :].rearrange("p (t c) -> p t c", t=4), ACT.Copy)\
                    .then_inc(s["fin_copied"], 1)

        @block.vector
        def _(dve):
            def sums(norm, t):
                dve.wait_ge(s["norm_sq"], norm.sq0 + t + 1)
                if t >= 2:
                    dve.wait_ge(s["norm_acc"], norm.acc0 + t - 1)
                dve.tensor_tensor(ssq, ssq, sq[:, t % 2, :], ALU.add).then_inc(s["norm_acc"], 1)

            def all_sums(norm):
                for t in range(1, norm.n):
                    sums(norm, t)

            def low(norm, name, src, base, slot):
                hi_ap, lo_ap = base
                dve.wait_ge(s["norm_r"], norm.index + 1)
                for t in range(norm.n + 1):
                    if t < norm.n:
                        if norm.out0 + t >= 2:
                            dve.wait_ge(s["norm_lo"], norm.out0 + t - 1)
                        dve.scalar_tensor_tensor(tmp[:, t % 2, :], src(t), gain(*name(t)), r_bc, ALU.mult,
                                                 ALU.mult).then_inc(s["norm_tmp"], 1)
                    if t:
                        dve.wait_ge(s["norm_hi"], norm.out0 + t)
                        dve.tensor_tensor(lo_ap[:, slot + t - 1, :], tmp[:, (t - 1) % 2, :],
                                          hi_ap[:, slot + t - 1, :].bitcast(F32), ALU.subtract)\
                            .then_inc(s["norm_lo"], 1)

            def gained_lo(norm, t, at):
                dve.wait_ge(s["norm_hi"], norm.out0 + t + 1)
                dve.scalar_tensor_tensor(hn_lo[:, t, :], x[:, t, :], gain(*at), hn_hi[:, t, :].bitcast(F32),
                                         ALU.mult, ALU.subtract).then_inc(s["norm_lo"], 1)

            def gained_x(norm, name, row):
                for t in range(KD):
                    gained_lo(norm, t, (name, row + t))
                    if t:
                        sums(norm, t)

            def tokens_lo(g, slot, sem, before):
                for t in range(4):
                    half = slice((t % 2) * 256, (t % 2) * 256 + 256)
                    dve.wait_ge(sem, before + t // 2 * 2 + 2)
                    ins = dve.scalar_tensor_tensor(hid_lo[:, slot + t // 2, half], ps[:, g.bank(t // 2), half],
                                                   r_col[:, t:t + 1], hid_hi[:, slot + t // 2, half].bitcast(F32),
                                                   ALU.mult, ALU.subtract)
                    if t % 2:
                        ins.then_inc(pair_free[g.pair], 1)

            def scaled(g, m, dst):
                dve.tensor_tensor(dst, ps[:, g.bank(m), :], r_bc, ALU.mult).then_inc(pair_free[g.pair], 1)

            def group_ready(g):
                dve.wait_ge(s["group_done"], g.done)

            def add_to(g, m, dst):
                dve.tensor_tensor(dst, ps[:, g.bank(m), :], dst, ALU.add).then_inc(pair_free[g.pair], 1)

            hn, hid = (hn_hi, hn_lo), (hid_hi, hid_lo)

            dve.wait_ge(s["consts_in"], 32)
            dve.wait_ge(s["pos_in"], 16)
            a, n = aux[:, 2, :], aux[:, 3, :]
            steps = [
                lambda: dve.tensor_copy(a, tab[:, 0, :].bitcast(I32)),
                lambda: dve.tensor_scalar(a, a, freq[:, 0:1], None, ALU.mult),
                lambda: dve.tensor_scalar(n, a, INV_TWO_PI, ROUND, ALU.mult, ALU.add),
                lambda: dve.tensor_scalar(n, n, ROUND, None, ALU.subtract),
                lambda: dve.scalar_tensor_tensor(a, n, -TWO_PI[0], a, ALU.mult, ALU.add),
                lambda: dve.scalar_tensor_tensor(a, n, -TWO_PI[1], a, ALU.mult, ALU.add),
                lambda: dve.scalar_tensor_tensor(a, n, -TWO_PI[2], a, ALU.mult, ALU.add),
                lambda: dve.scalar_tensor_tensor(a, n, -TWO_PI[3], a, ALU.mult, ALU.add),
                lambda: dve.tensor_scalar(a, a, SIN_MAX, -SIN_MAX, ALU.min, ALU.max),
            ]
            assert len(steps) == ANGLE_STEPS
            for k, step in enumerate(steps):
                if k:
                    dve.wait_ge(s["angle"], k)
                step().then_inc(s["angle"], 1)
            dve.wait_ge(s["sin_done"], 2)
            dve.tensor_scalar(tab[:, 1, :], tab[:, 1, :], freq[:, 1:2], None, ALU.mult).then_inc(s["table"], 1)
            dve.tensor_tensor(tab[:, 0, :], tab[:, 0, :], tab[:, 0, :], ALU.mult).then_inc(s["table"], 1)
            dve.wait_ge(s["table"], 2)
            dve.tensor_scalar(tab[:, 0, :], tab[:, 0, :], -2.0, 1.0, ALU.mult, ALU.add).then_inc(s["table"], 1)
            kr = [ap[:, 4:6, :].rearrange("p a (k c) -> p (a k) c", c=P) for ap in hid]
            kr_raw = aux[:, 0, :].rearrange("p (k c) -> p k c", k=KD)
            dve.wait_ge(s["kr_hi"], 1)
            for at in (0, 64):
                ins = dve.tensor_tensor(kr[1][:, :, at:at + 64], kr_raw, kr[0][:, :, at:at + 64].bitcast(F32),
                                        ALU.subtract)
            ins.then_inc(s["kr_lo"], 1)
            dve.wait_ge(s["ext_in"], 16)
            dve.memset(ext[:, 0:255], 0.0).then_inc(s["ext_built"], 1)
            dve.memset(ext[:, 255 + REL_TABLE:], 0.0).then_inc(s["ext_built"], 1)
            dve.wait_ge(s["ext_built"], 1)
            dve.tensor_scalar(ext[:, 0:255], ext[:, 0:255], ext[:, 255:256], None, ALU.add)\
                .then_inc(s["ext_built"], 1)

            all_sums(N_MIX)
            dve.wait_ge(s["gains_ready"], 1)
            low(N_MIX, lambda t: ("mix_pre_norm", t), lambda t: x[:, t, :], hn, 0)

            all_sums(N_Q)
            dve.wait_ge(s["table"], 3)
            dve.wait_ge(s["kr_done"], 1)
            dve.tensor_tensor(aux[64:96, 0, :], ps[0:32, 4, :], tab[0:32, 0, :], ALU.mult).then_inc(s["krope"], 1)
            dve.tensor_tensor(aux[64:96, 2, :], ps[32:64, 4, :], tab[32:64, 1, :], ALU.mult)\
                .then_inc(s["krope"], 1)
            dve.wait_ge(s["krope"], 2)
            dve.tensor_tensor(aux[64:96, 0, :], aux[64:96, 0, :], aux[64:96, 2, :], ALU.add)\
                .then_inc(s["krope"], 1)
            low(N_Q, lambda t: ("q_norm", t), lambda t: o_buf[:, t, :], hid, 0)
            all_sums(N_KV)
            low(N_KV, lambda t: ("kv_norm", t), lambda t: o_buf[:, 2 + t, :], hid, 2)
            dve.wait_ge(s["krope_hi"], 1)
            dve.tensor_tensor(hid_lo[64:96, 4, :], aux[64:96, 0, :], hid_hi[64:96, 4, :].bitcast(F32),
                              ALU.subtract).then_inc(s["krope_lo"], 1)
            for half in range(2):
                cg, xv, bg = (MIX.group(2 + 3 * half + n) for n in range(3))
                u = [o_buf[:, 4 + 2 * half + m, :] for m in range(2)]
                y = [aux[:, 2 + m, :] for m in range(2)]
                group_ready(xv)
                for m in range(2):
                    dve.wait_ge(pair_free[cg.pair], cg.freed(m))
                    dve.tensor_tensor(u[m], ps[:, xv.bank(m), :], u[m], ALU.mult)\
                        .then_inc(pair_free[xv.pair], 1)
                done = half * 8
                for tap in range(3):
                    for m in range(2):
                        w = gain("conv_w", 4 * tap + 2 * half + m)
                        if tap == 0:
                            dve.wait_ge(pair_free[xv.pair], xv.freed(m))
                            ins = dve.tensor_scalar(y[m], u[m], w, None, ALU.mult)
                        else:
                            dve.wait_ge(s["conv"], done + 2 * tap + m - 1)
                            ins = dve.scalar_tensor_tensor(y[m][:, tap:], u[m][:, 0:S - tap], w, y[m][:, tap:],
                                                           ALU.mult, ALU.add)
                        ins.then_inc(s["conv"], 1)
                group_ready(bg)
                for m in range(2):
                    dve.wait_ge(s["conv"], done + 5 + m)
                    dve.tensor_tensor(u[m], ps[:, bg.bank(m), :], y[m], ALU.mult)\
                        .then_inc(pair_free[bg.pair], 1)
                for m in range(2):
                    dve.wait_ge(pair_free[bg.pair], bg.freed(m))
                dve.sem_inc(s["conv"], 2)
                dve.sem_inc(s["conv_out"], 2)

            for n in range(2):
                g = UKV.group(n)
                for m in range(2):
                    for half in range(2):
                        h = 4 * n + 2 * m + half
                        dve.wait_ge(s["kv_hi"], h + 1)
                        ins = dve.tensor_tensor(hid_lo[0:NOPE, 4 + h, :], ps[64 * half:64 * half + 64, g.bank(m), :],
                                                hid_hi[0:NOPE, 4 + h, :].bitcast(F32), ALU.subtract)
                    ins.then_inc(pair_free[g.pair], 1)
            for n in range(2):
                g = UKV.group(2 + n)
                for m in range(2):
                    dve.wait_ge(s["kv_hi"], H1 + 2 * n + m + 1)
                    dve.tensor_tensor(hid_lo[:, 12 + 2 * n + m, :], ps[:, g.bank(m), :],
                                      hid_hi[:, 12 + 2 * n + m, :].bitcast(F32), ALU.subtract)\
                        .then_inc(pair_free[g.pair], 1)
            for h in range(H1):
                g = UQ.group(h // 2)
                at, j = h % 2, h % 4
                dve.wait_ge(s["sw_done"], h // 4 + 1)
                dve.tensor_tensor(sq[64:96, at, :], ps[32 * j:32 * j + 32, 4 + h // 4, :],
                                  tab[32 * j:32 * j + 32, 1, :], ALU.mult).then_inc(s["q_part"], 1)
                dve.wait_ge(s["q_nope"], h + 1)
                dve.tensor_tensor(tmp[64:96, at, :], ps[64:96, g.bank(at), :], tab[64:96, 0, :], ALU.mult)\
                    .then_inc(pair_free[g.pair], 1)
                dve.wait_ge(s["q_part"], h + 1)
                dve.wait_ge(pair_free[g.pair], g.freed(at))
                dve.tensor_tensor(tmp[64:96, at, :], tmp[64:96, at, :], sq[64:96, at, :], ALU.add)\
                    .then_inc(s["q_rope"], 1)
                dve.wait_ge(s["q_hi"], h + 1)
                dve.tensor_tensor(hn_lo[0:DQ, h, :], tmp[0:DQ, at, :], hn_hi[0:DQ, h, :].bitcast(F32),
                                  ALU.subtract).then_inc(s["q_lo"], 1)

            def masked_scores(a, h, i=0):
                if a.block2:
                    dve.wait_ge(s["mask_set"], 4)
                    dve.wait_ge(s[f"bias_in{h}"], i * 32 + 32)
                for t, done in Q_ORDER:
                    dve.wait_ge(s["att_s"], a.n(h, i) * 4 + done)
                    if a.block2:
                        dve.nop(nofuse=True)
                    col = 4 * (h % 2) + t
                    dve.tensor_tensor_reduce(score_sb(h, t), score_ps(t),
                                             aux[:, h if a.block2 else 1, 512 - 128 * (t + 1):],
                                             1.0 if a.block2 else DQ ** -0.5, FMIN, ALU.add, ALU.max,
                                             mx[:, col:col + 1]).then_inc(s["att_mx"], 1)
                dve.wait_ge(s["att_mx"], a.n(h, i) * 4 + 4)
                four = slice(4 * (h % 2), 4 * (h % 2) + 4)
                dve.tensor_scalar(nmx[:, four], mx[:, four], -1.0, None, ALU.mult).then_inc(s["att_nmx"], 1)

            def probabilities(a, h, i=0):
                four = slice(4 * (h % 2), 4 * (h % 2) + 4)
                dve.wait_ge(s["att_exp"], a.n(h, i) * 4 + 4)
                dve.reciprocal(rs[:, four], sm[:, four]).then_inc(s["att_rs"], 1)
                dve.wait_ge(s["att_rs"], a.n(h, i) + 1)
                for t in range(4):
                    col = 4 * (h % 2) + t
                    dve.tensor_scalar(score_sb(h, t), score_sb(h, t), rs[:, col:col + 1], None, ALU.mult)\
                        .then_inc(s["att_p"], 1)

            def prob_lo(a, h, i=0):
                for j, done in K_ORDER:
                    dve.wait_ge(s["att_hi"], a.n(h, i) * 4 + done)
                    dve.tensor_tensor(a.pt(hid_lo, h, j), trans_ps(j), a.pt(hid_hi, h, j).bitcast(F32),
                                      ALU.subtract).then_inc(s["att_lo"], 1)

            def out_lo(h, i):
                rows = slice(64 * (h % 2), 64 * (h % 2) + 64)
                dve.wait_ge(s["att_ohi"], h + 1 + i * 4)
                dve.tensor_tensor(hid_lo[rows, 6 + h // 2, :], ATT2.out_ps(h),
                                  hid_hi[rows, 6 + h // 2, :].bitcast(F32), ALU.subtract).then_inc(s["att_o"], 1)

            def attend(a, i=0, between=None):
                masked_scores(a, 0, i)
                masked_scores(a, 1, i)
                probabilities(a, 0, i)
                probabilities(a, 1, i)
                if between:
                    between()
                prob_lo(a, 0, i)
                for h in range(a.heads):
                    if h + 2 < a.heads:
                        masked_scores(a, h + 2, i)
                    if a.block2:
                        out_lo(h, i)
                    if h + 1 < a.heads:
                        prob_lo(a, h + 1, i)
                    if h + 2 < a.heads:
                        probabilities(a, h + 2, i)

            dve.wait_ge(s["mask_in"], 16)
            attend(ATT1)

            all_sums(N_CONVG)
            low(N_CONVG, lambda t: ("conv_group_norm", t), lambda t: o_buf[:, 4 + t, :], hn, 4)
            all_sums(N_ATTG)
            low(N_ATTG, lambda t: ("attn_group_norm", t), lambda t: o_buf[:, t, :], hn, 0)
            all_sums(N_POST)

            dve.wait_ge(s["norm_r"], N_POST.index + 1)
            for t in range(KD):
                if t >= 2:
                    dve.wait_ge(s["post_x"], 2 * t - 2)
                dve.scalar_tensor_tensor(tmp[:, t % 2, :], o_buf[:, t, :], gain("mix_post_norm", t), r_bc,
                                         ALU.mult, ALU.mult).then_inc(s["post_x"], 1)
                dve.wait_ge(s["post_x"], 2 * t + 1)
                dve.tensor_tensor(x[:, t, :], x[:, t, :], tmp[:, t % 2, :], ALU.add).then_inc(s["post_x"], 1)
                if t:
                    gained_lo(N_FFN, t - 1, ("ffn_pre_norm", t - 1))
                if t >= 2:
                    sums(N_FFN, t - 1)
            gained_lo(N_FFN, KD - 1, ("ffn_pre_norm", KD - 1))
            sums(N_FFN, KD - 1)
            dve.memset(o_buf[:, :, :], 0.0).then_inc(s["o_zero"], 1)
            for f in range(2):
                dve.wait_ge(s["p_hi"], f + 1)
                dve.tensor_tensor(hid_lo[:, 8 + f, :], ps[:, 4 + f, :], hid_hi[:, 8 + f, :].bitcast(F32),
                                  ALU.subtract).then_inc(s["p_lo"], 1)
            dve.wait_ge(s["o_zero"], 1)

            dve.wait_ge(s["norm_r"], N_FFN.index + 1)

            def ffn(ph, i, g_hid, kt, next_norm=None):
                for j in range(kt // 2):
                    gate, up = ph.group(2 * j, i), ph.group(2 * j + 1, i)
                    done = g_hid + 2 * j
                    group_ready(gate)
                    if j:
                        dve.wait_ge(s["ffn_part"], done)
                    for m in range(2):
                        scaled(gate, m, sq[:, m, :])
                    group_ready(up)
                    if j:
                        dve.wait_ge(s["ffn_lo"], done)
                    for m in range(2):
                        scaled(up, m, tmp[:, m, :])
                    for m in range(2):
                        dve.wait_ge(s["ffn_silu"], done + m + 1)
                        dve.wait_ge(pair_free[up.pair], up.freed(m))
                        dve.tensor_tensor(tmp[:, m, :], tmp[:, m, :], sq[:, m, :], ALU.mult)\
                            .then_inc(s["ffn_part"], 1)
                    for m in range(2):
                        dve.wait_ge(s["ffn_hi"], done + m + 1)
                        dve.tensor_tensor(hid_lo[:, 2 * j + m, :], tmp[:, m, :],
                                          hid_hi[:, 2 * j + m, :].bitcast(F32), ALU.subtract)\
                            .then_inc(s["ffn_lo"], 1)
                for m in range(4):
                    g = ph.group(kt + m, i)
                    group_ready(g)
                    for t in range(2):
                        add_to(g, t, o_buf[:, 2 * m + t, :])
                        if next_norm and 2 * m + t >= 2:
                            sums(next_norm, 2 * m + t - 1)

            with dve.Fori(0, 2) as i:
                ffn(FFN, i, i * 8, 8)
            ffn(FFN_LAST, 0, 16, 6, N_FPOST)
            sums(N_FPOST, KD - 1)

            dve.wait_ge(s["norm_r"], N_FPOST.index + 1)
            for t in range(KD):
                dve.scalar_tensor_tensor(tmp[:, t % 2, :], o_buf[:, t, :], gain("ffn_post_norm", t), r_bc,
                                         ALU.mult, ALU.mult).then_inc(s["ple_x"], 1)
                dve.wait_ge(s["ple_x"], 2 * t + 1)
                dve.tensor_tensor(x[:, t, :], x[:, t, :], tmp[:, t % 2, :], ALU.add).then_inc(s["ple_x"], 1)
                dve.wait_ge(s["ple_x"], 2 * t + 2)
                dve.wait_ge(s["ple_xhi"], t + 1)
                dve.tensor_tensor(hn_lo[:, t, :], x[:, t, :], hn_hi[:, t, :].bitcast(F32), ALU.subtract)\
                    .then_inc(s["ple_xlo"], 1)
                if t % 2 and t > 1:
                    sums_upto = t - 2
                    for k in ((1,) if sums_upto == 1 else (sums_upto - 1, sums_upto)):
                        sums(N_PLE, k)
            for k in (6, 7):
                sums(N_PLE, k)
            dve.wait_ge(s["norm_r"], N_PLE.index + 1)

            def gated(m, t):
                g, k = GATE.group(m), 2 * m + t
                if k >= 2:
                    dve.wait_ge(s["ple_e"], 3 * k - 3)
                dve.scalar_tensor_tensor(tmp[:, t, :], o_buf[:, k, :], gain("ple_norm", k), r_bc, ALU.mult,
                                         ALU.mult).then_inc(s["ple_e"], 1)
                dve.wait_ge(s["ple_e"], 3 * k + 1)
                dve.wait_ge(pair_free[g.pair], g.freed(t))
                dve.tensor_tensor(tmp[:, t, :], tmp[:, t, :], aux[:, 2 + t, :], ALU.mult)\
                    .then_inc(s["ple_e"], 1)
                dve.wait_ge(s["ple_e"], 3 * k + 2)
                dve.tensor_tensor(x[:, k, :], x[:, k, :], tmp[:, t, :], ALU.add).then_inc(s["ple_e"], 1)

            for m in range(3):
                for t in range(2):
                    gated(m, t)
                    if 2 * m + t >= 2:
                        sums(N_RET, 2 * m + t - 1)
            for t in range(2):
                gained_lo(N_RET, t, ("mix_norm_g_2", t))
            gated(3, 0)
            sums(N_RET, 5)
            gained_lo(N_RET, 2, ("mix_norm_g_2", 2))
            gated(3, 1)
            for t in range(3, 7):
                gained_lo(N_RET, t, ("mix_norm_g_2", t))
            sums(N_RET, 6)
            gained_lo(N_RET, 7, ("mix_norm_g_2", 7))
            sums(N_RET, 7)

            cos, sin = tab[:, 0, :], tab[:, 1, :]
            dve.wait_ge(s["ret_tab_in"], 16)
            dve.wait_ge(s["norm_r"], N_RET.index + 1)
            for table in (cos, sin):
                dve.tensor_tensor(table, table, r_bc, ALU.mult).then_inc(s["tab_scaled"], 1)
            dve.wait_ge(s["tab_scaled"], 2)
            dve.wait_ge(s["decay_in"], 16)
            with dve.Fori(0, RH) as h:
                last = RET.group(1, h)
                dve.wait_ge(pair_free[last.pair], last.empty)
                for n in range(2):
                    if n:
                        dve.wait_ge(s["ret_qk_lo"], h * 4 + 2)
                    g = RET.group(n, h)
                    t1, t2 = ps[:, g.bank(0), :], ps[:, g.bank(1), :]
                    group_ready(g)
                    dve.tensor_tensor(tmp[:, 0, :], t1, cos, ALU.mult).then_inc(s["ret_part"], 1)
                    dve.tensor_tensor(sq[:, 0, :], t2, sin, ALU.mult).then_inc(s["ret_part"], 1)
                    dve.tensor_tensor(sq[:, 1, :], t1, sin, ALU.mult).then_inc(pair_free[g.pair], 1)
                    dve.tensor_tensor(tmp[:, 1, :], t2, cos, ALU.mult).then_inc(pair_free[g.pair], 1)
                    dve.wait_ge(s["ret_part"], h * 4 + 2 * n + 2)
                    dve.tensor_tensor(tmp[:, 0, :], tmp[:, 0, :], sq[:, 0, :], ALU.subtract)\
                        .then_inc(s["ret_tmp"], 1)
                    dve.wait_ge(pair_free[g.pair], g.freed(1))
                    dve.tensor_tensor(tmp[:, 1, :], tmp[:, 1, :], sq[:, 1, :], ALU.add).then_inc(s["ret_tmp"], 1)
                    for t in range(2):
                        dve.wait_ge(s["ret_qk_hi"], h * 4 + 2 * n + t + 1)
                        dve.tensor_tensor(hid_lo[:, 2 * n + t, :], tmp[:, t, :],
                                          hid_hi[:, 2 * n + t, :].bitcast(F32), ALU.subtract)\
                            .then_inc(s["ret_qk_lo"], 1)
                tokens_lo(RET.group(2, h), 4, s["ret_v_hi"], h * 8)
                for j, done in K_ORDER:
                    dve.wait_ge(s["ret_s"], h * 4 + done)
                    dve.tensor_tensor(o_buf[:, j, j * P:], ret_score(j), aux[:, h, 0:S - j * P], ALU.mult)\
                        .then_inc(s["ret_sd"], 1)
                for n, (j, _) in enumerate(K_ORDER):
                    dve.wait_ge(s["ret_s_hi"], h * 4 + n + 1)
                    dve.tensor_tensor(hid_lo[:, 8 + j, j * P:], o_buf[:, j, j * P:],
                                      hid_hi[:, 8 + j, j * P:].bitcast(F32), ALU.subtract)\
                        .then_inc(s["ret_s_lo"], 1)
                tokens_lo(RET.group(3, h), 6, s["ret_v_hi"], h * 8 + 4)
                for d in range(1, 4):
                    dve.wait_ge(s["ret_o"], h * 4 + d + 1)
                    if d > 1:
                        dve.wait_ge(s["ret_sum"], h * 3 + d - 1)
                    dve.tensor_tensor(ssq, o_buf[:, 0, :] if d == 1 else ssq, o_buf[:, d, :], ALU.add)\
                        .then_inc(s["ret_sum"], 1)
                dve.wait_ge(s["ret_mean"], h + 1)
                for t in range(4):
                    dve.scalar_tensor_tensor(o_buf[:, t, :], ps[:, 4, :], -1.0 / RDV, o_buf[:, t, :], ALU.mult,
                                             ALU.add).then_inc(s["ret_d"], 1)
                for t in range(1, 4):
                    dve.wait_ge(s["ret_sq"], h * 4 + t + 1)
                    if t > 1:
                        dve.wait_ge(s["ret_acc"], h * 3 + t - 1)
                    dve.tensor_tensor(ssq, ssq, sq[:, t % 2, :], ALU.add).then_inc(s["ret_acc"], 1)
                gate = RET.group(4, h)
                group_ready(gate)
                for m in range(2):
                    scaled(gate, m, o_buf[:, 4 + m, :])
                dve.wait_ge(s["ret_rstd"], h + 1)
                at = GAIN_AT["ret_gn_g_2"]
                head_gains = gains[:, at:at + 16].rearrange("p (h t) -> p h t", t=4)
                for t in range(4):
                    dve.scalar_tensor_tensor(o_buf[:, t, :], o_buf[:, t, :], head_gains[:, h, t:t + 1],
                                             rstd[:, :], ALU.mult, ALU.mult).then_inc(s["ret_ys"], 1)
                for n in range(2):
                    if n:
                        gate = RET.group(5, h)
                        group_ready(gate)
                        for m in range(2):
                            scaled(gate, m, o_buf[:, 6 + m, :])
                    for t in (2 * n, 2 * n + 1):
                        dve.wait_ge(s["ret_gate"], h * 4 + t + 1)
                        dve.wait_ge(s["ret_ys"], h * 4 + t + 1)
                        dve.tensor_tensor(o_buf[:, t, :], o_buf[:, t, :], o_buf[:, 4 + t, :], ALU.mult)\
                            .then_inc(s["ret_y"], 1)
                    for t in (2 * n, 2 * n + 1):
                        dve.wait_ge(s["ret_y_hi"], h * 4 + t + 1)
                        dve.tensor_tensor(hid_lo[:, 12 + t, :], o_buf[:, t, :],
                                          hid_hi[:, 12 + t, :].bitcast(F32), ALU.subtract)\
                            .then_inc(s["ret_y_lo"], 1)
                for n in range(4):
                    g = RET.group(6 + n, h)
                    group_ready(g)
                    for m in range(2):
                        add_to(g, m, x[:, 2 * n + m, :])

            def mlp(ph, norm, base, next_norm, next_gain):
                dve.wait_ge(s["norm_r"], norm.index + 1)

                def body(i):
                    last = isinstance(i, int)
                    for m in range(4):
                        g = ph.group(m, i)
                        group_ready(g)
                        if m:
                            dve.wait_ge(s["mlp_sq"], base + i * 8 + 2 * m)
                        for t in range(2):
                            dve.scalar_tensor_tensor(sq[:, t, :], ps[:, g.bank(t), :], 0.0, r_bc, ALU.max,
                                                     ALU.mult).then_inc(pair_free[g.pair], 1)
                        for t in range(2):
                            dve.wait_ge(s["mlp_hi"], base + i * 8 + 2 * m + t + 1)
                            dve.tensor_tensor(hid_lo[:, 2 * m + t, :], tmp[:, t, :],
                                              hid_hi[:, 2 * m + t, :].bitcast(F32), ALU.subtract)\
                                .then_inc(s["mlp_lo"], 1)
                    for m in range(4):
                        g = ph.group(4 + m, i)
                        group_ready(g)
                        for t in range(2):
                            add_to(g, t, x[:, 2 * m + t, :])
                        for t in (2 * m, 2 * m + 1):
                            if last and next_gain:
                                gained_lo(next_norm, t, (next_gain[0], next_gain[1] + t))
                            if last and t:
                                sums(next_norm, t)

                with dve.Fori(0, MLP_GROUPS - 1) as i:
                    body(i)
                body(MLP_GROUPS - 1)

            gained_x(N_MLPA, "mlp_norm_g_2", 0)
            for h in range(4):
                dve.memset(aux[0:64, h, 448:512], MASKED).then_inc(s["mask_set"], 1)
            mlp(MLP_A, N_MLPA, 0, N_ATT, ("mix_norm_g_2", 8))
            dve.wait_ge(s["norm_r"], N_ATT.index + 1)
            with dve.Fori(0, H2 // 4) as i:
                for n in range(2):
                    g = ATT.group(n, i)
                    group_ready(g)
                    if n:
                        dve.wait_ge(s["att_in_lo"], i * 4 + 2)
                    for m in range(2):
                        dve.scalar_tensor_tensor(tmp[:, m, :], ps[:, g.bank(m), :], 1.0 if n else DH ** -0.5,
                                                 r_bc, ALU.mult, ALU.mult).then_inc(pair_free[g.pair], 1)
                    for m in range(2):
                        dve.wait_ge(s["att_in_hi"], i * 8 + 2 * n + m + 1)
                        dve.tensor_tensor(hid_lo[:, 2 * n + m, :], tmp[:, m, :],
                                          hid_hi[:, 2 * n + m, :].bitcast(F32), ALU.subtract)\
                            .then_inc(s["att_in_lo"], 1)
                attend(ATT2, i, lambda: tokens_lo(ATT.group(2, i), 4, s["att_in_hi"], i * 8 + 4))
                for n in range(4):
                    g = ATT.group(3 + n, i)
                    group_ready(g)
                    for m in range(2):
                        add_to(g, m, x[:, 2 * n + m, :])
            gained_x(N_MLPB, "mlp_norm_g_2", 8)
            mlp(MLP_B, N_MLPB, MLP_GROUPS * 8, N_FINAL, None)

            dve.wait_ge(s["norm_r"], N_FINAL.index + 1)
            for f in range(KD):
                if f >= 2:
                    dve.wait_ge(s["fin_t"], f - 1)
                dve.scalar_tensor_tensor(tmp[:, f % 2, :], x[:, f, :], gain("final_norm_g_2", f), r_bc, ALU.mult,
                                         ALU.mult).then_inc(s["fin_tmp"], 1)


_INS = ["x", "p", "positions", "mix_pre_norm", "w_in", "q_norm", "kv_norm", "w_uq", "w_ukv", "conv_w",
        "attn_group_norm", "conv_group_norm", "w_out", "mix_post_norm", "ffn_pre_norm", "w_gate", "w_up",
        "w_down", "ffn_post_norm", "w_ple_proj", "ple_norm", "w_ple_gate", "mix_norm_g_2", "ret_w_in_2",
        "ret_gn_g_2", "ret_w_out_2", "att_w_in_2", "att_rel_bias_2", "att_w_out_2", "mlp_norm_g_2",
        "mlp_w1_2", "mlp_w2_2", "final_norm_g_2"]


def constants():
    import numpy as np
    f = np.float32
    half = ROPE // 2
    inv_freq = f(1) / (f(10000) ** (np.arange(half, dtype=f) / f(half)))
    part = np.arange(P)
    freq = np.stack([inv_freq[part % half], np.where(part % ROPE < half, -1, 1)], 1).astype(f)
    causal = np.zeros((P, S), f)
    causal[:, S - P:] = np.where(np.arange(P)[None, :] <= part[:, None], 0, MASKED)
    inv = np.exp(-np.log(f(10000)) * np.arange(RDK // 2, dtype=f) / f(RDK // 2)).astype(f)
    ang = inv[:, None] * np.arange(S, dtype=f)[None, :]
    ret_rope = np.stack([np.cos(ang), np.sin(ang)], 1).astype(f)
    log_gamma = np.log1p(-np.exp2(-5.0 - np.arange(RH)))
    key, query = part[:, None, None], np.arange(S)[None, None, :]
    decay = np.exp(log_gamma[None, :, None] * np.abs(query - key)) * RDK ** -0.5
    decay = np.where(key // 64 <= query // 64, decay, 0).astype(f)
    return {"c_ident": np.eye(P, dtype=f), "c_freq": freq, "c_causal": causal, "c_ret_rope": ret_rope,
            "c_decay": decay}


def kernel(**inputs):
    import numpy as _np
    import concourse.bacc as _bacc
    from concourse import mybir as _mybir
    from concourse.bass_utils import run_bass_kernel_spmd as _run

    nc = _bacc.Bacc("TRN2", target_bir_lowering=False, num_devices=1)
    arrays, tensors = {}, {}
    given = {name: inputs[name] for name in _INS}
    given.update(constants())
    for name, value in given.items():
        a = _np.ascontiguousarray(value)
        arrays[f"in_{name}"] = a
        tensors[name] = nc.dram_tensor(f"in_{name}", a.shape, _mybir.dt.from_np(a.dtype),
                                       kind="ExternalInput").ap()
    out = nc.dram_tensor("out_0", (1, S, D), F32, kind="ExternalOutput").ap()
    build(nc, tensors, out)
    r = _run(nc, [arrays], core_ids=[0])
    return r.results[0]["out_0"]
```

```python
from contextlib import ExitStack

import concourse.bass as bass
from concourse import mybir

F32 = mybir.dt.float32
F32R = mybir.dt.float32r
I32 = mybir.dt.int32
ALU = mybir.AluOpType
ACT = mybir.ActivationFunctionType
P = 128
S = 512
D = 1024
KD = D // P
CH = 2048
EPS = 1e-6
MASKED = -3.0e38
FMIN = -3.4028235e38
INV_TWO_PI = 0.15915494309189535
ROUND = 12582912.0
TWO_PI = (6.25, 0.03125, 0.00193500518798828125, 3.0199159819e-07)
SIN_MAX = 3.1415925
ANGLE_STEPS = 9

Q_RANK = KV_RANK = 256
ROPE = 32
CONV = 512
H1 = 8
NOPE = 64
DQ = NOPE + ROPE
CONV0 = Q_RANK + KV_RANK + ROPE
D_FF = 2816
RH = 4
RDK = 256
RDV = 512
RQK = RH * RDK
H2 = 16
DH = 64
REL_TABLE = 320
EXT = 640
MLP_GROUPS = 4

GAIN_ROWS = [("mix_pre_norm", 8), ("q_norm", 2), ("kv_norm", 2), ("conv_w", 12), ("attn_group_norm", 4),
             ("conv_group_norm", 4), ("mix_post_norm", 8), ("ffn_pre_norm", 8), ("ffn_post_norm", 8),
             ("ple_norm", 8), ("mix_norm_g_2", 16), ("ret_gn_g_2", 16), ("mlp_norm_g_2", 16),
             ("final_norm_g_2", 8)]
GAIN_AT = {}
_row = 0
for _name, _n in GAIN_ROWS:
    GAIN_AT[_name] = _row
    _row += _n
N_GAINS = _row


class Phase:

    def __init__(self, prev, groups, iters=1):
        self.chunks, self.groups, self.iters = len(groups), sum(groups), iters
        self.upto = [sum(groups[:j]) for j in range(len(groups) + 1)]
        self.pair = ((self.groups + 1) // 2, self.groups // 2)
        self.prev = prev
        if prev is None:
            self.chunk0, self.group0, self.pair0 = 0, 0, (0, 0)
        else:
            self.chunk0 = prev.chunk0 + prev.chunks * prev.iters
            self.group0 = prev.group0 + prev.groups * prev.iters
            self.pair0 = tuple(prev.pair0[p] + prev.pair[p] * prev.iters for p in (0, 1))
        assert iters == 1 or self.chunks % 2 == 0

    def chunk(self, j, i=0):
        return Chunk(self, j, i)

    def group(self, pos, i=0):
        return Group(self, pos, i)


class Chunk:

    def __init__(self, ph, j, i):
        self.slot = (ph.chunk0 + j) % 2
        self.number = ph.chunk0 + j + i * ph.chunks
        self.loads = ((ph.chunk0 + j) // 2 + 1) * 16 + i * (ph.chunks // 2 * 16)
        self.early = isinstance(self.number, int) and self.number < 2
        if j >= 2:
            self.two_before = ph.group0 + i * ph.groups + ph.upto[j - 1]
        elif j == 1 and not self.early:
            self.two_before = ph.group0 + i * ph.groups
        elif not self.early:
            p = ph.prev
            self.two_before = ph.group0 - (p.upto[-1] - p.upto[-2])


class Group:

    def __init__(self, ph, pos, i):
        self.pair = pos % 2
        self.done = ph.group0 + pos + 1 + i * ph.groups
        self.empty = (ph.pair0[self.pair] + pos // 2) * 2 + i * (2 * ph.pair[self.pair])
        self.virgin = isinstance(self.empty, int) and self.empty == 0

    def bank(self, m):
        return 2 * self.pair + m

    def freed(self, m):
        return self.empty + m + 1


MIX = Phase(None, [1] * 8)
UKV = Phase(MIX, [4])
UQ = Phase(UKV, [4])
WOUT = Phase(UQ, [1] * 4)
PROJ = Phase(WOUT, [4])
FFN = Phase(PROJ, [1] * 12, 2)
FFN_LAST = Phase(FFN, [1] * 10)
GATE = Phase(FFN_LAST, [1] * 4)
RET = Phase(GATE, [1, 1, 1, 1, 1, 1, 2, 2], RH)
MLP_A = Phase(RET, [1] * 8, MLP_GROUPS)
ATT_ORDER = [(kind, g) for kind, g in zip("qkvqkvqkvoqkvooo", (0, 0, 0, 1, 1, 1, 2, 2, 2, 0, 3, 3, 3, 1, 2, 3))]
ATT = Phase(MLP_A, [4 if kind == "o" else 1 for kind, _ in ATT_ORDER])
MLP_B = Phase(ATT, [1] * 8, MLP_GROUPS)
N_CHUNKS = MLP_B.chunk0 + MLP_B.chunks * MLP_B.iters


class Norm:

    def __init__(self, prev, n, split):
        self.n, self.split = n, split
        self.index = prev.index + 1 if prev else 0
        self.sq0 = prev.sq0 + prev.n if prev else 0
        self.acc0 = prev.acc0 + prev.n - 1 if prev else 0
        self.out0 = prev.out0 + prev.split if prev else 0


N_MIX = Norm(None, 8, 8)
N_Q = Norm(N_MIX, 2, 2)
N_KV = Norm(N_Q, 2, 2)
N_CONVG = Norm(N_KV, 4, 4)
N_ATTG = Norm(N_CONVG, 4, 4)
N_POST = Norm(N_ATTG, 8, 0)
N_FFN = Norm(N_POST, 8, 8)
N_PLE = Norm(N_FFN, 8, 0)
N_FPOST = Norm(N_PLE, 8, 0)
N_RET = Norm(N_FPOST, 8, 8)
N_MLPA = Norm(N_RET, 8, 8)
N_ATT = Norm(N_MLPA, 8, 8)
N_MLPB = Norm(N_ATT, 8, 8)
N_FINAL = Norm(N_MLPB, 8, 0)

SEMAPHORES = """x_in0 x_in1 p_in rows0_in rows_in pos_in ident_in freq_in kr_in mask_in ext_in ext_out bias_in0
 bias_in1 bias_in2 bias_in3 decay_in ret_tab_in krep_done out_done raw_ready0 raw_ready1 w_hi_ready w_lo_ready group_done
 pair_free0 pair_free1 memset_done gains_t gains_ready x_t x_copied p_t p_hi p_lo
 norm_sq norm_acc norm_stat norm_ln norm_r col_stat col_ln col_r norm_tmp norm_hi norm_lo
 angle sin_done table kr_hi kr_lo kr_done krope krope_hi krope_lo
 conv_u conv conv_out kv_hi q_rope qr_hi qr_lo q_nope_hi q_rope_in q_rope_lo_in
 att_s att_mx att_nmx att_exp att_rs att_p att_t att_hi att_lo att_pv att_ohi att_o ext_built mask_set
 post_x o_zero ffn_hi ffn_lo ple_x ple_xhi ple_xlo ple_n ple_e
 ret_part ret_tmp ret_qk_hi ret_qk_lo ret_v_hi ret_s ret_sd ret_s_hi ret_s_lo ret_pv ret_o ret_sum
 ret_mean ret_d ret_sq ret_acc ret_var ret_ln ret_rstd ret_ys ret_gate ret_y ret_y_hi ret_y_lo
 mlp_sq mlp_hi mlp_lo att_in_hi att_in_lo tab_scaled ffn_silu ffn_part fin_tmp fin_t fin_copied""".split()


def build(nc, T, out):
    ext_rows = nc.dram_tensor("ext_rows", (H2, P, EXT), F32, kind="Internal").ap()

    with ExitStack() as ctx:
        def sb(name, shape, dt=F32):
            return ctx.enter_context(nc.sbuf_tensor(name, shape, dt))

        s = {name: ctx.enter_context(nc.semaphore(name)) for name in SEMAPHORES}
        raw_ready = [s["raw_ready0"], s["raw_ready1"]]
        pair_free = [s["pair_free0"], s["pair_free1"]]

        x = sb("x", [P, KD, S])
        o_at = nc.sbuf_base
        o_buf = sb("o_buf", [P, 8, S])
        probs_t = nc.alloc_sbuf_tensor_at("probs_t", (P, 8, S), F32R, offset=o_at)
        hn_hi = sb("hn_hi", [P, KD, S], F32R)
        hn_lo = sb("hn_lo", [P, KD, S], F32R)
        hid_at = nc.sbuf_base
        hid_hi = sb("hid_hi", [P, 16, S], F32R)
        hid_lo = sb("hid_lo", [P, 16, S], F32R)
        e_buf = nc.alloc_sbuf_tensor_at("e_buf", (P, KD, S), F32, offset=hid_at + 8 * S * 4)
        normed_x = nc.alloc_sbuf_tensor_at("normed_x", (P, KD, S), F32, offset=hid_at + 16 * S * 4)
        raw = sb("raw", [P, 2, CH])
        w_hi = sb("w_hi", [P, 2, CH], F32R)
        w_lo = sb("w_lo", [P, 2, CH], F32R)
        scr = sb("scr", [P, 6, S])
        tab = sb("tab", [P, 2, S])
        aux = sb("aux", [P, 4, S])
        ident = sb("ident", [P, P])
        ones = sb("ones", [P, P])
        gains = sb("gains", [P, N_GAINS])
        ext = sb("ext", [H2, EXT])
        freq = sb("freq", [P, 2])
        eps = sb("eps", [P, 1])
        small = sb("small", [P, 5, 8])
        rstd = sb("rstd", [P, S])
        ps = ctx.enter_context(nc.psum_tensor("ps", [P, 8, S], F32))

        ssq, sq, tmp, r_bc = scr[:, 0, :], scr[:, 1:3, :], scr[:, 3:5, :], scr[:, 5, :]
        sflat = scr[:, :, :].rearrange("p a b -> p (a b)")
        mx, nmx, sm, rs, r_col = (small[:, n, :] for n in range(5))

        def gain(name, t):
            at = GAIN_AT[name] + t
            return gains[:, at:at + 1]

        block = ctx.enter_context(nc.Block())

        def gain_rows(name):
            lead = " ".join("abc"[:len(T[name].shape) - 1])
            return T[name].rearrange(f"{lead} (t p) -> ({lead} t) p", p=P)

        def ukv_parts():
            slot = UKV.chunk0 % 2
            src = raw[:, slot, :].rearrange("p (k h t c) -> p k t h c", k=2, h=H1, t=2)
            hi_, lo_ = (ap[:, slot, :].rearrange("p (k t h c) -> p k t h c", k=2, t=2, h=H1) for ap in (w_hi, w_lo))
            for k in range(2):
                for t in range(2):
                    yield lo_[:, k, t], hi_[:, k, t], src[:, k, t]

        def uq_parts():
            slot = UQ.chunk0 % 2
            for k in range(2):
                src = raw[:, slot, k * 768:k * 768 + 768].rearrange("p (h c) -> p h c", h=H1)

                def to(start, width):
                    return [ap[:, slot, k * 1024 + start:k * 1024 + start + H1 * width]
                            .rearrange("p (h c) -> p h c", h=H1) for ap in (w_lo, w_hi)]
                yield (*to(0, NOPE), src[:, :, 0:NOPE])
                yield (*to(512, ROPE), src[:, :, NOPE:DQ])
                lo_, hi_ = to(768, ROPE)
                for half in (0, 16):
                    yield (lo_[:, :, half:half + 16], hi_[:, :, half:half + 16],
                           src[:, :, NOPE + 16 - half:NOPE + 32 - half])

        def spread_heads(engine, r, dst, src, moved):
            engine.wait_ge(s["qr_lo"], r + 1)
            for j in range(4):
                engine.dma_start(dst[64:96, 4 * r + j, :].bitcast(F32),
                                 src[32 * j:32 * j + 32, 2 + r, :].bitcast(F32)).then_inc(moved, 16)

        S_OFF = [0, 128, 384, 768]
        Q_ORDER = ((3, 1), (2, 3), (0, 3), (1, 4))
        K_ORDER = ((0, 1), (1, 3), (3, 3), (2, 4))

        Q1_HI = [hn_hi[0:DQ, h, :] for h in range(H1)]
        Q1_LO = [hn_lo[0:DQ, h, :] for h in range(H1)]
        K1_HI = [hid_hi[0:DQ, 4 + h, :] for h in range(H1)]
        K1_LO = [hid_lo[0:DQ, 4 + h, :] for h in range(H1)]

        class Attention:

            def __init__(self, base, heads, group=None, narrow=False):
                self.base, self.heads, self.group, self.narrow = base, heads, group, narrow
                self.block2 = group is not None
                self.slot = 8 * (group % 2) if self.block2 else 0

            def n(self, h):
                return self.base + h

            def first(self, h):
                return self.n(h) == 0

            def rows(self, h):
                return slice(64 * (h % 2), 64 * (h % 2) + 64)

            def qk(self, h):
                if self.block2:
                    q, k = self.slot + h // 2, self.slot + 2 + h // 2
                    r = self.rows(h)
                    return [(hid_hi[r, q, :], hid_hi[r, k, :]), (hid_hi[r, q, :], hid_lo[r, k, :]),
                            (hid_lo[r, q, :], hid_hi[r, k, :])]
                return [(Q1_HI[h], K1_HI[h]), (Q1_HI[h], K1_LO[h]), (Q1_LO[h], K1_HI[h])]

            def v(self, ap, h, j):
                if self.block2:
                    at = (j % 2) * 256 + (h // 2) * P
                    return ap[:, self.slot + 4 + j // 2, at:at + P]
                return ap[:, 12 + j, (h // 2) * P:(h // 2) * P + P]

            def pt(self, lo, j):
                ap = probs_t[:, 4 * lo + j, :] if self.block2 else (hid_hi, hid_lo)[lo][:, j, :]
                return ap[:, 0:512 - 128 * j]

            def out(self, ap, h):
                return ap[self.rows(h), self.slot + 6 + h // 2, :]

            def score_sb(self, h, t):
                at = (0 if self.narrow else h % 2) * 1280 + S_OFF[t]
                return sflat[:, at:at + 128 * (t + 1)]

            def score_ps(self, t):
                b, at = {3: (0, 0), 2: (1, 0), 0: (1, 384), 1: (2, 0)}[t]
                return ps[:, b + 4 * self.narrow, at:at + 128 * (t + 1)]

            def trans_ps(self, j):
                b, at = {0: (3, 0), 1: (4, 0), 3: (4, 384), 2: (5, 0)}[j]
                return ps[:, b + self.narrow, at:at + 512 - 128 * j]

            def out_bank(self, h):
                return 7 if self.narrow else 6 + h % 2

            def out_ps(self, h):
                return ps[self.rows(h), self.out_bank(h), :]

        ATT1 = Attention(0, H1)
        ATT2 = [Attention(H1 + 4 * g, 4, g, narrow=g < 3) for g in range(H2 // 4)]

        def att2_head(n):
            return ATT2[n // 4], n % 4

        def ret_score(j):
            b, at = {0: (4, 0), 1: (5, 0), 3: (5, 384), 2: (6, 0)}[j]
            return ps[:, b, at:at + 512 - 128 * j]

        def ret_v(ap, j, d):
            at = (j % 2) * 256 + (d % 2) * P
            return ap[:, 4 + 2 * (d // 2) + j // 2, at:at + P]

        @block.sync
        def _(sp):
            def load(c, src, k):
                if not c.early:
                    sp.wait_ge(s["w_lo_ready"], c.number - 1)
                cols = src.shape[-1]
                dst = raw[:, c.slot, 0:k * cols].rearrange("p (k c) -> p k c", k=k)
                sp.dma_start(dst, src).then_inc(raw_ready[c.slot], 16)

            w_in = T["w_in"][0].rearrange("(k p) c -> p k c", p=P)
            xt = o_buf[:, :, :].rearrange("p (t h) s -> p t (h s)", t=4)
            sp.dma_start(ident[:, :], T["c_ident"]).then_inc(s["ident_in"], 16)
            name, n = GAIN_ROWS[0]
            sp.dma_start(aux[0:n, 1, 0:P], gain_rows(name)).then_inc(s["rows0_in"], 16)
            load(MIX.chunk(0), w_in[:, :, 0:256], KD)
            for half in range(2):
                at = slice(half * 512, half * 512 + 512)
                for t in range(4):
                    sp.dma_start(xt[:, t, at], T["x"][0, t * P:(t + 1) * P, at]).then_inc(s[f"x_in{half}"], 16)
            load(MIX.chunk(1), w_in[:, :, 256:512], KD)
            for name, n in GAIN_ROWS[1:]:
                at = GAIN_AT[name]
                sp.dma_start(aux[at:at + n, 1, 0:P], gain_rows(name)).then_inc(s["rows_in"], 16)
            for half in range(2):
                for n, part in enumerate((1, 2, 0)):
                    at = CONV0 + part * CONV + half * 256
                    load(MIX.chunk(2 + 3 * half + n), w_in[:, :, at:at + 256], KD)
                    if half == 0 and n == 1:
                        sp.wait_ge(s["gains_t"], 2)
                        sp.dma_start(aux[:, 1, :], T["c_causal"]).then_inc(s["mask_in"], 16)
            load(UKV.chunk(0), T["w_ukv"][0].rearrange("(k p) c -> p k c", p=P), 2)
            load(UQ.chunk(0), T["w_uq"][0].rearrange("(k p) c -> p k c", p=P), 2)
            w_out = T["w_out"][0].rearrange("(k p) (m c) -> m p k c", p=P, c=256)
            for m in range(2):
                load(WOUT.chunk(m), w_out[m], KD)
            sp.wait_ge(s["conv_out"], 4)
            sp.dma_start(aux[:, 2:4, :].rearrange("p a (b c) -> p (a b) c", b=2),
                         T["p"][0, 0].rearrange("(t p) c -> p t c", p=P)).then_inc(s["p_in"], 16)
            spread_heads(sp, 0, hn_hi, hid_hi, s["q_rope_in"])
            spread_heads(sp, 1, hn_hi, hid_hi, s["q_rope_in"])
            spread_heads(sp, 1, hn_lo, hid_lo, s["q_rope_in"])
            sp.dma_start(tab[:, :, :], T["c_ret_rope"]).then_inc(s["ret_tab_in"], 16)
            for m in range(2, 4):
                load(WOUT.chunk(m), w_out[m], KD)
            load(PROJ.chunk(0), T["w_ple_proj"][0].rearrange("(k p) c -> p k c", p=P), 2)

            w_gate = T["w_gate"][0].rearrange("(k p) (m c) -> m p k c", p=P, c=256)
            w_up = T["w_up"][0].rearrange("(k p) (m c) -> m p k c", p=P, c=256)

            def load_ffn(ph, i, g, pairs):
                for j in range(pairs):
                    load(ph.chunk(2 * j, i), w_gate[g * 4 + j], KD)
                    load(ph.chunk(2 * j + 1, i), w_up[g * 4 + j], KD)

            down = T["w_down"][0, 0:2048, :].rearrange("(g k p) (m c) -> g m p k c", p=P, k=8, c=256)
            with sp.Fori(0, 2) as i:
                load_ffn(FFN, i, i, 4)
                for m in range(4):
                    load(FFN.chunk(8 + m, i), down[i, m], 8)
            load_ffn(FFN_LAST, 0, 2, 3)
            down = T["w_down"][0, 2048:D_FF, :].rearrange("(k p) (m c) -> m p k c", p=P, c=256)
            for m in range(4):
                load(FFN_LAST.chunk(6 + m), down[m], 6)
            pg = T["w_ple_gate"][0].rearrange("(k p) (m c) -> m p k c", p=P, c=256)
            for m in range(4):
                load(GATE.chunk(m), pg[m], KD)

            r_in = T["ret_w_in_2"][0]
            r_qk = r_in[:, 0:2 * RQK].rearrange("(k p) (t h c) -> t h p k c", p=P, t=2, c=256)
            r_vg = r_in[:, 2 * RQK:].rearrange("(k p) (t h n c) -> t h n p k c", p=P, t=2, n=2, c=256)
            r_out = T["ret_w_out_2"][0].rearrange("(h k p) (n c) -> h n p k c", p=P, k=4, c=512)
            with sp.Fori(0, RH) as h:
                load(RET.chunk(0, h), r_qk[0, h], KD)
                load(RET.chunk(1, h), r_qk[1, h], KD)
                load(RET.chunk(2, h), r_vg[0, h, 0], KD)
                load(RET.chunk(3, h), r_vg[0, h, 1], KD)
                load(RET.chunk(4, h), r_vg[1, h, 0], KD)
                load(RET.chunk(5, h), r_vg[1, h, 1], KD)
                load(RET.chunk(6, h), r_out[h, 0], 4)
                load(RET.chunk(7, h), r_out[h, 1], 4)

            def load_mlp(ph, layer):
                w1 = T["mlp_w1_2"][layer].rearrange("(k p) (g m c) -> g m p k c", p=P, m=4, c=256)
                w2 = T["mlp_w2_2"][layer].rearrange("(g k p) (m c) -> g m p k c", p=P, k=8, c=256)
                with sp.Fori(0, MLP_GROUPS) as i:
                    for m in range(4):
                        load(ph.chunk(m, i), w1[i, m], KD)
                    for m in range(4):
                        load(ph.chunk(4 + m, i), w2[i, m], 8)

            load_mlp(MLP_A, 0)
            a_in = T["att_w_in_2"][0].rearrange("(k p) (t g c) -> t g p k c", p=P, t=3, c=256)
            a_out = T["att_w_out_2"][0].rearrange("(g k p) c -> g p k c", p=P, k=2)

            def load_bias(n):
                if n >= 4:
                    sp.wait_ge(s["att_mx"], (H1 + n - 3) * 4)
                for q0, width in ((0, 448), (64, 512)):
                    rows = ext_rows[n].rearrange("q e -> (q e)")[0:P * (EXT - 1)].rearrange("(q e) -> q e", e=EXT - 1)
                    sp.dma_start(aux[q0:q0 + 64, n % 4, 0:width], rows[q0:q0 + 64, 127:127 + width])\
                        .then_inc(s[f"bias_in{n % 4}"], 16)

            for j, (kind, g) in enumerate(ATT_ORDER):
                load(ATT.chunk(j), a_out[g] if kind == "o" else a_in["qkv".index(kind), g], 2 if kind == "o" else KD)
                if j == 1:
                    sp.wait_ge(s["ext_out"], 16)
                    sp.wait_ge(s["mask_set"], 4)
                    for n in range(4):
                        load_bias(n)
                if 6 <= j < 15:
                    load_bias(j - 2)
            for n in range(13, H2):
                load_bias(n)
            load_mlp(MLP_B, 1)

            for half in range(2):
                sp.wait_ge(s["fin_copied"], 4 * half + 4)
                cols = slice(half * D // 2, half * D // 2 + D // 2)
                sp.dma_start(out[0, :, cols].rearrange("(t p) c -> p t c", p=P), xt[:, :, cols])\
                    .then_inc(s["out_done"], 16)
            sp.wait_ge(s["out_done"], 32)

        @block.gpsimd
        def _(pool):
            pool.memset(ones[:, :], 1.0).then_inc(s["memset_done"], 1)
            pool.memset(eps[:, :], EPS).then_inc(s["memset_done"], 1)
            pool.dma_start(tab[:, 0, :].bitcast(I32), bass.AP(T["positions"].tensor, 0, [[0, P], [1, S]]))\
                .then_inc(s["pos_in"], 16)
            pool.dma_start(freq[:, :], T["c_freq"]).then_inc(s["freq_in"], 16)
            kr_raw = aux[:, 0, :].rearrange("p (k c) -> p k c", k=KD)
            w_in = T["w_in"][0].rearrange("(k p) c -> p k c", p=P)
            at = Q_RANK + KV_RANK
            for dst, src, n in ((0, 0, 32), (32, 16, 16), (48, 0, 16)):
                pool.dma_start(kr_raw[:, :, dst:dst + n], w_in[:, :, at + src:at + src + n])\
                    .then_inc(s["kr_in"], 16)
            pool.dma_start(ext[:, 255:255 + REL_TABLE], T["att_rel_bias_2"][0]).then_inc(s["ext_in"], 16)

            def lo(number, slot):
                pool.wait_ge(s["w_hi_ready"], number + 1)
                for n in range(4):
                    at = slice(n * 512, n * 512 + 512)
                    ins = pool.tensor_tensor(w_lo[:, slot, at], raw[:, slot, at], w_hi[:, slot, at].bitcast(F32),
                                             ALU.subtract)
                ins.then_inc(s["w_lo_ready"], 1)

            for c in range(UKV.chunk0):
                lo(c, c % 2)
            for ph, parts in ((UKV, ukv_parts()), (UQ, uq_parts())):
                pool.wait_ge(s["w_hi_ready"], ph.chunk0 + 1)
                for w_lo_part, w_hi_part, raw_part in parts:
                    ins = pool.tensor_tensor(w_lo_part, raw_part, w_hi_part.bitcast(F32), ALU.subtract)
                ins.then_inc(s["w_lo_ready"], 1)
            lo(WOUT.chunk0, WOUT.chunk0 % 2)
            spread_heads(pool, 0, hn_lo, hid_lo, s["q_rope_lo_in"])
            first = WOUT.chunk0 + 1
            loops = (N_CHUNKS - first) // 2
            with pool.Fori(0, loops) as i:
                lo(first + 2 * i, first % 2)
                lo(first + 1 + 2 * i, (first + 1) % 2)
            for c in range(first + 2 * loops, N_CHUNKS):
                lo(c, c % 2)

        @block.tensor
        def _(pe):
            def chunk_ready(c):
                pe.wait_ge(s["w_lo_ready"], c.number + 1)

            def three(o, hi, lo, rhs_hi, rhs_lo, start, stop):
                pe.matmul(o, hi, rhs_hi, start=start, stop=False, skip_group_check=True)
                pe.matmul(o, hi, rhs_lo, start=False, stop=False, skip_group_check=True)
                return pe.matmul(o, lo, rhs_hi, start=False, stop=stop, skip_group_check=True)

            def group_empty(g):
                if not g.virgin:
                    pe.wait_ge(pair_free[g.pair], g.empty)

            def product(c, g, kt, cols, m0, act_hi, act_lo, act_wait=None, ks=None, start=True, stop=True):
                hi = w_hi[:, c.slot, 0:kt * cols].rearrange("p (k c) -> p k c", k=kt)
                lo = w_lo[:, c.slot, 0:kt * cols].rearrange("p (k c) -> p k c", k=kt)
                ks = ks or range(kt)
                if start:
                    group_empty(g)
                for k in ks:
                    if act_wait is not None:
                        act_wait(k)
                    for m in range(2):
                        at = slice((m0 + m) * P, (m0 + m) * P + P)
                        ins = three(ps[:, g.bank(m), :], hi[:, k, at], lo[:, k, at],
                                    act_hi[:, k, :], act_lo[:, k, :], start and k == ks[0], stop and k == ks[-1])
                if stop:
                    ins.then_inc(s["group_done"], 1)

            def normed(norm):
                return lambda k: pe.wait_ge(s["norm_lo"], norm.out0 + k + 1)

            def stat(norm):
                pe.wait_ge(s["norm_acc"], norm.acc0 + norm.n - 1)
                if norm.index:
                    pe.wait_ge(s["norm_ln"], norm.index)
                pe.matmul(ps[:, 7, :], ones[:, :], ssq, start=True, stop=True).then_inc(s["norm_stat"], 1)

            def stat_columns(norm):
                pe.wait_ge(s["norm_acc"], norm.acc0 + norm.n - 1)
                for t in range(4):
                    ins = pe.matmul(ps[:, 6, t:t + 1], ssq[:, t * P:(t + 1) * P], ones[:, 0:1], start=True, stop=True)
                ins.then_inc(s["col_stat"], 1)

            def stat_at(norm, at):
                return lambda k: stat(norm) if k == at else None

            pe.wait_ge(s["ident_in"], 16)
            pe.wait_ge(s["rows0_in"], 16)
            n0 = GAIN_ROWS[0][1]
            pe.transpose(ps[:, 6, 0:n0], aux[0:n0, 1, 0:P], ident[0:n0, 0:n0]).then_inc(s["gains_t"], 1)
            xt = o_buf[:, :, :].rearrange("p (t h) s -> p t (h s)", t=4)
            pe.wait_ge(s["gains_ready"], 1)

            def transpose_x(f):
                if f % 4 == 0:
                    pe.wait_ge(s[f"x_in{f // 4}"], 64)
                if f >= 4:
                    pe.wait_ge(s["x_copied"], f - 3)
                for t in range(4):
                    ins = pe.transpose(ps[:, 4 + f % 4, t * P:(t + 1) * P], xt[:, t, f * P:(f + 1) * P],
                                       ident[:, :])
                ins.then_inc(s["x_t"], 1)

            def next_x(k):
                if k + 3 < KD:
                    transpose_x(k + 3)
                pe.wait_ge(s["norm_lo"], N_MIX.out0 + k + 1)

            for f in range(3):
                transpose_x(f)
            chunk_ready(MIX.chunk(0))
            product(MIX.chunk(0), MIX.group(0), KD, 256, 0, hn_hi, hn_lo, next_x)
            pe.wait_ge(s["memset_done"], 2)
            stat(N_MIX)
            pe.wait_ge(s["rows_in"], 16 * (len(GAIN_ROWS) - 1))
            pe.transpose(ps[:, 6, 0:N_GAINS], aux[0:N_GAINS, 1, 0:P], ident[0:N_GAINS, 0:N_GAINS])\
                .then_inc(s["gains_t"], 1)
            chunk_ready(MIX.chunk(1))
            product(MIX.chunk(1), MIX.group(1), KD, 256, 0, hn_hi, hn_lo)
            pe.wait_ge(s["kr_lo"], 1)
            for k in range(KD):
                ins = three(ps[:, 4, :], hid_hi[:, 4 + k // 4, (k % 4) * P:(k % 4) * P + P],
                            hid_lo[:, 4 + k // 4, (k % 4) * P:(k % 4) * P + P],
                            hn_hi[:, k, :], hn_lo[:, k, :], k == 0, k == KD - 1)
            ins.then_inc(s["kr_done"], 1)
            for n in range(2, 8):
                chunk_ready(MIX.chunk(n))
                product(MIX.chunk(n), MIX.group(n), KD, 256, 0, hn_hi, hn_lo)
                if n == 2:
                    stat(N_Q)
                if n == 3:
                    stat(N_KV)
            c = UKV.chunk(0)
            chunk_ready(c)
            hi = w_hi[:, c.slot, :].rearrange("p (k t c) -> p k t c", k=2, t=2)
            lo = w_lo[:, c.slot, :].rearrange("p (k t c) -> p k t c", k=2, t=2)
            pe.wait_ge(s["norm_lo"], N_KV.out0 + 2)
            for n in range(2):
                g = UKV.group(n)
                group_empty(g)
                for m in range(2):
                    heads = slice((2 * n + m) * P, (2 * n + m) * P + P)
                    for k in range(2):
                        ins = three(ps[:, g.bank(m), :], hi[:, k, 0, heads], lo[:, k, 0, heads],
                                    hid_hi[:, 2 + k, :], hid_lo[:, 2 + k, :], k == 0, k == 1)
                ins.then_inc(s["group_done"], 1)
            for n in range(2):
                g = UKV.group(2 + n)
                group_empty(g)
                for m in range(2):
                    t = slice((2 * n + m) * P, (2 * n + m) * P + P)
                    for k in range(2):
                        ins = three(ps[:, g.bank(m), :], hid_hi[:, 2 + k, t], hid_lo[:, 2 + k, t],
                                    hi[:, k, 1, :], lo[:, k, 1, :], k == 0, k == 1)
                ins.then_inc(s["group_done"], 1)
            c = UQ.chunk(0)
            chunk_ready(c)
            hi = w_hi[:, c.slot, :].rearrange("p (k c) -> p k c", k=2)
            lo = w_lo[:, c.slot, :].rearrange("p (k c) -> p k c", k=2)
            pe.wait_ge(s["norm_lo"], N_Q.out0 + 2)
            for n, tiles in enumerate(((4, 6), (5, 7), (0, 1), (2, 3))):
                g = UQ.group(n)
                group_empty(g)
                for m, tile in enumerate(tiles):
                    at = slice(tile * P, tile * P + P)
                    for k in range(2):
                        ins = three(ps[:, g.bank(m), :], hi[:, k, at], lo[:, k, at],
                                    hid_hi[:, k, :], hid_lo[:, k, :], k == 0, k == 1)
                ins.then_inc(s["group_done"], 1)
                if n == 0:
                    stat(N_CONVG)

            def scores(a, h):
                if a.block2 and h == 0:
                    pe.wait_ge(s["att_in_lo"], a.group * 4 + 4)
                if not a.block2:
                    g = UQ.group(2 + h // 4)
                    pe.wait_ge(pair_free[g.pair], g.freed(h % 4 // 2))
                for t, bank_read in Q_ORDER:
                    if not a.first(h):
                        pe.wait_ge(s["att_mx"], a.n(h) * 4 - 4 + bank_read)
                    for n, (q, k) in enumerate(a.qk(h)):
                        ins = pe.matmul(a.score_ps(t), q[:, t * P:(t + 1) * P], k[:, 0:(t + 1) * P],
                                        start=(n == 0), stop=(n == 2), skip_group_check=True)
                    ins.then_inc(s["att_s"], 1)

            def transposes(a, h):
                pe.wait_ge(s["att_p"], a.n(h) * 4 + 4)
                for j, bank_read in K_ORDER:
                    if not a.first(h):
                        pe.wait_ge(s["att_lo"], a.n(h) * 4 - 4 + bank_read)
                    for t in range(j, 4):
                        ins = pe.transpose(a.trans_ps(j)[:, (t - j) * P:(t - j + 1) * P],
                                           a.score_sb(h, t)[:, j * P:(j + 1) * P], ident[:, :])
                    ins.then_inc(s["att_t"], 1)

            def values(a, h):
                if a.narrow:
                    pe.wait_ge(s["att_o"], a.n(h))
                elif h >= 2 or a.block2:
                    pe.wait_ge(s["att_o"], a.n(h) - 1)
                if a.block2 and h == 0:
                    g = ATT.group(ATT.upto[ATT_ORDER.index(("v", a.group))])
                    pe.wait_ge(pair_free[g.pair], g.freed(1))
                for n, (j, _) in enumerate(K_ORDER):
                    pe.wait_ge(s["att_lo"], a.n(h) * 4 + n + 1)
                    ins = three(ps[:, a.out_bank(h), j * P:], a.v(hid_hi, h, j), a.v(hid_lo, h, j),
                                a.pt(0, j), a.pt(1, j), n == 0, n == 3)
                ins.then_inc(s["att_pv"], 1)

            def attend(a, between=None):
                scores(a, 0)
                scores(a, 1)
                if between:
                    between()
                transposes(a, 0)
                for h in range(a.heads):
                    if h + 2 < a.heads:
                        scores(a, h + 2)
                    values(a, h)
                    if h + 1 < a.heads:
                        transposes(a, h + 1)

            for n in (2, 3):
                pe.wait_ge(pair_free[n % 2], UKV.group(n).freed(1))
            pe.wait_ge(s["krep_done"], 32)
            pe.wait_ge(s["q_rope_in"], 12 * 16)
            pe.wait_ge(s["q_rope_lo_in"], 4 * 16)
            for n in (2, 3):
                pe.wait_ge(pair_free[n % 2], UQ.group(n).freed(1))
            attend(ATT1)
            for m in range(2):
                chunk_ready(WOUT.chunk(m))

                def conv_wait(k):
                    if m == 0:
                        pe.wait_ge(s["norm_lo"], N_CONVG.out0 + k - 3)
                    elif k == 6:
                        stat(N_ATTG)
                product(WOUT.chunk(m), WOUT.group(m), KD, 256, 0, hn_hi, hn_lo, conv_wait, range(4, 8), stop=False)
            for m in range(2):
                product(WOUT.chunk(m), WOUT.group(m), KD, 256, 0, hn_hi, hn_lo,
                        (lambda k: pe.wait_ge(s["norm_lo"], N_ATTG.out0 + k + 1)) if m == 0 else None,
                        range(4), start=False)
            pe.wait_ge(s["p_in"], 16)
            pt = aux[:, 2:4, :].rearrange("p a (b c) -> p (a b) c", b=2)
            for f in range(2):
                for t in range(4):
                    ins = pe.transpose(ps[:, 4 + f, t * P:(t + 1) * P], pt[:, t, f * P:(f + 1) * P], ident[:, :])
                ins.then_inc(s["p_t"], 1)
            for m in range(2, 4):
                chunk_ready(WOUT.chunk(m))
                product(WOUT.chunk(m), WOUT.group(m), KD, 256, 0, hn_hi, hn_lo)
            c = PROJ.chunk(0)
            chunk_ready(c)
            pe.wait_ge(s["p_lo"], 2)
            for n in range(4):
                product(c, PROJ.group(n), 2, 1024, 2 * n, hid_hi[:, 0:2, :], hid_lo[:, 0:2, :])
                if n == 0:
                    stat(N_POST)

            def ffn(ph, i, g_hid, kt, first=False):
                for j in range(kt // 2):
                    for n in range(2):
                        chunk_ready(ph.chunk(2 * j + n, i))
                        product(ph.chunk(2 * j + n, i), ph.group(2 * j + n, i), KD, 256, 0, hn_hi, hn_lo,
                                (normed(N_FFN), stat_at(N_FFN, 3))[n] if first and j == 0 else None)
                        if ph is FFN and not first and j == 0 and n == 0:
                            stat(N_PLE)
                for m in range(4):
                    c = ph.chunk(kt + m, i)
                    chunk_ready(c)
                    product(c, ph.group(kt + m, i), kt, 256, 0, hid_hi, hid_lo,
                            (lambda k: pe.wait_ge(s["ffn_lo"], g_hid + k + 1)) if m == 0 else None)

            ffn(FFN, 0, 0, 8, first=True)
            ffn(FFN, 1, 8, 8)
            ffn(FFN_LAST, 0, 16, 6)
            stat(N_FPOST)
            for m in range(4):
                chunk_ready(GATE.chunk(m))
                product(GATE.chunk(m), GATE.group(m), KD, 256, 0, hn_hi, hn_lo,
                        (lambda k: pe.wait_ge(s["ple_xlo"], k + 1)) if m == 0 else None)


            def token_major(c, g, halfway=None):
                hi = w_hi[:, c.slot, :].rearrange("p (k c) -> p k c", k=KD)
                lo = w_lo[:, c.slot, :].rearrange("p (k c) -> p k c", k=KD)
                group_empty(g)
                for t in range(4):
                    if t == 2 and halfway:
                        halfway()
                    o = ps[:, g.bank(t // 2), (t % 2) * 256:(t % 2) * 256 + 256]
                    for k in range(KD):
                        at = slice(t * P, t * P + P)
                        ins = three(o, hn_hi[:, k, at], hn_lo[:, k, at], hi[:, k, :], lo[:, k, :],
                                    k == 0, k == KD - 1)
                ins.then_inc(s["group_done"], 1)

            def sum_hook(h):
                def hook(k):
                    if k == 2:
                        pe.wait_ge(s["ret_sum"], h * 3 + 3)
                        pe.matmul(ps[:, 4, :], ones[:, :], ssq, start=True, stop=True).then_inc(s["ret_mean"], 1)
                    if k == 7:
                        pe.wait_ge(s["ret_acc"], h * 3 + 3)
                        pe.matmul(ps[:, 5, :], ones[:, :], ssq, start=True, stop=True).then_inc(s["ret_var"], 1)
                return hook

            def head(h, first=False):
                for n in range(2):
                    chunk_ready(RET.chunk(n, h))
                    product(RET.chunk(n, h), RET.group(n, h), KD, 256, 0, hn_hi, hn_lo,
                            normed(N_RET) if first and n == 0 else None)
                    if first and n == 0:
                        stat_columns(N_RET)
                        stat(N_RET)
                chunk_ready(RET.chunk(2, h))
                token_major(RET.chunk(2, h), RET.group(2, h))
                pe.wait_ge(s["ret_qk_lo"], h * 4 + 4)
                for j, _ in K_ORDER:
                    o = ret_score(j)
                    for k in range(2):
                        at = slice(j * P, j * P + P)
                        ins = three(o, hid_hi[:, 2 + k, at], hid_lo[:, 2 + k, at],
                                    hid_hi[:, k, j * P:], hid_lo[:, k, j * P:], k == 0, k == 1)
                    ins.then_inc(s["ret_s"], 1)
                chunk_ready(RET.chunk(3, h))
                token_major(RET.chunk(3, h), RET.group(3, h))
                pe.wait_ge(s["ret_s_lo"], h * 4 + 4)
                for d in range(4):
                    if d % 2 == 0:
                        g = RET.group(2 + d // 2, h)
                        pe.wait_ge(pair_free[g.pair], g.freed(1))
                    for j in range(4):
                        ins = three(ps[:, 4 + d, j * P:], ret_v(hid_hi, j, d), ret_v(hid_lo, j, d),
                                    hid_hi[:, 8 + j, j * P:], hid_lo[:, 8 + j, j * P:], j == 0, j == 3)
                    ins.then_inc(s["ret_pv"], 1)
                for n in (4, 5):
                    chunk_ready(RET.chunk(n, h))
                    product(RET.chunk(n, h), RET.group(n, h), KD, 256, 0, hn_hi, hn_lo,
                            sum_hook(h) if n == 4 else None)
                for n in range(4):
                    c = RET.chunk(6 + n // 2, h)
                    if n % 2 == 0:
                        chunk_ready(c)
                    product(c, RET.group(6 + n, h), 4, 512, 2 * (n % 2), hid_hi[:, 12:16, :],
                            hid_lo[:, 12:16, :],
                            (lambda k: pe.wait_ge(s["ret_y_lo"], h * 4 + k + 1)) if n == 0 else None)

            head(0, first=True)
            with pe.Fori(1, RH) as h:
                head(h)

            def mlp(ph, norm, base):
                def body(i, first=False):
                    for m in range(4):
                        chunk_ready(ph.chunk(m, i))
                        product(ph.chunk(m, i), ph.group(m, i), KD, 256, 0, hn_hi, hn_lo,
                                normed(norm) if first and m == 0 else None)
                        if first and m == 0:
                            stat(norm)
                    for m in range(4):
                        chunk_ready(ph.chunk(4 + m, i))
                        product(ph.chunk(4 + m, i), ph.group(4 + m, i), 8, 256, 0, hid_hi, hid_lo,
                                (lambda k: pe.wait_ge(s["mlp_lo"], base + i * 8 + k + 1)) if m == 0 else None)

                body(0, first=True)
                with pe.Fori(1, MLP_GROUPS) as i:
                    body(i)

            mlp(MLP_A, N_MLPA, 0)

            def att_product(j, halfway=None, act_wait=None):
                kind, four = ATT_ORDER[j]
                c, g = ATT.chunk(j), ATT.group(ATT.upto[j])
                chunk_ready(c)
                if kind == "v":
                    token_major(c, g, halfway)
                elif kind == "o":
                    pe.wait_ge(s["att_o"], ATT2[four].n(3) + 1)
                    for n in range(4):
                        if n == 2 and halfway:
                            halfway()
                        out = slice(ATT2[four].slot + 6, ATT2[four].slot + 8)
                        product(c, ATT.group(ATT.upto[j] + n), 2, 1024, 2 * n, hid_hi[:, out, :], hid_lo[:, out, :])
                else:
                    product(c, g, KD, 256, 0, hn_hi, hn_lo, act_wait or (lambda k: k == 3 and halfway and halfway()))

            att_product(0, act_wait=normed(N_ATT))
            stat_columns(N_ATT)
            stat(N_ATT)
            att_product(1)
            att_product(2, lambda: scores(*att2_head(0)))
            for n in range(12):
                transposes(*att2_head(n))

                def halfway():
                    values(*att2_head(n))
                    if n < 11:
                        scores(*att2_head(n + 1))

                if n < 11:
                    att_product(3 + n, halfway)
                else:
                    halfway()

            def while_scored():
                pe.wait_ge(s["att_mx"], ATT2[3].n(1) * 4 + 4)
                att_product(14)
                for n in (2, 3):
                    g = ATT.group(ATT.upto[14] + n)
                    pe.wait_ge(pair_free[g.pair], g.freed(1))

            for n in (2, 3):
                g = ATT.group(ATT.upto[13] + n)
                pe.wait_ge(pair_free[g.pair], g.freed(1))
            attend(ATT2[3], while_scored)
            att_product(15)
            mlp(MLP_B, N_MLPB, MLP_GROUPS * 8)
            stat(N_FINAL)
            for f in range(KD):
                pe.wait_ge(s["fin_tmp"], f + 1)
                for t in range(4):
                    ins = pe.transpose(ps[:, f, t * P:(t + 1) * P], normed_x[:, f, t * P:(t + 1) * P], ident[:, :])
                ins.then_inc(s["fin_t"], 1)

        @block.scalar
        def _(act):
            def split(c):
                act.wait_ge(raw_ready[c.slot], c.loads)
                if not c.early:
                    act.wait_ge(s["group_done"], c.two_before)
                act.activation(w_hi[:, c.slot, :], raw[:, c.slot, :], ACT.Copy).then_inc(s["w_hi_ready"], 1)

            def group_ready(g):
                act.wait_ge(s["group_done"], g.done)

            def copy_out(g, m, dst, func=ACT.Copy):
                act.activation(dst, ps[:, g.bank(m), :], func).then_inc(pair_free[g.pair], 1)

            def square(norm, t, src, into=sq):
                if t == 0:
                    if norm.index:
                        act.wait_ge(s["norm_stat"], norm.index)
                    act.activation(ssq, src, ACT.Square).then_inc(s["norm_sq"], 1)
                else:
                    used = norm.acc0 + max(0, t - 2)
                    if used:
                        act.wait_ge(s["norm_acc"], used)
                    act.activation(into[:, t % 2, :], src, ACT.Square).then_inc(s["norm_sq"], 1)

            def rsqrt_columns(nth, dim):
                act.wait_ge(s["col_stat"], nth + 1)
                act.activation(r_col[:, 0:4], ps[:, 6, 0:4], ACT.Ln, scale=1.0 / dim, bias=eps[:, 0:1])\
                    .then_inc(s["col_ln"], 1)
                act.wait_ge(s["col_ln"], nth + 1)
                act.activation(r_col[:, 0:4], r_col[:, 0:4], ACT.Exp, scale=-0.5).then_inc(s["col_r"], 1)

            def rsqrt(norm, dim, r=r_bc):
                act.wait_ge(s["norm_stat"], norm.index + 1)
                act.activation(r, ps[:, 7, :], ACT.Ln, scale=1.0 / dim, bias=eps[:, 0:1])\
                    .then_inc(s["norm_ln"], 1)
                act.wait_ge(s["norm_ln"], norm.index + 1)
                act.activation(r, r, ACT.Exp, scale=-0.5).then_inc(s["norm_r"], 1)

            def hi_tile(norm, t, dst):
                act.wait_ge(s["norm_tmp"], norm.out0 - N_MIX.split + t + 1)
                act.activation(dst, tmp[:, t % 2, :], ACT.Copy).then_inc(s["norm_hi"], 1)

            def gained_hi(norm, t, at):
                act.activation(hn_hi[:, t, :], x[:, t, :], ACT.Copy, scale=gain(*at)).then_inc(s["norm_hi"], 1)

            def gained_x(norm, adding, name, row, following):
                for t in range(KD):
                    g = adding[t // 2]
                    act.wait_ge(pair_free[g.pair], g.freed(t % 2))
                    gained_hi(norm, t, (name, row + t))
                    if t < 2:
                        square(norm, t, x[:, t, :])
                split(following)
                for t in range(2, KD):
                    square(norm, t, x[:, t, :])

            n0 = GAIN_ROWS[0][1]
            act.wait_ge(s["gains_t"], 1)
            act.activation(gains[:, 0:n0], ps[:, 6, 0:n0], ACT.Copy).then_inc(s["gains_ready"], 1)
            split(MIX.chunk(0))
            act.preload_act_table_set("natural_log_exp_and_others")
            act.wait_ge(s["gains_ready"], 1)
            for f in range(KD):
                act.wait_ge(s["x_t"], f + 1)
                act.activation(x[:, f, :], ps[:, 4 + f % 4, :], ACT.Copy).then_inc(s["x_copied"], 1)
                act.wait_ge(s["x_copied"], f + 1)
                gained_hi(N_MIX, f, ("mix_pre_norm", f))
                square(N_MIX, f, x[:, f, :])
                if f == 2:
                    split(MIX.chunk(1))
            kr_dst = hid_hi[:, 4:6, :].rearrange("p a (k c) -> p (a k) c", c=P)
            kr_raw = aux[:, 0, :].rearrange("p (k c) -> p k c", k=KD)
            act.wait_ge(s["kr_in"], 48)
            act.activation(kr_dst[:, :, 0:64], kr_raw, ACT.Copy)
            act.activation(kr_dst[:, :, 64:128], kr_raw, ACT.Copy).then_inc(s["kr_hi"], 1)
            act.wait_ge(s["memset_done"], 2)
            rsqrt(N_MIX, D, rstd[:, :])
            act.wait_ge(s["gains_t"], 2)
            act.activation(gains[:, n0:], ps[:, 6, n0:N_GAINS], ACT.Copy).then_inc(s["gains_ready"], 1)

            g = MIX.group(0)
            for m in range(2):
                act.wait_ge(pair_free[g.pair], g.freed(m))
                square(N_Q, m, o_buf[:, m, :])
            split(MIX.chunk(2))
            act.wait_ge(s["angle"], ANGLE_STEPS)
            act.activation(tab[:, 1, :], aux[:, 2, :], ACT.Sin).then_inc(s["sin_done"], 1)
            act.activation(tab[:, 0, :], aux[:, 2, :], ACT.Sin, scale=0.5).then_inc(s["sin_done"], 1)
            act.preload_act_table_set("natural_log_exp_and_others")
            split(MIX.chunk(3))
            rsqrt(N_Q, Q_RANK)
            for t in range(2):
                hi_tile(N_Q, t, hid_hi[:, t, :])
            for t in range(2):
                act.wait_ge(pair_free[MIX.group(1).pair], MIX.group(1).freed(t))
                square(N_KV, t, o_buf[:, 2 + t, :])
            split(MIX.chunk(4))
            rsqrt(N_KV, KV_RANK)
            for t in range(2):
                hi_tile(N_KV, t, hid_hi[:, 2 + t, :])
            split(MIX.chunk(5))
            act.wait_ge(s["krope"], 4)
            act.activation(hid_hi[64:96, 4, :], aux[64:96, 0, :], ACT.Copy).then_inc(s["krope_hi"], 1)
            act.wait_ge(s["krope_hi"], 1)
            act.wait_ge(s["krope_lo"], 1)
            for ap in (hid_hi[:, :, :].bitcast(F32), hid_lo[:, :, :].bitcast(F32)):
                act.dma_start(ap[64:96, 5:12, :], ap[64:96, 4:5, :].to_broadcast([32, 7, S]))\
                    .then_inc(s["krep_done"], 16)
            split(MIX.chunk(6))
            split(MIX.chunk(7))

            for c, parts in ((UKV.chunk(0), ukv_parts()), (UQ.chunk(0), uq_parts())):
                act.wait_ge(raw_ready[c.slot], c.loads)
                act.wait_ge(s["group_done"], c.two_before)
                for _w_lo, w_hi_part, raw_part in parts:
                    ins = act.activation(w_hi_part, raw_part, ACT.Copy)
                ins.then_inc(s["w_hi_ready"], 1)
            for n in range(2):
                g = UKV.group(n)
                group_ready(g)
                for m in range(2):
                    for half in range(2):
                        act.activation(hid_hi[0:NOPE, 4 + 4 * n + 2 * m + half, :],
                                       ps[64 * half:64 * half + 64, g.bank(m), :], ACT.Copy)\
                            .then_inc(s["kv_hi"], 1)
            act.wait_ge(s["conv_out"], 4)
            for t in range(4):
                square(N_CONVG, t, o_buf[:, 4 + t, :])
            for n in range(2):
                g = UKV.group(2 + n)
                group_ready(g)
                for m in range(2):
                    act.activation(hid_hi[:, 12 + 2 * n + m, :], ps[:, g.bank(m), :], ACT.Copy)\
                        .then_inc(s["kv_hi"], 1)
            split(WOUT.chunk(0))
            for r in range(2):
                act.wait_ge(s["q_rope"], r + 1)
                act.activation(hid_hi[:, 2 + r, :], tmp[:, r, :], ACT.Copy).then_inc(s["qr_hi"], 1)
            for h in range(H1):
                g = UQ.group(2 + h // 4)
                group_ready(g)
                act.activation(hn_hi[0:NOPE, h, :], ps[64 * (h % 2):64 * (h % 2) + 64, g.bank(h % 4 // 2), :],
                               ACT.Copy).then_inc(s["q_nope_hi"], 1)
            rsqrt(N_CONVG, CONV)
            split(WOUT.chunk(1))

            def exps(a, h):
                act.wait_ge(s["att_nmx"], a.n(h) + 1)
                for t in range(4):
                    col = slice(4 * (h % 2) + t, 4 * (h % 2) + t + 1)
                    act.activation(a.score_sb(h, t), a.score_sb(h, t), ACT.Exp, bias=nmx[:, col],
                                   accum_out=sm[:, col]).then_inc(s["att_exp"], 1)

            def prob_hi(a, h):
                if not a.first(h):
                    act.wait_ge(s["att_pv"], a.n(h))
                for j, done in K_ORDER:
                    act.wait_ge(s["att_t"], a.n(h) * 4 + done)
                    act.activation(a.pt(0, j), a.trans_ps(j), ACT.Copy).then_inc(s["att_hi"], 1)

            def empty_out(a, h):
                act.wait_ge(s["att_pv"], a.n(h) + 1)
                if a.block2:
                    act.activation(a.out(hid_hi, h), a.out_ps(h), ACT.Copy).then_inc(s["att_ohi"], 1)
                else:
                    act.activation(o_buf[a.rows(h), h // 2, :], a.out_ps(h), ACT.Copy).then_inc(s["att_o"], 1)

            def attend(a):
                exps(a, 0)
                exps(a, 1)
                prob_hi(a, 0)
                for h in range(a.heads):
                    empty_out(a, h)
                    if h + 1 < a.heads:
                        prob_hi(a, h + 1)
                    if h + 2 < a.heads:
                        exps(a, h + 2)

            attend(ATT1)

            for t in range(4):
                hi_tile(N_CONVG, t, hn_hi[:, 4 + t, :])
            act.wait_ge(s["att_o"], H1)
            for t in range(4):
                square(N_ATTG, t, o_buf[:, t, :])
            rsqrt(N_ATTG, CONV)
            for t in range(4):
                hi_tile(N_ATTG, t, hn_hi[:, t, :])

            def copy_e(n):
                g = PROJ.group(n)
                group_ready(g)
                for m in range(2):
                    copy_out(g, m, e_buf[:, 2 * n + m, :])

            for m, following in enumerate((WOUT.chunk(2), WOUT.chunk(3), PROJ.chunk(0), None)):
                g = WOUT.group(m)
                group_ready(g)
                if following:
                    split(following)
                for t in range(2):
                    square(N_POST, 2 * m + t, ps[:, g.bank(t), :])
                for t in range(2):
                    copy_out(g, t, o_buf[:, 2 * m + t, :])
                if m == 1:
                    for f in range(2):
                        act.wait_ge(s["p_t"], f + 1)
                        act.activation(hid_hi[:, f, :], ps[:, 4 + f, :], ACT.Copy).then_inc(s["p_hi"], 1)
            copy_e(0)
            rsqrt(N_POST, D)
            split(FFN.chunk(0))
            copy_e(1)
            for t in range(KD):
                act.wait_ge(s["post_x"], 2 * t + 2)
                gained_hi(N_FFN, t, ("ffn_pre_norm", t))
                if t < 2:
                    square(N_FFN, t, x[:, t, :])
                if t in (1, 3):
                    copy_e(2 + t // 2)
                if t == 4:
                    split(FFN.chunk(1))

            for t in range(2, KD):
                square(N_FFN, t, x[:, t, :])

            def gate_up(ph, i, g_hid, pairs, first=False):
                for j in range(pairs):
                    gate, up = ph.group(2 * j, i), ph.group(2 * j + 1, i)
                    if ph is FFN and j == 0:
                        if not first:
                            act.preload_act_table_set("natural_log_exp_and_others")
                        if first:
                            split(ph.chunk(2))
                            rsqrt(N_FFN, D)
                            act.wait_ge(s["ext_built"], 3)
                            act.dma_start(ext_rows, ext[:, :].unsqueeze(1).to_broadcast([H2, P, EXT]))\
                                .then_inc(s["ext_out"], 16)
                        else:
                            rsqrt(N_PLE, D, rstd[:, :])
                        act.preload_act_table_set("silu_and_others")
                    for m in range(2):
                        act.wait_ge(pair_free[gate.pair], gate.freed(m))
                        act.activation(sq[:, m, :], sq[:, m, :], ACT.Silu).then_inc(s["ffn_silu"], 1)
                    if j or not first:
                        split(ph.chunk(2 * j + 2, i))
                    group_ready(up)
                    split(ph.chunk(2 * j + 3, i))
                    for m in range(2):
                        act.wait_ge(s["ffn_part"], g_hid + 2 * j + m + 1)
                        act.activation(hid_hi[:, 2 * j + m, :], tmp[:, m, :], ACT.Copy).then_inc(s["ffn_hi"], 1)

            for i in range(2):
                gate_up(FFN, i, i * 8, 4, first=i == 0)
                for m in range(4):
                    split(FFN.chunk(10 + m, i))
                    if i == 0:
                        for t in (2 * m, 2 * m + 1):
                            square(N_PLE, t, e_buf[:, t, :], aux[:, 0:2, :])
            gate_up(FFN_LAST, 0, 16, 3)
            act.preload_act_table_set("natural_log_exp_and_others")
            for m in range(4):
                g = FFN_LAST.group(6 + m)
                group_ready(g)
                if m < 3:
                    split(FFN_LAST.chunk(8 + m))
                for t in range(2):
                    act.wait_ge(pair_free[g.pair], g.freed(t))
                    square(N_FPOST, 2 * m + t, o_buf[:, 2 * m + t, :])
            split(FFN_LAST.chunk(11))
            rsqrt(N_FPOST, D)

            for t in range(KD):
                act.wait_ge(s["ple_x"], 2 * t + 2)
                act.activation(hn_hi[:, t, :], x[:, t, :], ACT.Copy).then_inc(s["ple_xhi"], 1)
            act.preload_act_table_set("sigmoid_and_others")
            for m in range(4):
                g = GATE.group(m)
                group_ready(g)
                if m < 3:
                    split(GATE.chunk(m + 2))
                if m == 3:
                    for t in range(2):
                        gained_hi(N_RET, t, ("mix_norm_g_2", t))
                for t in range(2):
                    if m:
                        act.wait_ge(s["ple_e"], 2 * (2 * m + t) - 3)
                    copy_out(g, t, aux[:, 2 + t, :], ACT.Sigmoid)
                if m == 3:
                    for t in range(2, 6):
                        gained_hi(N_RET, t, ("mix_norm_g_2", t))
                    split(GATE.chunk(5))
                for t in range(2):
                    act.wait_ge(s["ple_e"], 2 * (2 * m + t + 1))
                    if m == 3:
                        gained_hi(N_RET, 6 + t, ("mix_norm_g_2", 6 + t))
                    square(N_RET, 2 * m + t, x[:, 2 * m + t, :])
            act.dma_start(aux[:, :, :], T["c_decay"]).then_inc(s["decay_in"], 16)
            act.preload_act_table_set("natural_log_exp_and_others")

            def tokens_hi(g, slot, sem):
                group_ready(g)
                for t in range(4):
                    half = slice((t % 2) * 256, (t % 2) * 256 + 256)
                    act.activation(hid_hi[:, slot + t // 2, half], ps[:, g.bank(t // 2), half], ACT.Copy,
                                   scale=r_col[:, t:t + 1]).then_inc(sem, 1)

            def head(h, first=False):
                if not first:
                    split(RET.chunk(1, h))
                for n in range(2):
                    if first and n == 0:
                        rsqrt_columns(0, D)
                        rsqrt(N_RET, D)
                    group_ready(RET.group(n, h))
                    split(RET.chunk(n + 2, h))
                    for t in range(2):
                        act.wait_ge(s["ret_tmp"], h * 4 + 2 * n + t + 1)
                        act.activation(hid_hi[:, 2 * n + t, :], tmp[:, t, :], ACT.Copy)\
                            .then_inc(s["ret_qk_hi"], 1)
                act.wait_ge(s["col_r"], 1)
                group_ready(RET.group(2, h))
                split(RET.chunk(4, h))
                tokens_hi(RET.group(2, h), 4, s["ret_v_hi"])
                for n, (j, _) in enumerate(K_ORDER):
                    act.wait_ge(s["ret_sd"], h * 4 + n + 1)
                    act.activation(hid_hi[:, 8 + j, j * P:], o_buf[:, j, j * P:], ACT.Copy)\
                        .then_inc(s["ret_s_hi"], 1)
                group_ready(RET.group(3, h))
                tokens_hi(RET.group(3, h), 6, s["ret_v_hi"])
                act.wait_ge(s["ret_s_lo"], h * 4 + 4)
                for d in range(4):
                    act.wait_ge(s["ret_pv"], h * 4 + d + 1)
                    act.activation(o_buf[:, d, :], ps[:, 4 + d, :], ACT.Copy).then_inc(s["ret_o"], 1)
                split(RET.chunk(5, h))
                for t in range(4):
                    act.wait_ge(s["ret_d"], h * 4 + t + 1)
                    if t == 3:
                        act.wait_ge(s["ret_acc"], h * 3 + 1)
                    act.activation(sq[:, t % 2, :] if t else ssq, o_buf[:, t, :], ACT.Square)\
                        .then_inc(s["ret_sq"], 1)
                act.wait_ge(s["ret_var"], h + 1)
                act.activation(rstd[:, :], ps[:, 5, :], ACT.Ln, scale=1.0 / RDV, bias=eps[:, 0:1])\
                    .then_inc(s["ret_ln"], 1)
                act.wait_ge(s["ret_ln"], h + 1)
                act.activation(rstd[:, :], rstd[:, :], ACT.Exp, scale=-0.5).then_inc(s["ret_rstd"], 1)
                act.preload_act_table_set("silu_and_others")
                for n in range(2):
                    g = RET.group(4 + n, h)
                    group_ready(g)
                    if n == 0:
                        split(RET.chunk(6, h))
                    for m in range(2):
                        act.wait_ge(pair_free[g.pair], g.freed(m))
                        act.activation(o_buf[:, 4 + 2 * n + m, :], o_buf[:, 4 + 2 * n + m, :], ACT.Silu)\
                            .then_inc(s["ret_gate"], 1)
                    for t in (2 * n, 2 * n + 1):
                        act.wait_ge(s["ret_y"], h * 4 + t + 1)
                        act.activation(hid_hi[:, 12 + t, :], o_buf[:, t, :], ACT.Copy).then_inc(s["ret_y_hi"], 1)
                act.preload_act_table_set("natural_log_exp_and_others")
                split(RET.chunk(7, h))
                split(RET.chunk(8, h))

            head(0, first=True)
            with act.Fori(1, RH) as h:
                head(h)

            def mlp(ph, norm, base, next_norm, next_gain):
                def up(i, first=False):
                    for m in range(4):
                        if first and m == 0:
                            rsqrt(norm, D)
                        g = ph.group(m, i)
                        group_ready(g)
                        split(ph.chunk(m + 2, i))
                        if m:
                            act.wait_ge(s["mlp_lo"], base + i * 8 + 2 * m)
                        for t in range(2):
                            act.wait_ge(pair_free[g.pair], g.freed(t))
                            act.activation(tmp[:, t, :], sq[:, t, :], ACT.Square).then_inc(s["mlp_sq"], 1)
                        for t in range(2):
                            act.wait_ge(s["mlp_sq"], base + i * 8 + 2 * m + t + 1)
                            act.activation(hid_hi[:, 2 * m + t, :], tmp[:, t, :], ACT.Copy)\
                                .then_inc(s["mlp_hi"], 1)

                def down_splits(i):
                    for m in range(4):
                        split(ph.chunk(6 + m, i))

                up(0, first=True)
                down_splits(0)
                with act.Fori(1, MLP_GROUPS - 1) as i:
                    up(i)
                    down_splits(i)
                i = MLP_GROUPS - 1
                up(i)
                for m in range(4):
                    g = ph.group(4 + m, i)
                    group_ready(g)
                    following = ph.chunk(6 + m, i) if m < 2 or next_gain else None
                    if following and m < 3:
                        split(following)
                    for t in range(2):
                        act.wait_ge(pair_free[g.pair], g.freed(t))
                        if next_gain:
                            gained_hi(next_norm, 2 * m + t, (next_gain[0], next_gain[1] + 2 * m + t))
                        square(next_norm, 2 * m + t, x[:, 2 * m + t, :])
                    if following and m == 3:
                        split(following)

            gained_x(N_MLPA, [RET.group(n, RH - 1) for n in range(6, 10)], "mlp_norm_g_2", 0, MLP_A.chunk(1))
            mlp(MLP_A, N_MLPA, 0, N_ATT, ("mix_norm_g_2", 8))

            def take(j):
                kind, four = ATT_ORDER[j]
                g, slot = ATT.group(ATT.upto[j]), ATT2[four].slot
                if kind == "v":
                    tokens_hi(g, slot + 4, s["att_in_hi"])
                elif kind != "o":
                    for m in range(2):
                        act.wait_ge(pair_free[g.pair], g.freed(m))
                        act.activation(hid_hi[:, slot + 2 * "qk".index(kind) + m, :], tmp[:, m, :], ACT.Copy)\
                            .then_inc(s["att_in_hi"], 1)

            rsqrt_columns(1, D)
            rsqrt(N_ATT, D)
            act.wait_ge(s["col_r"], 2)
            split(ATT.chunk(2))
            take(0)
            group_ready(ATT.group(1))
            split(ATT.chunk(3))
            take(1)
            exps(*att2_head(0))
            for n in range(12):
                take(2 + n)
                prob_hi(*att2_head(n))
                split(ATT.chunk(4 + n))
                empty_out(*att2_head(n))
                if n < 11:
                    exps(*att2_head(n + 1))
            attend(ATT2[3])
            split(MLP_B.chunk(0))
            gained_x(N_MLPB, [ATT.group(ATT.groups - n) for n in (4, 3, 2, 1)], "mlp_norm_g_2", 8, MLP_B.chunk(1))
            mlp(MLP_B, N_MLPB, MLP_GROUPS * 8, N_FINAL, None)

            rsqrt(N_FINAL, D)
            for f in range(KD):
                act.wait_ge(s["fin_t"], f + 1)
                dst = o_buf[:, :, :].rearrange("p (t h) s -> p t (h s)", t=4)[:, :, f * P:(f + 1) * P]
                act.activation(dst, ps[:, f, :].rearrange("p (t c) -> p t c", t=4), ACT.Copy)\
                    .then_inc(s["fin_copied"], 1)

        @block.vector
        def _(dve):
            def sums(norm, t, squares=sq):
                dve.wait_ge(s["norm_sq"], norm.sq0 + t + 1)
                if t >= 2:
                    dve.wait_ge(s["norm_acc"], norm.acc0 + t - 1)
                dve.tensor_tensor(ssq, ssq, squares[:, t % 2, :], ALU.add).then_inc(s["norm_acc"], 1)

            def all_sums(norm):
                for t in range(1, norm.n):
                    sums(norm, t)

            def low(norm, name, src, base, slot):
                hi_ap, lo_ap = base
                dve.wait_ge(s["norm_r"], norm.index + 1)
                for t in range(norm.n + 1):
                    if t < norm.n:
                        if norm.out0 + t >= 2:
                            dve.wait_ge(s["norm_lo"], norm.out0 + t - 1)
                        dve.scalar_tensor_tensor(tmp[:, t % 2, :], src(t), gain(*name(t)), r_bc, ALU.mult,
                                                 ALU.mult).then_inc(s["norm_tmp"], 1)
                    if t:
                        dve.wait_ge(s["norm_hi"], norm.out0 + t)
                        dve.tensor_tensor(lo_ap[:, slot + t - 1, :], tmp[:, (t - 1) % 2, :],
                                          hi_ap[:, slot + t - 1, :].bitcast(F32), ALU.subtract)\
                            .then_inc(s["norm_lo"], 1)

            def gained_lo(norm, t, at):
                dve.wait_ge(s["norm_hi"], norm.out0 + t + 1)
                dve.scalar_tensor_tensor(hn_lo[:, t, :], x[:, t, :], gain(*at), hn_hi[:, t, :].bitcast(F32),
                                         ALU.mult, ALU.subtract).then_inc(s["norm_lo"], 1)

            def gained_x(norm, name, row):
                for t in range(KD):
                    gained_lo(norm, t, (name, row + t))
                all_sums(norm)

            def tokens_lo(g, slot, sem, before):
                for t in range(4):
                    half = slice((t % 2) * 256, (t % 2) * 256 + 256)
                    dve.wait_ge(sem, before + t // 2 * 2 + 2)
                    ins = dve.scalar_tensor_tensor(hid_lo[:, slot + t // 2, half], ps[:, g.bank(t // 2), half],
                                                   r_col[:, t:t + 1], hid_hi[:, slot + t // 2, half].bitcast(F32),
                                                   ALU.mult, ALU.subtract)
                    if t % 2:
                        ins.then_inc(pair_free[g.pair], 1)

            def scaled(g, m, dst, r=r_bc):
                dve.tensor_tensor(dst, ps[:, g.bank(m), :], r, ALU.mult).then_inc(pair_free[g.pair], 1)

            def group_ready(g):
                dve.wait_ge(s["group_done"], g.done)

            def add_to(g, m, dst):
                dve.tensor_tensor(dst, ps[:, g.bank(m), :], dst, ALU.add).then_inc(pair_free[g.pair], 1)

            hn, hid = (hn_hi, hn_lo), (hid_hi, hid_lo)

            dve.wait_ge(s["freq_in"], 16)
            dve.wait_ge(s["pos_in"], 16)
            a, n = aux[:, 2, :], aux[:, 3, :]
            steps = [
                lambda: dve.tensor_copy(a, tab[:, 0, :].bitcast(I32)),
                lambda: dve.tensor_scalar(a, a, freq[:, 0:1], None, ALU.mult),
                lambda: dve.tensor_scalar(n, a, INV_TWO_PI, ROUND, ALU.mult, ALU.add),
                lambda: dve.tensor_scalar(n, n, ROUND, None, ALU.subtract),
                lambda: dve.scalar_tensor_tensor(a, n, -TWO_PI[0], a, ALU.mult, ALU.add),
                lambda: dve.scalar_tensor_tensor(a, n, -TWO_PI[1], a, ALU.mult, ALU.add),
                lambda: dve.scalar_tensor_tensor(a, n, -TWO_PI[2], a, ALU.mult, ALU.add),
                lambda: dve.scalar_tensor_tensor(a, n, -TWO_PI[3], a, ALU.mult, ALU.add),
                lambda: dve.tensor_scalar(a, a, SIN_MAX, -SIN_MAX, ALU.min, ALU.max),
            ]
            assert len(steps) == ANGLE_STEPS
            for k, step in enumerate(steps):
                if k:
                    dve.wait_ge(s["angle"], k)
                step().then_inc(s["angle"], 1)
            dve.wait_ge(s["gains_ready"], 1)
            for f in range(KD):
                dve.wait_ge(s["x_copied"], f + 1)
                gained_lo(N_MIX, f, ("mix_pre_norm", f))
                if f:
                    sums(N_MIX, f)
            kr = [ap[:, 4:6, :].rearrange("p a (k c) -> p (a k) c", c=P) for ap in hid]
            kr_raw = aux[:, 0, :].rearrange("p (k c) -> p k c", k=KD)
            dve.wait_ge(s["kr_hi"], 1)
            for at in (0, 64):
                ins = dve.tensor_tensor(kr[1][:, :, at:at + 64], kr_raw, kr[0][:, :, at:at + 64].bitcast(F32),
                                        ALU.subtract)
            ins.then_inc(s["kr_lo"], 1)

            r = rstd[:, :]
            dve.wait_ge(s["norm_r"], N_MIX.index + 1)
            group_ready(MIX.group(0))
            for m in range(2):
                scaled(MIX.group(0), m, o_buf[:, m, :], r)
            all_sums(N_Q)
            group_ready(MIX.group(1))
            for m in range(2):
                scaled(MIX.group(1), m, o_buf[:, 2 + m, :], r)
            dve.wait_ge(s["ext_in"], 16)
            dve.memset(ext[:, 0:255], 0.0).then_inc(s["ext_built"], 1)
            dve.memset(ext[:, 255 + REL_TABLE:], 0.0).then_inc(s["ext_built"], 1)
            dve.wait_ge(s["ext_built"], 1)
            dve.tensor_scalar(ext[:, 0:255], ext[:, 0:255], ext[:, 255:256], None, ALU.add)\
                .then_inc(s["ext_built"], 1)

            dve.wait_ge(s["sin_done"], 2)
            dve.tensor_scalar(tab[:, 1, :], tab[:, 1, :], freq[:, 1:2], None, ALU.mult).then_inc(s["table"], 1)
            dve.tensor_tensor(tab[:, 0, :], tab[:, 0, :], tab[:, 0, :], ALU.mult).then_inc(s["table"], 1)
            dve.wait_ge(s["table"], 2)
            dve.tensor_scalar(tab[:, 0, :], tab[:, 0, :], -2.0, 1.0, ALU.mult, ALU.add).then_inc(s["table"], 1)
            dve.wait_ge(s["table"], 3)
            dve.wait_ge(s["kr_done"], 1)
            dve.tensor_tensor(aux[64:96, 0, :], ps[0:32, 4, :], tab[0:32, 0, :], ALU.mult).then_inc(s["krope"], 1)
            dve.tensor_tensor(aux[64:96, 2, :], ps[32:64, 4, :], tab[32:64, 1, :], ALU.mult)\
                .then_inc(s["krope"], 1)
            dve.wait_ge(s["krope"], 2)
            dve.tensor_tensor(aux[64:96, 0, :], aux[64:96, 0, :], aux[64:96, 2, :], ALU.add)\
                .then_inc(s["krope"], 1)
            dve.wait_ge(s["krope"], 3)
            dve.tensor_tensor(aux[64:96, 0, :], aux[64:96, 0, :], rstd[64:96, :], ALU.mult)\
                .then_inc(s["krope"], 1)

            def c_gate(half):
                g = MIX.group(2 + 3 * half)
                group_ready(g)
                for m in range(2):
                    scaled(g, m, o_buf[:, 4 + 2 * half + m, :], r)

            c_gate(0)
            dve.wait_ge(s["gains_ready"], 2)
            low(N_Q, lambda t: ("q_norm", t), lambda t: o_buf[:, t, :], hid, 0)
            all_sums(N_KV)
            low(N_KV, lambda t: ("kv_norm", t), lambda t: o_buf[:, 2 + t, :], hid, 2)
            dve.wait_ge(s["krope_hi"], 1)
            dve.tensor_tensor(hid_lo[64:96, 4, :], aux[64:96, 0, :], hid_hi[64:96, 4, :].bitcast(F32),
                              ALU.subtract).then_inc(s["krope_lo"], 1)
            for half in range(2):
                cg, xv, bg = (MIX.group(2 + 3 * half + n) for n in range(3))
                u = [o_buf[:, 4 + 2 * half + m, :] for m in range(2)]
                y = [aux[:, 2 + m, :] for m in range(2)]
                if half:
                    c_gate(1)
                group_ready(xv)
                for m in range(2):
                    dve.wait_ge(pair_free[cg.pair], cg.freed(m))
                    dve.tensor_tensor(u[m], ps[:, xv.bank(m), :], u[m], ALU.mult)\
                        .then_inc(pair_free[xv.pair], 1)
                for m in range(2):
                    dve.wait_ge(pair_free[xv.pair], xv.freed(m))
                    dve.tensor_tensor(u[m], u[m], r, ALU.mult).then_inc(s["conv_u"], 1)
                if half:
                    dve.wait_ge(s["conv_out"], 2)
                done = half * 6
                for tap in range(3):
                    for m in range(2):
                        w = gain("conv_w", 4 * tap + 2 * half + m)
                        if tap == 0:
                            dve.wait_ge(s["conv_u"], 2 * half + m + 1)
                            ins = dve.tensor_scalar(y[m], u[m], w, None, ALU.mult)
                        else:
                            dve.wait_ge(s["conv"], done + 2 * tap + m - 1)
                            ins = dve.scalar_tensor_tensor(y[m][:, tap:], u[m][:, 0:S - tap], w, y[m][:, tap:],
                                                           ALU.mult, ALU.add)
                        ins.then_inc(s["conv"], 1)
                group_ready(bg)
                for m in range(2):
                    dve.wait_ge(s["conv"], done + 5 + m)
                    dve.tensor_tensor(u[m], ps[:, bg.bank(m), :], y[m], ALU.mult)\
                        .then_inc(pair_free[bg.pair], 1)
                for m in range(2):
                    dve.wait_ge(pair_free[bg.pair], bg.freed(m))
                    dve.tensor_tensor(u[m], u[m], r, ALU.mult).then_inc(s["conv_out"], 1)

            for n in range(2):
                g = UKV.group(n)
                for m in range(2):
                    for half in range(2):
                        h = 4 * n + 2 * m + half
                        dve.wait_ge(s["kv_hi"], h + 1)
                        ins = dve.tensor_tensor(hid_lo[0:NOPE, 4 + h, :], ps[64 * half:64 * half + 64, g.bank(m), :],
                                                hid_hi[0:NOPE, 4 + h, :].bitcast(F32), ALU.subtract)
                    ins.then_inc(pair_free[g.pair], 1)
            all_sums(N_CONVG)
            for n in range(2):
                g = UKV.group(2 + n)
                for m in range(2):
                    dve.wait_ge(s["kv_hi"], H1 + 2 * n + m + 1)
                    dve.tensor_tensor(hid_lo[:, 12 + 2 * n + m, :], ps[:, g.bank(m), :],
                                      hid_hi[:, 12 + 2 * n + m, :].bitcast(F32), ALU.subtract)\
                        .then_inc(pair_free[g.pair], 1)
            for r in range(2):
                g = UQ.group(r)
                group_ready(g)
                dve.tensor_tensor(tmp[:, r, :], ps[:, g.bank(0), :], tab[:, 0, :], ALU.mult)\
                    .then_inc(pair_free[g.pair], 1)
                if r == 0:
                    dve.wait_ge(s["norm_acc"], N_CONVG.acc0 + 3)
                dve.tensor_tensor(sq[:, r, :], ps[:, g.bank(1), :], tab[:, 1, :], ALU.mult)\
                    .then_inc(pair_free[g.pair], 1)
                dve.wait_ge(pair_free[g.pair], g.freed(1))
                dve.tensor_tensor(tmp[:, r, :], tmp[:, r, :], sq[:, r, :], ALU.add).then_inc(s["q_rope"], 1)
                dve.wait_ge(s["q_rope"], r + 1)
                dve.wait_ge(s["qr_hi"], r + 1)
                dve.tensor_tensor(hid_lo[:, 2 + r, :], tmp[:, r, :], hid_hi[:, 2 + r, :].bitcast(F32),
                                  ALU.subtract).then_inc(s["qr_lo"], 1)
            for h in range(H1):
                g = UQ.group(2 + h // 4)
                dve.wait_ge(s["q_nope_hi"], h + 1)
                ins = dve.tensor_tensor(hn_lo[0:NOPE, h, :],
                                        ps[64 * (h % 2):64 * (h % 2) + 64, g.bank(h % 4 // 2), :],
                                        hn_hi[0:NOPE, h, :].bitcast(F32), ALU.subtract)
                if h % 2:
                    ins.then_inc(pair_free[g.pair], 1)

            def masked_scores(a, h):
                if a.block2:
                    dve.wait_ge(s["mask_set"], 4)
                    dve.wait_ge(s[f"bias_in{h}"], a.group * 32 + 32)
                for t, done in Q_ORDER:
                    dve.wait_ge(s["att_s"], a.n(h) * 4 + done)
                    col = 4 * (h % 2) + t
                    dve.tensor_tensor_reduce(a.score_sb(h, t), a.score_ps(t),
                                             aux[:, h if a.block2 else 1, 512 - 128 * (t + 1):],
                                             1.0 if a.block2 else DQ ** -0.5, FMIN, ALU.add, ALU.max,
                                             mx[:, col:col + 1]).then_inc(s["att_mx"], 1)
                dve.wait_ge(s["att_mx"], a.n(h) * 4 + 4)
                four = slice(4 * (h % 2), 4 * (h % 2) + 4)
                dve.tensor_scalar(nmx[:, four], mx[:, four], -1.0, None, ALU.mult).then_inc(s["att_nmx"], 1)

            def probabilities(a, h):
                four = slice(4 * (h % 2), 4 * (h % 2) + 4)
                dve.wait_ge(s["att_exp"], a.n(h) * 4 + 4)
                dve.reciprocal(rs[:, four], sm[:, four]).then_inc(s["att_rs"], 1)
                dve.wait_ge(s["att_rs"], a.n(h) + 1)
                for t in range(4):
                    col = 4 * (h % 2) + t
                    dve.tensor_scalar(a.score_sb(h, t), a.score_sb(h, t), rs[:, col:col + 1], None, ALU.mult)\
                        .then_inc(s["att_p"], 1)

            def prob_lo(a, h):
                for j, done in K_ORDER:
                    dve.wait_ge(s["att_hi"], a.n(h) * 4 + done)
                    dve.tensor_tensor(a.pt(1, j), a.trans_ps(j), a.pt(0, j).bitcast(F32), ALU.subtract)\
                        .then_inc(s["att_lo"], 1)

            def out_lo(a, h):
                dve.wait_ge(s["att_ohi"], a.n(h) - H1 + 1)
                dve.tensor_tensor(a.out(hid_lo, h), a.out_ps(h), a.out(hid_hi, h).bitcast(F32), ALU.subtract)\
                    .then_inc(s["att_o"], 1)

            def attend(a, between=None):
                masked_scores(a, 0)
                masked_scores(a, 1)
                probabilities(a, 0)
                probabilities(a, 1)
                if between:
                    between()
                prob_lo(a, 0)
                for h in range(a.heads):
                    if h + 2 < a.heads:
                        masked_scores(a, h + 2)
                    if a.block2:
                        out_lo(a, h)
                    if h + 1 < a.heads:
                        prob_lo(a, h + 1)
                    if h + 2 < a.heads:
                        probabilities(a, h + 2)

            dve.wait_ge(s["mask_in"], 16)
            attend(ATT1)

            dve.wait_ge(s["att_pv"], H1)
            low(N_CONVG, lambda t: ("conv_group_norm", t), lambda t: o_buf[:, 4 + t, :], hn, 4)
            all_sums(N_ATTG)
            low(N_ATTG, lambda t: ("attn_group_norm", t), lambda t: o_buf[:, t, :], hn, 0)
            for t in range(1, 4):
                sums(N_POST, t)
            for f in range(2):
                dve.wait_ge(s["p_hi"], f + 1)
                dve.tensor_tensor(hid_lo[:, f, :], ps[:, 4 + f, :], hid_hi[:, f, :].bitcast(F32),
                                  ALU.subtract).then_inc(s["p_lo"], 1)
            for t in range(4, KD):
                sums(N_POST, t)

            def mix_normed(t):
                dve.scalar_tensor_tensor(tmp[:, t % 2, :], o_buf[:, t, :], gain("mix_post_norm", t), r_bc,
                                         ALU.mult, ALU.mult).then_inc(s["post_x"], 1)

            dve.wait_ge(s["norm_r"], N_POST.index + 1)
            for t in range(KD):
                if t == 0:
                    mix_normed(0)
                dve.wait_ge(s["post_x"], 2 * t + 1)
                dve.tensor_tensor(x[:, t, :], x[:, t, :], tmp[:, t % 2, :], ALU.add).then_inc(s["post_x"], 1)
                if t + 1 < KD:
                    mix_normed(t + 1)
                gained_lo(N_FFN, t, ("ffn_pre_norm", t))
            all_sums(N_FFN)

            dve.wait_ge(s["norm_r"], N_FFN.index + 1)

            def ffn(ph, i, g_hid, kt, next_norm=None):
                for j in range(kt // 2):
                    gate, up = ph.group(2 * j, i), ph.group(2 * j + 1, i)
                    done = g_hid + 2 * j
                    group_ready(gate)
                    if j:
                        dve.wait_ge(s["ffn_part"], done)
                    for m in range(2):
                        scaled(gate, m, sq[:, m, :])
                    group_ready(up)
                    if j:
                        dve.wait_ge(s["ffn_lo"], done)
                    for m in range(2):
                        scaled(up, m, tmp[:, m, :])
                    for m in range(2):
                        dve.wait_ge(s["ffn_silu"], done + m + 1)
                        dve.wait_ge(pair_free[up.pair], up.freed(m))
                        dve.tensor_tensor(tmp[:, m, :], tmp[:, m, :], sq[:, m, :], ALU.mult)\
                            .then_inc(s["ffn_part"], 1)
                    for m in range(2):
                        dve.wait_ge(s["ffn_hi"], done + m + 1)
                        dve.tensor_tensor(hid_lo[:, 2 * j + m, :], tmp[:, m, :],
                                          hid_hi[:, 2 * j + m, :].bitcast(F32), ALU.subtract)\
                            .then_inc(s["ffn_lo"], 1)
                    if next_norm is None and i == 0 and j == 0:
                        dve.memset(o_buf[:, :, :], 0.0).then_inc(s["o_zero"], 1)
                        dve.wait_ge(s["o_zero"], 1)
                for m in range(4):
                    g = ph.group(kt + m, i)
                    group_ready(g)
                    for t in range(2):
                        add_to(g, t, o_buf[:, 2 * m + t, :])
                        if next_norm and 2 * m + t >= 2:
                            sums(next_norm, 2 * m + t - 1)
                    for t in (2 * m, 2 * m + 1):
                        if ph is FFN and i == 0 and t:
                            sums(N_PLE, t, aux[:, 0:2, :])
                        if ph is FFN and i == 1:
                            dve.wait_ge(s["norm_r"], N_PLE.index + 1)
                            dve.scalar_tensor_tensor(e_buf[:, t, :], e_buf[:, t, :], gain("ple_norm", t),
                                                     rstd[:, :], ALU.mult, ALU.mult).then_inc(s["ple_n"], 1)

            for i in range(2):
                ffn(FFN, i, i * 8, 8)
            ffn(FFN_LAST, 0, 16, 6, N_FPOST)
            sums(N_FPOST, KD - 1)

            def ffn_normed(t):
                dve.scalar_tensor_tensor(tmp[:, t % 2, :], o_buf[:, t, :], gain("ffn_post_norm", t), r_bc,
                                         ALU.mult, ALU.mult).then_inc(s["ple_x"], 1)

            dve.wait_ge(s["norm_r"], N_FPOST.index + 1)
            for t in range(KD):
                if t == 0:
                    ffn_normed(0)
                dve.wait_ge(s["ple_x"], 2 * t + 1)
                dve.tensor_tensor(x[:, t, :], x[:, t, :], tmp[:, t % 2, :], ALU.add).then_inc(s["ple_x"], 1)
                if t + 1 < KD:
                    ffn_normed(t + 1)
                dve.wait_ge(s["ple_x"], 2 * t + 2)
                dve.wait_ge(s["ple_xhi"], t + 1)
                dve.tensor_tensor(hn_lo[:, t, :], x[:, t, :], hn_hi[:, t, :].bitcast(F32), ALU.subtract)\
                    .then_inc(s["ple_xlo"], 1)
            dve.wait_ge(s["ple_n"], KD)

            def gated(m, t):
                g, k = GATE.group(m), 2 * m + t
                if k >= 2:
                    dve.wait_ge(s["ple_e"], 2 * k - 2)
                dve.wait_ge(pair_free[g.pair], g.freed(t))
                dve.tensor_tensor(tmp[:, t, :], e_buf[:, k, :], aux[:, 2 + t, :], ALU.mult)\
                    .then_inc(s["ple_e"], 1)
                dve.wait_ge(s["ple_e"], 2 * k + 1)
                dve.tensor_tensor(x[:, k, :], x[:, k, :], tmp[:, t, :], ALU.add).then_inc(s["ple_e"], 1)

            for m in range(3):
                for t in range(2):
                    gated(m, t)
                    if 2 * m + t >= 2:
                        sums(N_RET, 2 * m + t - 1)
            for t in range(2):
                gained_lo(N_RET, t, ("mix_norm_g_2", t))
            gated(3, 0)
            sums(N_RET, 5)
            gained_lo(N_RET, 2, ("mix_norm_g_2", 2))
            gated(3, 1)
            for t in range(3, 7):
                gained_lo(N_RET, t, ("mix_norm_g_2", t))
            sums(N_RET, 6)
            gained_lo(N_RET, 7, ("mix_norm_g_2", 7))
            sums(N_RET, 7)

            cos, sin = tab[:, 0, :], tab[:, 1, :]
            dve.wait_ge(s["ret_tab_in"], 16)
            dve.wait_ge(s["norm_r"], N_RET.index + 1)
            for table in (cos, sin):
                dve.tensor_tensor(table, table, r_bc, ALU.mult).then_inc(s["tab_scaled"], 1)
            dve.wait_ge(s["tab_scaled"], 2)
            dve.wait_ge(s["decay_in"], 16)
            with dve.Fori(0, RH) as h:
                last = RET.group(1, h)
                dve.wait_ge(pair_free[last.pair], last.empty)
                for n in range(2):
                    if n:
                        dve.wait_ge(s["ret_qk_lo"], h * 4 + 2)
                    g = RET.group(n, h)
                    t1, t2 = ps[:, g.bank(0), :], ps[:, g.bank(1), :]
                    group_ready(g)
                    dve.tensor_tensor(tmp[:, 0, :], t1, cos, ALU.mult).then_inc(s["ret_part"], 1)
                    dve.tensor_tensor(sq[:, 0, :], t2, sin, ALU.mult).then_inc(s["ret_part"], 1)
                    dve.tensor_tensor(sq[:, 1, :], t1, sin, ALU.mult).then_inc(pair_free[g.pair], 1)
                    dve.tensor_tensor(tmp[:, 1, :], t2, cos, ALU.mult).then_inc(pair_free[g.pair], 1)
                    dve.wait_ge(s["ret_part"], h * 4 + 2 * n + 2)
                    dve.tensor_tensor(tmp[:, 0, :], tmp[:, 0, :], sq[:, 0, :], ALU.subtract)\
                        .then_inc(s["ret_tmp"], 1)
                    dve.wait_ge(pair_free[g.pair], g.freed(1))
                    dve.tensor_tensor(tmp[:, 1, :], tmp[:, 1, :], sq[:, 1, :], ALU.add).then_inc(s["ret_tmp"], 1)
                    for t in range(2):
                        dve.wait_ge(s["ret_qk_hi"], h * 4 + 2 * n + t + 1)
                        dve.tensor_tensor(hid_lo[:, 2 * n + t, :], tmp[:, t, :],
                                          hid_hi[:, 2 * n + t, :].bitcast(F32), ALU.subtract)\
                            .then_inc(s["ret_qk_lo"], 1)
                tokens_lo(RET.group(2, h), 4, s["ret_v_hi"], h * 8)
                for j, done in K_ORDER:
                    dve.wait_ge(s["ret_s"], h * 4 + done)
                    dve.tensor_tensor(o_buf[:, j, j * P:], ret_score(j), aux[:, h, 0:S - j * P], ALU.mult)\
                        .then_inc(s["ret_sd"], 1)
                for n, (j, _) in enumerate(K_ORDER):
                    dve.wait_ge(s["ret_s_hi"], h * 4 + n + 1)
                    dve.tensor_tensor(hid_lo[:, 8 + j, j * P:], o_buf[:, j, j * P:],
                                      hid_hi[:, 8 + j, j * P:].bitcast(F32), ALU.subtract)\
                        .then_inc(s["ret_s_lo"], 1)
                tokens_lo(RET.group(3, h), 6, s["ret_v_hi"], h * 8 + 4)
                for d in range(1, 4):
                    dve.wait_ge(s["ret_o"], h * 4 + d + 1)
                    if d > 1:
                        dve.wait_ge(s["ret_sum"], h * 3 + d - 1)
                    dve.tensor_tensor(ssq, o_buf[:, 0, :] if d == 1 else ssq, o_buf[:, d, :], ALU.add)\
                        .then_inc(s["ret_sum"], 1)
                dve.wait_ge(s["ret_mean"], h + 1)
                for t in range(4):
                    dve.scalar_tensor_tensor(o_buf[:, t, :], ps[:, 4, :], -1.0 / RDV, o_buf[:, t, :], ALU.mult,
                                             ALU.add).then_inc(s["ret_d"], 1)
                for t in range(1, 4):
                    dve.wait_ge(s["ret_sq"], h * 4 + t + 1)
                    if t > 1:
                        dve.wait_ge(s["ret_acc"], h * 3 + t - 1)
                    dve.tensor_tensor(ssq, ssq, sq[:, t % 2, :], ALU.add).then_inc(s["ret_acc"], 1)
                gate = RET.group(4, h)
                group_ready(gate)
                for m in range(2):
                    scaled(gate, m, o_buf[:, 4 + m, :])
                dve.wait_ge(s["ret_rstd"], h + 1)
                at = GAIN_AT["ret_gn_g_2"]
                head_gains = gains[:, at:at + 16].rearrange("p (h t) -> p h t", t=4)
                for t in range(4):
                    dve.scalar_tensor_tensor(o_buf[:, t, :], o_buf[:, t, :], head_gains[:, h, t:t + 1],
                                             rstd[:, :], ALU.mult, ALU.mult).then_inc(s["ret_ys"], 1)
                for n in range(2):
                    if n:
                        gate = RET.group(5, h)
                        group_ready(gate)
                        for m in range(2):
                            scaled(gate, m, o_buf[:, 6 + m, :])
                    for t in (2 * n, 2 * n + 1):
                        dve.wait_ge(s["ret_gate"], h * 4 + t + 1)
                        dve.wait_ge(s["ret_ys"], h * 4 + t + 1)
                        dve.tensor_tensor(o_buf[:, t, :], o_buf[:, t, :], o_buf[:, 4 + t, :], ALU.mult)\
                            .then_inc(s["ret_y"], 1)
                    for t in (2 * n, 2 * n + 1):
                        dve.wait_ge(s["ret_y_hi"], h * 4 + t + 1)
                        dve.tensor_tensor(hid_lo[:, 12 + t, :], o_buf[:, t, :],
                                          hid_hi[:, 12 + t, :].bitcast(F32), ALU.subtract)\
                            .then_inc(s["ret_y_lo"], 1)
                for n in range(4):
                    g = RET.group(6 + n, h)
                    group_ready(g)
                    for m in range(2):
                        add_to(g, m, x[:, 2 * n + m, :])

            def mlp(ph, norm, base, next_norm, next_gain):
                dve.wait_ge(s["norm_r"], norm.index + 1)

                def body(i):
                    last = isinstance(i, int)
                    for m in range(4):
                        g = ph.group(m, i)
                        group_ready(g)
                        if m:
                            dve.wait_ge(s["mlp_sq"], base + i * 8 + 2 * m)
                        for t in range(2):
                            dve.scalar_tensor_tensor(sq[:, t, :], ps[:, g.bank(t), :], 0.0, r_bc, ALU.max,
                                                     ALU.mult).then_inc(pair_free[g.pair], 1)
                        for t in range(2):
                            dve.wait_ge(s["mlp_hi"], base + i * 8 + 2 * m + t + 1)
                            dve.tensor_tensor(hid_lo[:, 2 * m + t, :], tmp[:, t, :],
                                              hid_hi[:, 2 * m + t, :].bitcast(F32), ALU.subtract)\
                                .then_inc(s["mlp_lo"], 1)
                    for m in range(4):
                        g = ph.group(4 + m, i)
                        group_ready(g)
                        for t in range(2):
                            add_to(g, t, x[:, 2 * m + t, :])
                        for t in (2 * m, 2 * m + 1):
                            if last and next_gain:
                                gained_lo(next_norm, t, (next_gain[0], next_gain[1] + t))
                            if last and t:
                                sums(next_norm, t)

                with dve.Fori(0, MLP_GROUPS - 1) as i:
                    body(i)
                body(MLP_GROUPS - 1)

            gained_x(N_MLPA, "mlp_norm_g_2", 0)
            for h in range(4):
                dve.memset(aux[0:64, h, 448:512], MASKED).then_inc(s["mask_set"], 1)
            mlp(MLP_A, N_MLPA, 0, N_ATT, ("mix_norm_g_2", 8))
            dve.wait_ge(s["norm_r"], N_ATT.index + 1)

            def scale(j):
                kind, four = ATT_ORDER[j]
                if kind in "qk":
                    g = ATT.group(ATT.upto[j])
                    group_ready(g)
                    before = four * 4 + 2 * "qk".index(kind)
                    if before:
                        dve.wait_ge(s["att_in_lo"], before)
                    for m in range(2):
                        dve.scalar_tensor_tensor(tmp[:, m, :], ps[:, g.bank(m), :],
                                                 DH ** -0.5 if kind == "q" else 1.0, r_bc, ALU.mult, ALU.mult)\
                            .then_inc(pair_free[g.pair], 1)

            def take(j):
                kind, four = ATT_ORDER[j]
                slot = ATT2[four].slot
                if kind == "v":
                    tokens_lo(ATT.group(ATT.upto[j]), slot + 4, s["att_in_hi"], four * 8 + 4)
                elif kind != "o":
                    at = 2 * "qk".index(kind)
                    for m in range(2):
                        dve.wait_ge(s["att_in_hi"], four * 8 + at + m + 1)
                        dve.tensor_tensor(hid_lo[:, slot + at + m, :], tmp[:, m, :],
                                          hid_hi[:, slot + at + m, :].bitcast(F32), ALU.subtract)\
                            .then_inc(s["att_in_lo"], 1)

            def add_out(j, parts):
                if ATT_ORDER[j][0] == "o":
                    for n in parts:
                        g = ATT.group(ATT.upto[j] + n)
                        group_ready(g)
                        for m in range(2):
                            add_to(g, m, x[:, 2 * n + m, :])

            for j in range(2):
                scale(j)
                take(j)
            masked_scores(*att2_head(0))
            probabilities(*att2_head(0))
            for n in range(12):
                scale(2 + n)
                take(2 + n)
                prob_lo(*att2_head(n))
                if n < 11:
                    add_out(3 + n, (0, 1))
                out_lo(*att2_head(n))
                if n < 11:
                    masked_scores(*att2_head(n + 1))
                    add_out(3 + n, (2,))
                    probabilities(*att2_head(n + 1))
                    add_out(3 + n, (3,))
            attend(ATT2[3], lambda: add_out(14, range(4)))
            for n in range(4):
                add_out(15, (n,))
                if n:
                    for t in (2 * n - 2, 2 * n - 1):
                        gained_lo(N_MLPB, t, ("mlp_norm_g_2", 8 + t))
            for t in (6, 7):
                gained_lo(N_MLPB, t, ("mlp_norm_g_2", 8 + t))
            all_sums(N_MLPB)
            mlp(MLP_B, N_MLPB, MLP_GROUPS * 8, N_FINAL, None)

            dve.wait_ge(s["norm_r"], N_FINAL.index + 1)
            for f in range(KD):
                dve.scalar_tensor_tensor(normed_x[:, f, :], x[:, f, :], gain("final_norm_g_2", f), r_bc, ALU.mult,
                                         ALU.mult).then_inc(s["fin_tmp"], 1)


_INS = ["x", "p", "positions", "mix_pre_norm", "w_in", "q_norm", "kv_norm", "w_uq", "w_ukv", "conv_w",
        "attn_group_norm", "conv_group_norm", "w_out", "mix_post_norm", "ffn_pre_norm", "w_gate", "w_up",
        "w_down", "ffn_post_norm", "w_ple_proj", "ple_norm", "w_ple_gate", "mix_norm_g_2", "ret_w_in_2",
        "ret_gn_g_2", "ret_w_out_2", "att_w_in_2", "att_rel_bias_2", "att_w_out_2", "mlp_norm_g_2",
        "mlp_w1_2", "mlp_w2_2", "final_norm_g_2"]


def constants():
    import numpy as np
    f = np.float32
    half = ROPE // 2
    inv_freq = f(1) / (f(10000) ** (np.arange(half, dtype=f) / f(half)))
    part = np.arange(P)
    freq = np.stack([inv_freq[part % half], np.where(part % ROPE < half, -1, 1)], 1).astype(f)
    causal = np.zeros((P, S), f)
    causal[:, S - P:] = np.where(np.arange(P)[None, :] <= part[:, None], 0, MASKED)
    inv = np.exp(-np.log(f(10000)) * np.arange(RDK // 2, dtype=f) / f(RDK // 2)).astype(f)
    ang = inv[:, None] * np.arange(S, dtype=f)[None, :]
    ret_rope = np.stack([np.cos(ang), np.sin(ang)], 1).astype(f)
    log_gamma = np.log1p(-np.exp2(-5.0 - np.arange(RH)))
    key, query = part[:, None, None], np.arange(S)[None, None, :]
    decay = np.exp(log_gamma[None, :, None] * np.abs(query - key)) * RDK ** -0.5
    decay = np.where(key // 64 <= query // 64, decay, 0).astype(f)
    return {"c_ident": np.eye(P, dtype=f), "c_freq": freq, "c_causal": causal, "c_ret_rope": ret_rope,
            "c_decay": decay}


def kernel(**inputs):
    import numpy as _np
    import concourse.bacc as _bacc
    from concourse import mybir as _mybir
    from concourse.bass_utils import run_bass_kernel_spmd as _run

    nc = _bacc.Bacc("TRN2", target_bir_lowering=False, num_devices=1)
    arrays, tensors = {}, {}
    given = {name: inputs[name] for name in _INS}
    given.update(constants())
    for name, value in given.items():
        a = _np.ascontiguousarray(value)
        arrays[f"in_{name}"] = a
        tensors[name] = nc.dram_tensor(f"in_{name}", a.shape, _mybir.dt.from_np(a.dtype),
                                       kind="ExternalInput").ap()
    out = nc.dram_tensor("out_0", (1, S, D), F32, kind="ExternalOutput").ap()
    build(nc, tensors, out)
    r = _run(nc, [arrays], core_ids=[0])
    return r.results[0]["out_0"]
```
